# Optimizing a Trainium2 kernel written in Bass

```python
import jax, jax.numpy as jnp
from jax import lax
import numpy as np
import math
import jax
import jax.numpy as jnp

D_MODEL = 1024
BATCH = 1
SEQ = 256
DEPTH = 1

D_MIX = D_MODEL
CONV_W = D_MIX // 4
LRU_W = (D_MIX - CONV_W) // 2
GLA_V = D_MIX - CONV_W - LRU_W
CONV_K = 31
LRU_CONV_K = 4
LRU_BLOCKS = 6
LRU_BW = LRU_W // LRU_BLOCKS
LRU_C = 8.0
GLA_HEADS = 4
GLA_DV = GLA_V // GLA_HEADS
GLA_DK = GLA_DV // 2
GLA_RANK = 16
GLA_TAU = 16.0
GLA_CHUNK = 64
IN_WIDTH = 2 * CONV_W + 2 * LRU_W + 2 * GLA_HEADS * GLA_DK + GLA_V + GLA_RANK + GLA_V
N_GROUPS = 4
EXPERTS_PER_GROUP = 4
TOP_K = 2
D_EXPERT = D_MODEL // 2
EPS = 1e-6


def rms_norm(x, g):
    xf = x.astype(jnp.float32)
    y = xf * lax.rsqrt(jnp.mean(xf * xf, axis=-1, keepdims=True) + EPS)
    return (y * g.astype(jnp.float32)).astype(x.dtype)

def layer_norm(x, g, b):
    xf = x.astype(jnp.float32)
    mu = jnp.mean(xf, axis=-1, keepdims=True)
    var = jnp.mean(jnp.square(xf - mu), axis=-1, keepdims=True)
    y = (xf - mu) * lax.rsqrt(var + EPS)
    return (y * g.astype(jnp.float32) + b.astype(jnp.float32)).astype(x.dtype)

def causal_dw_conv(x, w, b):
    k = w.shape[0]
    y = lax.conv_general_dilated(
        x, w[:, None, :].astype(x.dtype), window_strides=(1,), padding=((k - 1, 0),),
        dimension_numbers=("NWC", "WIO", "NWC"), feature_group_count=x.shape[-1])
    return y + b

def rg_lru(xb, w_a, b_a, w_i, b_i, lam):
    bsz, s, w = xb.shape
    xh = xb.reshape(bsz, s, LRU_BLOCKS, LRU_BW)
    r = jax.nn.sigmoid(jnp.einsum("bshi,hij->bshj", xh, w_a).reshape(bsz, s, w) + b_a)
    i = jax.nn.sigmoid(jnp.einsum("bshi,hij->bshj", xh, w_i).reshape(bsz, s, w) + b_i)
    log_a = -LRU_C * r.astype(jnp.float32) * jax.nn.softplus(-lam.astype(jnp.float32))
    a = jnp.exp(log_a)
    mult = jnp.sqrt(-jnp.expm1(2.0 * log_a))
    u = mult * (i * xb).astype(jnp.float32)

    def combine(left, right):
        a1, b1 = left
        a2, b2 = right
        return a1 * a2, a2 * b1 + b2

    _, h = lax.associative_scan(combine, (a, u), axis=1)
    return h.astype(xb.dtype)

def gla_chunked(q, k, v, lg):
    bsz, s, h, dk = q.shape
    n = s // GLA_CHUNK

    def chunk(t):
        return t.reshape(bsz, n, GLA_CHUNK, h, t.shape[-1]).transpose(0, 3, 1, 2, 4)

    q, k, v, lg = chunk(q) * (dk ** -0.5), chunk(k), chunk(v), chunk(lg)
    b = lax.cumsum(lg, axis=3)
    b_last = b[:, :, :, -1:, :]
    q_in = q * jnp.exp(b)
    k_in = k * jnp.exp(-b)
    mask = jnp.tril(jnp.ones((GLA_CHUNK, GLA_CHUNK), dtype=bool))
    scores = jnp.where(mask, jnp.einsum("bhncd,bhnjd->bhncj", q_in, k_in), 0.0)
    o_intra = jnp.einsum("bhncj,bhnje->bhnce", scores, v)
    kv = jnp.einsum("bhncd,bhnce->bhnde", k * jnp.exp(b_last - b), v)
    decay = jnp.exp(b_last[:, :, :, 0, :])

    def step(state, inp):
        d, kvn = inp
        return d[..., None] * state + kvn, state

    s0 = jnp.zeros((bsz, h, dk, v.shape[-1]), jnp.float32)
    _, s_prev = lax.scan(step, s0, (decay.transpose(2, 0, 1, 3), kv.transpose(2, 0, 1, 3, 4)))
    s_prev = s_prev.transpose(1, 2, 0, 3, 4)
    o = o_intra + jnp.einsum("bhncd,bhnde->bhnce", q_in, s_prev)
    return o.transpose(0, 2, 3, 1, 4).reshape(bsz, s, h, v.shape[-1])

def token_mix(h, w_in, conv_dw_w, conv_dw_b, conv_ln_g, conv_ln_b, lru_conv_w, lru_conv_b,
              lru_w_a, lru_b_a, lru_w_i, lru_b_i, lru_lam, gla_w_gate, gla_b_gate, gla_norm_g, w_out):
    bsz, s, _ = h.shape
    sizes = [CONV_W, CONV_W, LRU_W, LRU_W, GLA_HEADS * GLA_DK, GLA_HEADS * GLA_DK, GLA_V, GLA_RANK, GLA_V]
    z = h @ w_in
    cv_v, cv_g, lr_x, lr_y, q, k, v, g_lr, og = jnp.split(z, np.cumsum(sizes)[:-1].tolist(), axis=-1)
    u = cv_v * jax.nn.sigmoid(cv_g)
    u = causal_dw_conv(u, conv_dw_w, conv_dw_b)
    u = jax.nn.silu(layer_norm(u, conv_ln_g, conv_ln_b))
    r = rg_lru(causal_dw_conv(lr_x, lru_conv_w, lru_conv_b), lru_w_a, lru_b_a, lru_w_i, lru_b_i, lru_lam)
    r = r * jax.nn.gelu(lr_y)
    lg = jax.nn.log_sigmoid((g_lr @ gla_w_gate + gla_b_gate).astype(jnp.float32)) / GLA_TAU
    o = gla_chunked(q.reshape(bsz, s, GLA_HEADS, GLA_DK).astype(jnp.float32),
                    k.reshape(bsz, s, GLA_HEADS, GLA_DK).astype(jnp.float32),
                    v.reshape(bsz, s, GLA_HEADS, GLA_DV).astype(jnp.float32),
                    lg.reshape(bsz, s, GLA_HEADS, GLA_DK))
    o = rms_norm(o, gla_norm_g.reshape(GLA_HEADS, GLA_DV)).reshape(bsz, s, GLA_V).astype(h.dtype)
    o = o * jax.nn.silu(og)
    mixed = jnp.concatenate([u, r, o], axis=-1)
    return mixed @ w_out

def hier_moe(h, w_rg, b_rg, w_re, b_re, w_gate, w_up, w_down):
    hf = h.astype(jnp.float32)
    g_logits = hf @ w_rg.astype(jnp.float32) + b_rg.astype(jnp.float32)
    p_g = jax.nn.softmax(g_logits, axis=-1)
    g_star = jnp.argmax(g_logits, axis=-1)
    p_sel = jnp.take_along_axis(p_g, g_star[..., None], axis=-1)
    e_all = jnp.einsum("bsd,gde->bsge", hf, w_re.astype(jnp.float32)) + b_re.astype(jnp.float32)
    e_logits = jnp.take_along_axis(e_all, g_star[..., None, None], axis=2)[:, :, 0]
    top_v, top_i = lax.top_k(e_logits, TOP_K)
    top_w = jax.nn.softmax(top_v, axis=-1) * p_sel
    w_in_group = jnp.sum(jax.nn.one_hot(top_i, EXPERTS_PER_GROUP) * top_w[..., None], axis=-2)
    comb = (jax.nn.one_hot(g_star, N_GROUPS)[..., None] * w_in_group[..., None, :]).astype(h.dtype)
    y = jnp.zeros_like(h)
    for g in range(N_GROUPS):
        a = jnp.einsum("bsd,edf->bsef", h, w_gate[g])
        up = jnp.einsum("bsd,edf->bsef", h, w_up[g])
        hid = jax.nn.silu(a) * up * comb[:, :, g, :, None]
        y = y + jnp.einsum("bsef,efd->bsd", hid, w_down[g])
    return y

def first_inputs(seed: int = 0) -> dict:
    key = jax.random.key(seed)
    ks = jax.random.split(key, 32)
    f32 = jnp.float32

    def nrm(k, shape, scale):
        return jax.random.normal(k, shape, f32) * scale

    L = DEPTH
    a0 = jax.random.uniform(ks[14], (L, LRU_W), f32, 0.9, 0.999)
    return {
        "x": nrm(ks[0], (BATCH, SEQ, D_MODEL), 1.0),
        "c": nrm(ks[1], (BATCH, D_MODEL), 1.0),
        "w_ada": nrm(ks[2], (L, D_MODEL, 6 * D_MODEL), 0.5 * D_MODEL ** -0.5),
        "b_ada": nrm(ks[3], (L, 6 * D_MODEL), 0.02),
        "g_mix": 1.0 + nrm(ks[4], (L, D_MODEL), 0.02),
        "w_in": nrm(ks[5], (L, D_MODEL, IN_WIDTH), D_MODEL ** -0.5),
        "conv_dw_w": nrm(ks[6], (L, CONV_K, CONV_W), CONV_K ** -0.5),
        "conv_dw_b": nrm(ks[7], (L, CONV_W), 0.02),
        "conv_ln_g": 1.0 + nrm(ks[8], (L, CONV_W), 0.02),
        "conv_ln_b": nrm(ks[9], (L, CONV_W), 0.02),
        "lru_conv_w": nrm(ks[10], (L, LRU_CONV_K, LRU_W), LRU_CONV_K ** -0.5),
        "lru_conv_b": nrm(ks[11], (L, LRU_W), 0.02),
        "lru_w_a": nrm(ks[12], (L, LRU_BLOCKS, LRU_BW, LRU_BW), LRU_BW ** -0.5),
        "lru_b_a": nrm(ks[13], (L, LRU_W), 0.02),
        "lru_w_i": nrm(ks[15], (L, LRU_BLOCKS, LRU_BW, LRU_BW), LRU_BW ** -0.5),
        "lru_b_i": nrm(ks[16], (L, LRU_W), 0.02),
        "lru_lam": jnp.log(a0) - jnp.log1p(-a0),
        "gla_w_gate": nrm(ks[17], (L, GLA_RANK, GLA_HEADS * GLA_DK), GLA_RANK ** -0.5),
        "gla_b_gate": nrm(ks[18], (L, GLA_HEADS * GLA_DK), 0.02),
        "gla_norm_g": 1.0 + nrm(ks[19], (L, GLA_V), 0.02),
        "w_out": nrm(ks[20], (L, D_MIX, D_MODEL), D_MIX ** -0.5),
        "g_ffn": 1.0 + nrm(ks[21], (L, D_MODEL), 0.02),
        "w_route_group": nrm(ks[22], (L, D_MODEL, N_GROUPS), D_MODEL ** -0.5),
        "b_route_group": nrm(ks[23], (L, N_GROUPS), 0.01),
        "w_route_expert": nrm(ks[24], (L, N_GROUPS, D_MODEL, EXPERTS_PER_GROUP), D_MODEL ** -0.5),
        "b_route_expert": nrm(ks[25], (L, N_GROUPS, EXPERTS_PER_GROUP), 0.01),
        "w_gate": nrm(ks[26], (L, N_GROUPS, EXPERTS_PER_GROUP, D_MODEL, D_EXPERT), D_MODEL ** -0.5),
        "w_up": nrm(ks[27], (L, N_GROUPS, EXPERTS_PER_GROUP, D_MODEL, D_EXPERT), D_MODEL ** -0.5),
        "w_down": nrm(ks[28], (L, N_GROUPS, EXPERTS_PER_GROUP, D_EXPERT, D_MODEL), D_EXPERT ** -0.5),
        "g_final": 1.0 + nrm(ks[29], (D_MODEL,), 0.02),
    }

def first_block(x, c, w_ada, b_ada, g_mix, w_in, conv_dw_w, conv_dw_b, conv_ln_g, conv_ln_b,
              lru_conv_w, lru_conv_b, lru_w_a, lru_b_a, lru_w_i, lru_b_i, lru_lam,
              gla_w_gate, gla_b_gate, gla_norm_g, w_out, g_ffn, w_route_group, b_route_group,
              w_route_expert, b_route_expert, w_gate, w_up, w_down, g_final):
    c_act = jax.nn.silu(c)
    for l in range(DEPTH):
        mod = (c_act @ w_ada[l] + b_ada[l])[:, None, :]
        sh1, sc1, gt1, sh2, sc2, gt2 = jnp.split(mod, 6, axis=-1)
        h = rms_norm(x, g_mix[l]) * (1.0 + sc1) + sh1
        x = x + gt1 * token_mix(h, w_in[l], conv_dw_w[l], conv_dw_b[l], conv_ln_g[l], conv_ln_b[l],
                                lru_conv_w[l], lru_conv_b[l], lru_w_a[l], lru_b_a[l], lru_w_i[l],
                                lru_b_i[l], lru_lam[l], gla_w_gate[l], gla_b_gate[l], gla_norm_g[l],
                                w_out[l])
        h = rms_norm(x, g_ffn[l]) * (1.0 + sc2) + sh2
        x = x + gt2 * hier_moe(h, w_route_group[l], b_route_group[l], w_route_expert[l],
                               b_route_expert[l], w_gate[l], w_up[l], w_down[l])
    return rms_norm(x, g_final)


GRID_W = 64
CTX_LEN = 256

RET_HEADS = 4
RET_QK_DIM = 128
RET_V_DIM = 256
RET_QK_WIDTH = RET_HEADS * RET_QK_DIM
RET_V_WIDTH = RET_HEADS * RET_V_DIM
RET_CHUNK = 128
ROPE_BASE = 10000.0

HY_WIDTH = 512
HY_SHORT = 3
HY_POS_DIM = 33
HY_BANDS = (HY_POS_DIM - 1) // 2
HY_FFN = 64
HY_DECAY_TARGET = 1e-2
HY_FAST_PCT = 0.3
HY_SLOW_PCT = 1.5

EXPERTS_PER_GROUP_2 = 8
N_EXPERTS = N_GROUPS * EXPERTS_PER_GROUP_2
EXPERT_HIDDEN = 512
MOE_BLOCK = 128

IN_WIDTH_2 = 2 * RET_QK_WIDTH + 2 * RET_V_WIDTH + 3 * HY_WIDTH + 2 * D_MODEL
IN_SPLITS = (RET_QK_WIDTH, 2 * RET_QK_WIDTH, 2 * RET_QK_WIDTH + RET_V_WIDTH, 2 * RET_QK_WIDTH + 2 * RET_V_WIDTH, 2 * RET_QK_WIDTH + 2 * RET_V_WIDTH + 3 * HY_WIDTH, 2 * RET_QK_WIDTH + 2 * RET_V_WIDTH + 3 * HY_WIDTH + D_MODEL)


def rms_norm_2(x, gain=None):
    x32 = x.astype(jnp.float32)
    y = x32 * lax.rsqrt(jnp.mean(jnp.square(x32), axis=-1, keepdims=True) + EPS)
    if gain is not None:
        y = y * gain.astype(jnp.float32)
    return y.astype(x.dtype)

def modulate(h, shift, scale):
    return h * (1.0 + scale) + shift

def grid_rope_angles(n_tokens):
    rows = n_tokens // GRID_W
    r, col = jnp.meshgrid(jnp.arange(rows, dtype=jnp.float32), jnp.arange(GRID_W, dtype=jnp.float32), indexing='ij')
    n_freq = RET_QK_DIM // 4
    inv_freq = ROPE_BASE ** (-jnp.arange(n_freq, dtype=jnp.float32) / n_freq)
    return r.reshape(-1)[:, None] * inv_freq, col.reshape(-1)[:, None] * inv_freq

def rope_1d(x, ang):
    n_freq = ang.shape[-1]
    x1, x2 = x[..., :n_freq], x[..., n_freq:]
    cos, sin = jnp.cos(ang), jnp.sin(ang)
    return jnp.concatenate([x1 * cos - x2 * sin, x1 * sin + x2 * cos], axis=-1)

def rope_grid(x, ang_row, ang_col):
    half = RET_QK_DIM // 2
    return jnp.concatenate([rope_1d(x[..., :half], ang_row), rope_1d(x[..., half:], ang_col)], axis=-1)

def split_heads(t, n_heads):
    b, n, _ = t.shape
    return t.reshape(b, n, n_heads, -1).transpose(0, 2, 1, 3)

def retention_scan(q, k, v, log_g, s0, strict):
    b, h, n, _ = q.shape
    dv = v.shape[-1]
    n_chunks = n // RET_CHUNK
    pos = jnp.arange(RET_CHUNK, dtype=jnp.float32)
    diff = pos[:, None] - pos[None, :]
    mask = (diff > 0) if strict else (diff >= 0)
    lg = log_g[:, None, None]
    decay_in = jnp.where(mask[None], jnp.exp(lg * jnp.maximum(diff, 0.0)[None]), 0.0)
    decay_q = jnp.exp(lg * (pos + 1.0)[None, :, None])
    decay_k = jnp.exp(lg * (RET_CHUNK - 1.0 - pos)[None, :, None])
    decay_chunk = jnp.exp(lg * RET_CHUNK)

    def chunks(t):
        return t.reshape(b, h, n_chunks, RET_CHUNK, t.shape[-1]).transpose(2, 0, 1, 3, 4)

    def step(state, qkv):
        qc, kc, vc = qkv
        scores = jnp.einsum('bhid,bhjd->bhij', qc, kc) * decay_in
        out = jnp.einsum('bhij,bhjv->bhiv', scores, vc) + jnp.einsum('bhid,bhdv->bhiv', qc, state) * decay_q
        state = state * decay_chunk + jnp.einsum('bhjd,bhjv->bhdv', kc * decay_k, vc)
        return state, out

    s_final, o = lax.scan(step, s0, (chunks(q), chunks(k), chunks(v)))
    return o.transpose(1, 2, 0, 3, 4).reshape(b, h, n, dv), s_final

def retention_bidir(q, k, v, log_g, s0_fwd, s0_bwd):
    o_f, s_f = retention_scan(q, k, v, log_g[0], s0_fwd, False)
    o_b, s_b = retention_scan(jnp.flip(q, 2), jnp.flip(k, 2), jnp.flip(v, 2), log_g[1], s0_bwd, True)
    return o_f + jnp.flip(o_b, 2), s_f, s_b

def retention_readout(o, g):
    b, h, n, dv = o.shape
    o = rms_norm_2(o).transpose(0, 2, 1, 3).reshape(b, n, h * dv)
    return jax.nn.silu(g) * o.astype(g.dtype)

def short_conv(u, w, bias):
    n = u.shape[1]
    pad = HY_SHORT // 2
    up = jnp.pad(u, ((0, 0), (pad, pad), (0, 0)))
    return sum(up[:, j:j + n] * w[j] for j in range(HY_SHORT)) + bias

def hyena_filters(n, w1, b1, freq, w2, b2, w3):
    f32 = jnp.float32
    t = jnp.arange(n, dtype=f32) / n
    bands = jnp.linspace(1e-4, HY_BANDS - 1, HY_BANDS, dtype=f32)
    phase = 2.0 * math.pi * t[:, None] * bands[None, :]
    feats = jnp.concatenate([t[:, None], jnp.cos(phase), -jnp.sin(phase)], axis=-1)
    freq = freq.astype(f32)
    hid = jnp.sin(freq * (feats @ w1.astype(f32) + b1.astype(f32)))
    hid = jnp.sin(freq * (hid @ w2.astype(f32) + b2.astype(f32)))
    filt = hid @ w3.astype(f32)
    slow = abs(math.log(HY_DECAY_TARGET)) / HY_SLOW_PCT
    fast = abs(math.log(HY_DECAY_TARGET)) / HY_FAST_PCT
    deltas = jnp.tile(jnp.linspace(slow, fast, HY_WIDTH, dtype=f32), 2)
    filt = filt * jnp.exp(-t[:, None] * deltas[None, :])
    filt = filt / jnp.sum(jnp.abs(filt), axis=0, keepdims=True)
    return filt[:, :HY_WIDTH], filt[:, HY_WIDTH:]

def long_conv_bidir(z, h_fwd, h_bwd):
    n = z.shape[1]
    nfft = 2 * n
    zf = jnp.fft.rfft(z.astype(jnp.float32), n=nfft, axis=1)
    hf = jnp.fft.rfft(h_fwd, n=nfft, axis=0) + jnp.conj(jnp.fft.rfft(h_bwd, n=nfft, axis=0))
    return jnp.fft.irfft(zf * hf[None], n=nfft, axis=1)[:, :n]

def hyena_branch(u, conv_w, conv_b, ffn_w1, ffn_b1, ffn_freq, ffn_w2, ffn_b2, ffn_w3, skip):
    x0, x1, v = jnp.split(short_conv(u, conv_w, conv_b), 3, axis=-1)
    z = x1 * v
    h_fwd, h_bwd = hyena_filters(u.shape[1], ffn_w1, ffn_b1, ffn_freq, ffn_w2, ffn_b2, ffn_w3)
    y = long_conv_bidir(z, h_fwd, h_bwd).astype(u.dtype) + z * skip
    return x0 * y

def merge_branches(ret_gated, hy_out, gate_ret, gate_hy, ret_w_o, hy_w_o, w_out):
    mixed = jax.nn.sigmoid(gate_ret) * (ret_gated @ ret_w_o) + jax.nn.sigmoid(gate_hy) * (hy_out @ hy_w_o)
    return mixed @ w_out

def moe_ffn(u, rg_w, rg_b, re_w, re_b, w1, w3, w2):
    n_tok = u.shape[0]
    f32 = jnp.float32
    group_p = jax.nn.softmax((u @ rg_w).astype(f32) + rg_b.astype(f32), axis=-1)
    p_star, g_star = lax.top_k(group_p, 1)
    expert_logits = ((u @ re_w).astype(f32) + re_b.astype(f32)).reshape(n_tok, N_GROUPS, EXPERTS_PER_GROUP_2)
    in_group = jnp.take_along_axis(expert_logits, g_star[:, :, None], axis=1)[:, 0]
    w_top, e_top = lax.top_k(jax.nn.softmax(in_group, axis=-1), TOP_K)
    weights = p_star * w_top / jnp.sum(w_top, axis=-1, keepdims=True)
    expert_id = g_star * EXPERTS_PER_GROUP_2 + e_top
    n_assign = n_tok * TOP_K
    flat_e = expert_id.reshape(n_assign)
    flat_tok = jnp.arange(n_assign, dtype=jnp.int32) // TOP_K
    flat_w = weights.reshape(n_assign)
    order = jnp.argsort(flat_e)
    se, stok, sw = flat_e[order], flat_tok[order], flat_w[order]
    counts = jnp.bincount(flat_e, length=N_EXPERTS)
    starts = jnp.cumsum(counts) - counts
    padded = (counts + MOE_BLOCK - 1) // MOE_BLOCK * MOE_BLOCK
    padded_end = jnp.cumsum(padded)
    padded_start = padded_end - padded
    dest = padded_start[se] + jnp.arange(n_assign, dtype=jnp.int32) - starts[se]
    n_blocks = -(-(n_assign + N_EXPERTS * (MOE_BLOCK - 1)) // MOE_BLOCK)
    n_rows = n_blocks * MOE_BLOCK
    row_tok = jnp.zeros((n_rows,), jnp.int32).at[dest].set(stok)
    block_expert = jnp.minimum(jnp.searchsorted(padded_end, jnp.arange(n_blocks, dtype=jnp.int32) * MOE_BLOCK, side='right'), N_EXPERTS - 1)
    xb = u[row_tok].reshape(n_blocks, MOE_BLOCK, u.shape[1])

    def expert_block(args):
        xblk, e = args
        return (jax.nn.silu(xblk @ w1[e]) * (xblk @ w3[e])) @ w2[e]

    yb = lax.map(expert_block, (xb, block_expert)).reshape(n_rows, u.shape[1])
    y = yb[dest] * sw[:, None].astype(u.dtype)
    return jax.ops.segment_sum(y, stok, num_segments=n_tok)

def second_inputs(seed: int = 0) -> dict:
    key = jax.random.key(seed)
    ks = jax.random.split(key, 32)
    f32 = jnp.float32

    def nrm(k, shape, scale):
        return scale * jax.random.normal(k, shape, f32)

    base_logit = np.log(2.0 ** (5 + np.arange(RET_HEADS)) - 1.0).astype(np.float32)
    return {
        'x': nrm(ks[0], (BATCH, SEQ, D_MODEL), 1.0),
        'c': nrm(ks[1], (BATCH, D_MODEL), 1.0),
        'ctx': nrm(ks[2], (BATCH, CTX_LEN, D_MODEL), 1.0),
        'c_ctx': nrm(ks[3], (D_MODEL,), 1.0),
        'ada_w': nrm(ks[4], (DEPTH, D_MODEL, 6 * D_MODEL), 0.5 * D_MODEL ** -0.5),
        'ada_b': nrm(ks[5], (DEPTH, 6 * D_MODEL), 0.02),
        'norm1_g': 1.0 + nrm(ks[6], (DEPTH, D_MODEL), 0.05),
        'norm2_g': 1.0 + nrm(ks[7], (DEPTH, D_MODEL), 0.05),
        'w_in': nrm(ks[8], (DEPTH, D_MODEL, IN_WIDTH_2), D_MODEL ** -0.5),
        'b_in': nrm(ks[9], (DEPTH, IN_WIDTH_2), 0.02),
        'ret_decay_logit': jnp.asarray(base_logit)[None, None, :] + nrm(ks[10], (DEPTH, 2, RET_HEADS), 0.1),
        'ret_w_o': nrm(ks[11], (DEPTH, RET_V_WIDTH, D_MODEL), RET_V_WIDTH ** -0.5),
        'hy_conv_w': nrm(ks[12], (DEPTH, HY_SHORT, 3 * HY_WIDTH), HY_SHORT ** -0.5),
        'hy_conv_b': nrm(ks[13], (DEPTH, 3 * HY_WIDTH), 0.02),
        'hy_ffn_w1': nrm(ks[14], (DEPTH, HY_POS_DIM, HY_FFN), HY_POS_DIM ** -0.5),
        'hy_ffn_b1': nrm(ks[15], (DEPTH, HY_FFN), 0.02),
        'hy_ffn_freq': 1.0 + nrm(ks[16], (DEPTH, HY_FFN), 0.05),
        'hy_ffn_w2': nrm(ks[17], (DEPTH, HY_FFN, HY_FFN), HY_FFN ** -0.5),
        'hy_ffn_b2': nrm(ks[18], (DEPTH, HY_FFN), 0.02),
        'hy_ffn_w3': nrm(ks[19], (DEPTH, HY_FFN, 2 * HY_WIDTH), HY_FFN ** -0.5),
        'hy_skip': nrm(ks[20], (DEPTH, HY_WIDTH), 0.5),
        'hy_w_o': nrm(ks[21], (DEPTH, HY_WIDTH, D_MODEL), HY_WIDTH ** -0.5),
        'w_out': nrm(ks[22], (DEPTH, D_MODEL, D_MODEL), D_MODEL ** -0.5),
        'router_group_w': nrm(ks[23], (DEPTH, D_MODEL, N_GROUPS), D_MODEL ** -0.5),
        'router_group_b': nrm(ks[24], (DEPTH, N_GROUPS), 0.01),
        'router_expert_w': nrm(ks[25], (DEPTH, D_MODEL, N_EXPERTS), D_MODEL ** -0.5),
        'router_expert_b': nrm(ks[26], (DEPTH, N_EXPERTS), 0.01),
        'expert_w1': nrm(ks[27], (DEPTH, N_EXPERTS, D_MODEL, EXPERT_HIDDEN), D_MODEL ** -0.5),
        'expert_w3': nrm(ks[28], (DEPTH, N_EXPERTS, D_MODEL, EXPERT_HIDDEN), D_MODEL ** -0.5),
        'expert_w2': nrm(ks[29], (DEPTH, N_EXPERTS, EXPERT_HIDDEN, D_MODEL), EXPERT_HIDDEN ** -0.5),
        'final_norm_g': 1.0 + nrm(ks[30], (D_MODEL,), 0.05),
    }

def second_block(x, c, ctx, c_ctx, ada_w, ada_b, norm1_g, norm2_g, w_in, b_in, ret_decay_logit, ret_w_o, hy_conv_w, hy_conv_b, hy_ffn_w1, hy_ffn_b1, hy_ffn_freq, hy_ffn_w2, hy_ffn_b2, hy_ffn_w3, hy_skip, hy_w_o, w_out, router_group_w, router_group_b, router_expert_w, router_expert_b, expert_w1, expert_w3, expert_w2, final_norm_g):
    f32 = jnp.float32
    batch, n_tokens = x.shape[0], x.shape[1]
    ang_row, ang_col = grid_rope_angles(n_tokens)
    silu_c = jax.nn.silu(c)
    silu_cc = jax.nn.silu(c_ctx)
    k_scale = RET_QK_DIM ** -0.5
    for layer in range(DEPTH):
        last = layer == DEPTH - 1
        sh1, sc1, gt1, sh2, sc2, gt2 = jnp.split((silu_c @ ada_w[layer] + ada_b[layer])[:, None, :], 6, axis=-1)
        csh1, csc1, cgt1, csh2, csc2, cgt2 = jnp.split(silu_cc @ ada_w[layer] + ada_b[layer], 6, axis=-1)
        h = modulate(rms_norm_2(x, norm1_g[layer]), sh1, sc1)
        hc = modulate(rms_norm_2(ctx, norm1_g[layer]), csh1, csc1)
        q, k, v, g, hy_u, gate_ret, gate_hy = jnp.split(h @ w_in[layer] + b_in[layer], IN_SPLITS, axis=-1)
        qc, kc, vc, gc, hyc_u, gate_ret_c, gate_hy_c = jnp.split(hc @ w_in[layer] + b_in[layer], IN_SPLITS, axis=-1)
        log_g = jax.nn.log_sigmoid(ret_decay_logit[layer].astype(f32))
        zero_state = jnp.zeros((batch, RET_HEADS, RET_QK_DIM, RET_V_DIM), f32)
        o_ctx, s_fwd, s_bwd = retention_bidir(split_heads(qc, RET_HEADS).astype(f32), split_heads(kc, RET_HEADS).astype(f32) * k_scale, split_heads(vc, RET_HEADS).astype(f32), log_g, zero_state, zero_state)
        q_h = rope_grid(split_heads(q, RET_HEADS).astype(f32), ang_row, ang_col)
        k_h = rope_grid(split_heads(k, RET_HEADS).astype(f32), ang_row, ang_col) * k_scale
        o_lat, _, _ = retention_bidir(q_h, k_h, split_heads(v, RET_HEADS).astype(f32), log_g, s_fwd, s_bwd)
        hy_args = (hy_conv_w[layer], hy_conv_b[layer], hy_ffn_w1[layer], hy_ffn_b1[layer], hy_ffn_freq[layer], hy_ffn_w2[layer], hy_ffn_b2[layer], hy_ffn_w3[layer], hy_skip[layer])
        out_args = (ret_w_o[layer], hy_w_o[layer], w_out[layer])
        moe_args = (router_group_w[layer], router_group_b[layer], router_expert_w[layer], router_expert_b[layer], expert_w1[layer], expert_w3[layer], expert_w2[layer])
        mix = merge_branches(retention_readout(o_lat, g), hyena_branch(hy_u, *hy_args), gate_ret, gate_hy, *out_args)
        x = x + gt1 * mix
        h2 = modulate(rms_norm_2(x, norm2_g[layer]), sh2, sc2)
        if last:
            x = x + gt2 * moe_ffn(h2.reshape(-1, D_MODEL), *moe_args).reshape(x.shape)
        else:
            mix_c = merge_branches(retention_readout(o_ctx, gc), hyena_branch(hyc_u, *hy_args), gate_ret_c, gate_hy_c, *out_args)
            ctx = ctx + cgt1 * mix_c
            h2c = modulate(rms_norm_2(ctx, norm2_g[layer]), csh2, csc2)
            y = moe_ffn(jnp.concatenate([h2.reshape(-1, D_MODEL), h2c.reshape(-1, D_MODEL)], axis=0), *moe_args)
            n_lat = batch * n_tokens
            x = x + gt2 * y[:n_lat].reshape(x.shape)
            ctx = ctx + cgt2 * y[n_lat:].reshape(ctx.shape)
    return rms_norm_2(x, final_norm_g)


def setup_inputs(seed=0):
    out = dict(first_inputs(seed))
    for name, value in second_inputs(seed + 1).items():
        if name != "x":
            out[name + "_2"] = value
    return out


def reference(
    x, c, w_ada, b_ada, g_mix, w_in, conv_dw_w, conv_dw_b, conv_ln_g, conv_ln_b, lru_conv_w,
    lru_conv_b, lru_w_a, lru_b_a, lru_w_i, lru_b_i, lru_lam, gla_w_gate, gla_b_gate, gla_norm_g,
    w_out, g_ffn, w_route_group, b_route_group, w_route_expert, b_route_expert, w_gate, w_up,
    w_down, g_final, c_2, ctx_2, c_ctx_2, ada_w_2, ada_b_2, norm1_g_2, norm2_g_2, w_in_2,
    b_in_2, ret_decay_logit_2, ret_w_o_2, hy_conv_w_2, hy_conv_b_2, hy_ffn_w1_2, hy_ffn_b1_2,
    hy_ffn_freq_2, hy_ffn_w2_2, hy_ffn_b2_2, hy_ffn_w3_2, hy_skip_2, hy_w_o_2, w_out_2,
    router_group_w_2, router_group_b_2, router_expert_w_2, router_expert_b_2, expert_w1_2,
    expert_w3_2, expert_w2_2, final_norm_g_2,
):
    x = first_block(
        x, c, w_ada, b_ada, g_mix, w_in, conv_dw_w, conv_dw_b, conv_ln_g, conv_ln_b, lru_conv_w,
        lru_conv_b, lru_w_a, lru_b_a, lru_w_i, lru_b_i, lru_lam, gla_w_gate, gla_b_gate,
        gla_norm_g, w_out, g_ffn, w_route_group, b_route_group, w_route_expert, b_route_expert,
        w_gate, w_up, w_down, g_final,
    )
    return second_block(
        x, c_2, ctx_2, c_ctx_2, ada_w_2, ada_b_2, norm1_g_2, norm2_g_2, w_in_2, b_in_2,
        ret_decay_logit_2, ret_w_o_2, hy_conv_w_2, hy_conv_b_2, hy_ffn_w1_2, hy_ffn_b1_2,
        hy_ffn_freq_2, hy_ffn_w2_2, hy_ffn_b2_2, hy_ffn_w3_2, hy_skip_2, hy_w_o_2, w_out_2,
        router_group_w_2, router_group_b_2, router_expert_w_2, router_expert_b_2, expert_w1_2,
        expert_w3_2, expert_w2_2, final_norm_g_2,
    )


_drawn_inputs = setup_inputs


def setup_inputs(seed=0):
    import zlib

    import numpy as np

    out = dict(_drawn_inputs(seed))
    spreads = {}
    factors = {'g_mix': 6.458,
     'conv_dw_b': 6.959,
     'conv_ln_g': 8.0,
     'conv_ln_b': 8.0,
     'lru_conv_b': 6.719,
     'lru_b_a': 8.0,
     'lru_b_i': 8.0,
     'gla_b_gate': 8.0,
     'gla_norm_g': 8.0,
     'g_ffn': 4.647,
     'b_route_group': 8.0,
     'b_route_expert': 7.612,
     'g_final': 2.701,
     'norm1_g_2': 3.479,
     'norm2_g_2': 3.423,
     'b_in_2': 6.27,
     'hy_conv_b_2': 8.0,
     'hy_ffn_b1_2': 8.0,
     'hy_ffn_freq_2': 8.0,
     'hy_ffn_b2_2': 8.0,
     'router_group_b_2': 8.0,
     'router_expert_b_2': 8.0}
    for name, (base, spread) in spreads.items():
        noise = np.random.default_rng([zlib.crc32(name.encode()), seed]).standard_normal(out[name].shape)
        drawn = base * np.exp(spread * noise) if base else spread * noise
        out[name] = jnp.asarray(drawn.astype(out[name].dtype))
    for name, factor in factors.items():
        out[name] = (out[name] * factor).astype(out[name].dtype)
    return out
```

```python
from contextlib import ExitStack

import concourse.bass as bass
import numpy as np
from concourse import mybir

F32 = mybir.dt.float32
ALU = mybir.AluOpType
ACT = mybir.ActivationFunctionType
AX = mybir.AxisListType

P = 128
T = 256
TT = T // P
D = 1024
DK = D // P
EPS = 1e-6

CONV_W, CONV_K = 256, 31
LRU_W, LRU_K = 384, 4
GH, GDK, GDV, GCH = 4, 48, 96, 64
PAIR = 2 * GDK
CT, LT = CONV_W // P, LRU_W // P

RH, RDK, RDV = 4, 128, 256
HYW = 512
HYT = HYW // P

SLOTS = 6
SLAB = 4096
BANKS = 8

WIN_CUTS = [(0, 512), (512, 896), (896, 1280), (1280, 1664), (1664, 2064), (2064, 2448)]
WOUT_CUTS = [(0, 384), (384, 768), (768, 1024)]
WIN2_ORDER = [512, 1024, 1536, 0, 2048, 2560, 3072, 3584, 4096, 4608, 5120, 5632, 6144]

COLS = [("c", 8), ("c2", 16), ("b_ada", 48), ("b_ada2", 48), ("g_mix", 8), ("conv_w", 62), ("conv_b", 2), ("ln_g", 2),
        ("ln_b", 2), ("lru_w", 12), ("lru_b", 3), ("lru_ba", 3), ("lru_bi", 3), ("lam", 3), ("gla_b", 2), ("gla_g", 4),
        ("g_ffn", 8), ("g_final", 8), ("g1", 8), ("g2", 8), ("b_in", 52), ("decay", 8), ("hy_w", 36), ("hy_b", 12),
        ("f_b1", 1), ("f_freq", 1), ("f_b2", 1), ("skip", 4), ("g_out", 8), ("br1", 20), ("br2", 36),
        ("eps", 1), ("head", 2), ("neg_t", 2), ("pos", 2), ("rpos", 2), ("pos1", 2), ("tie4", 4), ("tie8", 8)]
AT, n_ = {}, 0
for name_, w_ in COLS:
    AT[name_] = n_
    n_ += w_
NCOL = n_


def stream_plan():
    ada1 = [("ada1", j) for j in range(12)]
    ada2 = [("ada2", j) for j in range(12)]
    first = (ada1[0:4] + [("win", j) for j in range(6)] + ada1[4:12] + ada2[0:4] + [("wout", j) for j in range(3)]
             + ada2[4:12])
    second = ([("win2", j) for j in range(13)] + [("ret_o", 0), ("ret_o", 1), ("hy_o", 0), ("wout2", 0), ("wout2", 1)])
    return first, second


def bank_plan():
    names = ["n1_ss", "f1", "a1_0", "f2", "f3_00", "f3_01", "f3_10", "f3_11", "a1_1", "f4_0", "f4_1",
             "f5_0", "f5_1", "f5_2", "f5_3",
             "cvg", "cvv", "lrx01", "lrx2", "lry01", "lry2", "q01", "k01", "v0", "v1", "glr", "lgp", "og01", "og23",
             "a1_2", "lru0", "lru1", "lru2", "a1_3", "k2t", "sc01", "sc23", "kv0", "kv1", "kv2", "o01", "o23",
             "os01", "os23", "a1_4", "a1_5", "a2_0", "a2_1", "mu", "var",
             "wo01", "wo23", "wo45", "wo67", "n2_ss", "a2_2", "nc_ss", "a2_3", "rt1", "a2_4", "a2_5"]
    names += [f"moe1_{b}" for b in range(BANKS)]
    names += ["nf_ss", "m1_ss"]
    names += ["kT01", "kT23", "kc0", "kc1", "vx00", "vx01", "vc00", "vc01", "vx10", "vx11", "vc10", "vc11",
              "st0", "st1", "st2", "st3", "rk01", "rk23", "q2_01", "q2_23", "rq01", "rq23",
              "g01", "g23", "g45", "g67", "s0", "s1", "s2", "s3", "o0", "o1", "rs0", "o2", "rs1", "o3", "rs2", "rs3"]
    names += [f"hy{2 * j}" for j in range(6)] + [f"gr{2 * j}" for j in range(4)] + [f"gh{2 * j}" for j in range(4)]
    names += ["zt0", "zt1", "zr0", "zi0", "zr1", "zi1", "yt0", "yt2"]
    names += [f"ro{2 * j}" for j in range(4)] + [f"ho{2 * j}" for j in range(4)] + [f"w2_{2 * j}" for j in range(4)]
    names += ["m2_ss", "rt2"] + [f"moe2_{b}" for b in range(BANKS)] + ["mf_ss"]
    place = {}
    used = [0] * BANKS
    at = 0
    for n in names:
        b = int(n[-1]) if n.startswith("moe") else at % BANKS
        at += not n.startswith("moe")
        place[n] = (b, used[b])
        used[b] += 1
    return place


def build(nc, a, out):
    first, second = stream_plan()
    place = bank_plan()
    N1 = len(first)
    E1, E2 = 16, 32
    N2 = N1 + 3 * E1
    N3 = N2 + len(second)
    slab_no = {key: n for n, key in enumerate(first)}
    slab_no.update({key: N2 + n for n, key in enumerate(second)})

    with ExitStack() as ctx:
        def sb(name, shape):
            return ctx.enter_context(nc.sbuf_tensor(name, shape, F32))

        sems = {}

        def S(name):
            if name not in sems:
                sems[name] = ctx.enter_context(nc.semaphore(name.replace(" ", "_")))
            return sems[name]

        psum = [ctx.enter_context(nc.psum_tensor(f"bank{b}", [P, 512], F32)) for b in range(BANKS)]
        filled = [S(f"filled{b}") for b in range(BANKS)]
        drained = [S(f"drained{b}") for b in range(BANKS)]
        landed = [S(f"landed{s}") for s in range(SLOTS)]
        freed = [S(f"freed{s}") for s in range(SLOTS)]

        ring = sb("ring", [P, SLOTS, SLAB])
        cols = sb("cols_sb", [P, NCOL])
        X = sb("X", [P, DK, T])
        H = sb("H", [P, DK, T])
        W = sb("W", [P, DK, T])
        HF = sb("HF", [P, 2, 2, HYW])
        ident = sb("ident", [P, P])
        ones = sb("ones", [P, P])
        wr = sb("wr", [P, DK * 20 + DK * 36])
        root = sb("root", [P, T])
        rstd = sb("rstd", [P, T])
        mod1 = sb("mod1", [P, 48])
        mod2 = sb("mod2", [P, 48, 2])
        gs = sb("gs", [P, 5, DK])
        cact = sb("cact", [P, 24])
        lgs = sb("lgs", [P, 5, 8])
        sml = sb("sml", [P, 24])
        lru_scale = sb("lru_scale", [P, 2, LT])
        gdec = sb("gdec", [PAIR, 2, 4])
        ctxdec = sb("ctxdec", [P, 2, RH, TT])
        backb = sb("backb", [P, RH])
        route = sb("route", [P, 304])
        comb = sb("comb", [P, TT, 32])
        pool = sb("pool", [P, 69 * T])

        def view(tile, *shape, rows=P):
            n = int(np.prod(shape))
            v = pool[0:rows, int(tile * T):int(tile * T) + n]
            if len(shape) == 1:
                return v
            names = "abcd"[:len(shape)]
            return v.rearrange(f"p ({' '.join(names)}) -> p {' '.join(names)}",
                               **{k: s for k, s in zip(names[1:], shape[1:])})

        def col(name, i=0, n=1, rows=slice(0, P)):
            return cols[rows, AT[name] + i:AT[name] + i + n]

        upad = view(0, CT, CONV_K - 1 + T)
        u2 = view(3, CT, T)
        lxpad = view(5, LT, LRU_K - 1 + T)
        xc = view(9, LT, T)
        rg = view(12, LT, T)
        ig = view(15, LT, T)
        ag = view(18, LT, T)
        gy = view(21, LT, T)
        cvsg = view(12, CT, T)
        qT = view(24, 2, T, rows=PAIR)
        kT1 = view(26, 2, T, rows=PAIR)
        vtok = view(28, TT, GH * GDV)
        glr = view(31, T, rows=16)
        lgx = view(32, 2, T, rows=PAIR)
        bcum = view(34, 2, T, rows=PAIR)
        diff = view(36, 2, T, rows=PAIR)
        eb = view(38, 2, T, rows=PAIR)
        lruw = view(40, 2, LT, P)
        gmask = view(43, P)
        segm = view(43.5, T, rows=PAIR)
        glaw = view(44.5, 2, PAIR, rows=16)
        qz = view(46, GH, T, rows=PAIR)
        kin = view(50, 2, T, rows=PAIR)
        k2z = view(52, TT, 2, 2, PAIR)
        sm = view(56, GH, TT, P)
        states = view(60, 3, 2, 2 * GDV, rows=PAIR)
        sog = view(65, GH, T)
        feats = view(12, T, rows=33)
        fw1 = view(13, 64, rows=33)
        fw2 = view(13.25, 64, rows=64)
        deltas = view(14, HYW)
        basis = view(16, 2, TT, T)
        fw3 = view(20, 1024, rows=64)
        arg = view(24, T, rows=64)
        rnd = view(25, T, rows=64)
        hid1 = view(26, T, rows=64)
        hid2 = view(27, T, rows=64)
        filt = view(46, TT, 2, HYW)
        absf = view(54, TT, 2, HYW)
        decay = view(62, TT, HYW)
        hid = view(45, 2, 4, T)
        act_g = view(53, 2, T)
        act_w = view(55, 2, T)
        diag = view(57, 2, TT, P)
        HC = view(0, DK, T)
        sigR = view(0, DK, T)
        VC = view(8, TT, 1024)
        sigH = view(8, DK, T)
        Ef, Eb = view(8, T), view(9, T)
        qf, qb = view(10, 2, T), view(12, 2, T)
        S0 = view(16, RH, 2, RDV)
        x0 = view(16, HYT, T)
        zT = view(20, HYT, T)
        brow = view(24, 1536, rows=1)
        kdec = view(24, RH, 2, TT, P)
        sg = view(24, DK, T)
        hypad = view(32, 12, T + 2)
        kr = view(45, RH, T)
        qr = view(49, RH, T)
        hyo = view(45, HYT, T)
        cv1, cv2 = view(49, T), view(50, T)
        V = view(53, TT, 1024)
        ztok = view(53, TT, HYW)
        ztmp = view(57, TT, HYW)
        mcs = view(61, 2, TT, T)
        rope = view(65, 2, T)
        perm = view(67, P)
        irow = view(67.5, T)
        W4 = W[:, 0:4, :]
        kraw, qraw = W[:, 0:4, :], W[:, 4:8, :]
        KC = W[:, 4:8, :].rearrange("p (t a) b -> p t (a b)", t=TT)
        Dm = W[:, 0:2, :]
        Pm = [W[:, 2:4, :], W[:, 4:6, :]]
        osq = W[:, 6:8, :]
        Y = W[:, :, :].rearrange("p (r t a) b -> p r t (a b)", r=2, t=TT)

        zeros = view(59, 512)
        dtmp, rtmp = view(0, 2, T), view(2, 2, T)
        gla_root = view(56, GH, T, rows=GDV)
        X1 = ["wo01", "wo23", "wo45", "wo67"]
        X4 = ["w2_0", "w2_2", "w2_4", "w2_6"]
        NORM = {key: n for n, key in enumerate(["n1", "n2", "nc", "nf", "m1", "m2", "mf"])}
        rv = {"gexp": route[:, 80:88].rearrange("p (t g) -> p t g", t=TT), "pexp": route[:, 256:258]}

        def lru_neg(t):
            return lru_scale[:, 0, t:t + 1]

        def lru_pos(t):
            return lru_scale[:, 1, t:t + 1]

        def bank(name):
            return psum[place[name][0]]

        def wait_product(eng, name):
            b, use = place[name]
            eng.wait_ge(filled[b], use + 1)

        def gone(name):
            return drained[place[name][0]]

        def wait_taken(eng, name):
            b, use = place[name]
            eng.wait_ge(drained[b], use + 1)

        def wait_slab(eng, n):
            eng.wait_ge(landed[n % SLOTS], 32 * (n // SLOTS + 1))

        def slab(key, k, w, base=0):
            s = slab_no[key] % SLOTS
            return ring[:, s, base:base + k * w].rearrange("p (k w) -> p k w", k=k)

        def bc(ap, shape):
            return ap.broadcast_to(shape)

        block = ctx.enter_context(nc.Block())

        def experts(sp, w_gate, w_up, w_down, n0, count):
            up = [w.rearrange("e (k p) f -> e p k f", p=P) for w in (w_gate, w_up, w_down)]
            with sp.Fori(0, count // 2) as i:
                for j in range(6):
                    n, w = n0 + j, up[j % 3]
                    k = w.shape[2]
                    s = n % SLOTS
                    src = w[bass.ds(i * 2 + j // 3, 1)].rearrange("o p k f -> p (o k) f")
                    dst = ring[:, s, :].rearrange("p (k w) -> p k w", k=k)
                    sp.wait_ge(freed[s], i + n // SLOTS)
                    sp.dma_start(dst[:, 0:k // 2], src[:, 0:k // 2]).then_inc(landed[s], 16)
                    sp.dma_start(dst[:, k // 2:k], src[:, k // 2:k]).then_inc(landed[s], 16)

        @block.sync
        def _(sp):
            def load(n, halves):
                s = n % SLOTS
                if n >= SLOTS:
                    sp.wait_ge(freed[s], n // SLOTS)
                for dst, src in halves:
                    sp.dma_start(dst, src).then_inc(landed[s], 16)

            def columns(n, w, c0, c1):
                v = w.rearrange("(k p) f -> p k f", p=P)[:, :, c0:c1]
                d = ring[:, n % SLOTS, 0:8 * (c1 - c0)].rearrange("p (k w) -> p k w", k=8)
                load(n, [(d[:, 0:4], v[:, 0:4]), (d[:, 4:8], v[:, 4:8])])

            for key in first + second:
                n = slab_no[key]
                kind, j = key
                if n == N2:
                    experts(sp, a["w_gate"], a["w_up"], a["w_down"], N1, E1)
                if kind == "ada1":
                    columns(n, a["w_ada"], 512 * j, 512 * j + 512)
                elif kind == "ada2":
                    columns(n, a["ada_w_2"], 512 * j, 512 * j + 512)
                elif kind == "win":
                    columns(n, a["w_in"], *WIN_CUTS[j])
                elif kind == "wout":
                    c0, c1 = WOUT_CUTS[j]
                    w = c1 - c0
                    top = a["w_out"][0:640, c0:c1].rearrange("(k p) f -> p k f", p=P)
                    low = a["w_out"][640:1024, c0:c1].rearrange("(k p) f -> p k f", p=GDV)
                    load(n, [(ring[:, n % SLOTS, 0:5 * w].rearrange("p (k w) -> p k w", k=5), top),
                             (ring[0:GDV, n % SLOTS, 5 * w:9 * w].rearrange("p (k w) -> p k w", k=4), low)])
                elif kind == "win2":
                    columns(n, a["w_in_2"], WIN2_ORDER[j], WIN2_ORDER[j] + 512)
                elif kind == "ret_o":
                    columns(n, a["ret_w_o_2"], 512 * j, 512 * j + 512)
                elif kind == "wout2":
                    columns(n, a["w_out_2"], 512 * j, 512 * j + 512)
                elif kind == "hy_o":
                    v = a["hy_w_o_2"].rearrange("(k p) f -> p k f", p=P)
                    d = ring[:, n % SLOTS, :].rearrange("p (k w) -> p k w", k=4)
                    load(n, [(d[:, 0:2], v[:, 0:2]), (d[:, 2:4], v[:, 2:4])])
            experts(sp, a["expert_w1_2"], a["expert_w3_2"], a["expert_w2_2"], N3, E2)

        @block.gpsimd
        def _(pool_e):
            pool_e.memset(ones[:, :], 1.0).then_inc(S("ones set"), 1)
            pool_e.memset(upad[:, :, 0:CONV_K - 1], 0.0)
            pool_e.memset(lxpad[:, :, 0:LRU_K - 1], 0.0).then_inc(S("pads zero"), 1)
            for n in range(4):
                wait_taken(pool_e, f"f5_{n}")
            pool_e.memset(k2z[:, :, :, :, :], 0.0).then_inc(S("heads zero"), 1)
            for n in X1:
                wait_taken(pool_e, n)
            pool_e.memset(hypad[:, :, 0:1], 0.0)
            pool_e.memset(hypad[:, :, T + 1:T + 2], 0.0).then_inc(S("hyena pads zero"), 1)

        def readout_act(act, h):
            wait_product(act, f"o{h}")
            nc.scalar.activation(osq, bank(f"o{h}")[:, :].rearrange("p (a b) -> p a b", a=2),
                                 ACT.Square).then_inc(S("readout squared"), 1)
            wait_product(act, f"rs{h}")
            if h:
                act.wait_ge(S("readout ready"), h)
            nc.scalar.activation(root[:, :], bank(f"rs{h}")[:, 0:T], ACT.Sqrt, scale=1.0 / RDV,
                                 bias=col("eps")).then_inc(gone(f"rs{h}"), 1)

        @block.scalar
        def _(act):
            steps = [0]

            def link(ins):
                steps[0] += 1
                ins.then_inc(S("scalar step"), 1)
                act.wait_ge(S("scalar step"), steps[0])

            def squares(key, src):
                for j in range(4):
                    nc.scalar.activation(W[:, 2 * j:2 * j + 2, :], src[:, 2 * j:2 * j + 2, :],
                                         ACT.Square).then_inc(S("squared"), 1)

            def norm_root(key):
                wait_product(act, key + "_ss")
                nc.scalar.activation(root[:, :], bank(key + "_ss")[:, 0:T], ACT.Sqrt, scale=1.0 / D,
                                     bias=col("eps")).then_inc(gone(key + "_ss"), 1)

            def modulate(key, dst, scales, shifts, ready):
                act.wait_ge(S("norm scaled"), NORM[key] + 1)
                for k in range(DK):
                    if shifts is None:
                        ins = nc.scalar.activation(dst[:, k, :], dst[:, k, :], ACT.Copy, scale=scales(k))
                    else:
                        ins = nc.scalar.activation(dst[:, k, :], dst[:, k, :], ACT.Identity, scale=scales(k),
                                                   bias=shifts(k))
                    ins.then_inc(S(ready), 1)

            act.dma_start(cols[:, :], a["cols"]).then_inc(S("cols loaded"), 16)
            act.dma_start(X[:, :, :], a["xT"]).then_inc(S("x loaded"), 16)
            act.dma_start(view(12, 12 * T), a["fpack"]).then_inc(S("filter pack loaded"), 16)
            act.dma_start(ident[:, :], a["ident"]).then_inc(S("mixer pack loaded"), 16)
            act.dma_start(view(40, 1408), a["mpack"]).then_inc(S("mixer pack loaded"), 16)
            act.dma_start(wr[:, :], a["wr"]).then_inc(S("mixer pack loaded"), 16)

            act.wait_ge(S("cols loaded"), 16)
            nc.scalar.activation(cact[:, :], col("c", 0, 24), ACT.Silu).then_inc(S("c ready"), 1)
            link(nc.scalar.activation(sml[:, 0:3], col("lam", 0, 3), ACT.Abs))
            nc.scalar.activation(sml[:, 0:3], sml[:, 0:3], ACT.Exp, scale=-1.0).then_inc(S("softplus exp"), 1)
            act.wait_ge(S("softplus arg"), 1)
            nc.scalar.activation(sml[:, 6:9], sml[:, 3:6], ACT.Ln).then_inc(S("softplus log"), 1)
            act.wait_ge(S("x loaded"), 16)
            squares("n1", X)
            norm_root("n1")
            act.wait_ge(S("filter pack loaded"), 16)
            for tt in range(TT):
                nc.scalar.activation(decay[:, tt, :], deltas, ACT.Exp,
                                     scale=col("neg_t", tt)).then_inc(S("decay ready"), 1)
            for h, dst in enumerate((hid1, hid2)):
                act.wait_ge(S("sine argument"), h + 1)
                nc.scalar.activation(dst, arg, ACT.Sin).then_inc(S("sine ready"), 1)
            for n in range(4):
                wait_taken(act, f"f3_{n // 2}{n % 2}")
                nc.scalar.activation(absf[:, n // 2, n % 2, :], filt[:, n // 2, n % 2, :],
                                     ACT.Abs).then_inc(S("filter abs"), 1)
            modulate("n1", H, lambda k: gs[:, 0, k:k + 1], lambda k: mod1[:, k:k + 1], "h1 ready")
            for n in range(4):
                wait_product(act, f"f5_{n}")
                nc.scalar.activation(HF[:, n // 2, n % 2, :], bank(f"f5_{n}")[:, :], ACT.Copy,
                                     scale=1.0 / T).then_inc(gone(f"f5_{n}"), 1)

            wait_product(act, "cvg")
            nc.scalar.activation(cvsg, bank("cvg")[:, :].rearrange("p (a b) -> p a b", a=2),
                                 ACT.Sigmoid).then_inc(gone("cvg"), 1)
            for n, (t0, m) in {"lrx01": (0, 2), "lrx2": (2, 1)}.items():
                wait_product(act, n)
                nc.scalar.activation(lxpad[:, t0:t0 + m, LRU_K - 1:],
                                     bank(n)[:, 0:m * T].rearrange("p (a b) -> p a b", a=m),
                                     ACT.Copy).then_inc(gone(n), 1)
            for n, (t0, m) in {"lry01": (0, 2), "lry2": (2, 1)}.items():
                wait_product(act, n)
                nc.scalar.activation(gy[:, t0:t0 + m, :], bank(n)[:, 0:m * T].rearrange("p (a b) -> p a b", a=m),
                                     ACT.Gelu_apprx_tanh).then_inc(gone(n), 1)
            for n, dst in (("q01", qT), ("k01", kT1)):
                wait_product(act, n)
                nc.scalar.activation(dst, bank(n)[0:PAIR, :].rearrange("p (a b) -> p a b", a=2),
                                     ACT.Copy).then_inc(gone(n), 1)
            for tt in range(TT):
                wait_product(act, f"v{tt}")
                nc.scalar.activation(vtok[:, tt, :], bank(f"v{tt}")[:, 0:GH * GDV],
                                     ACT.Copy).then_inc(gone(f"v{tt}"), 1)
            wait_product(act, "glr")
            nc.scalar.activation(glr, bank("glr")[0:16, 0:T], ACT.Copy).then_inc(gone("glr"), 1)
            wait_product(act, "lgp")
            for pr in range(2):
                ins = nc.scalar.activation(lgx[:, pr, :], bank("lgp")[0:PAIR, pr * T:pr * T + T], ACT.Identity,
                                           bias=col("gla_b", pr, rows=slice(0, PAIR)))
            ins.then_inc(gone("lgp"), 1)
            wait_taken(act, "lgp")
            lnb = W[0:PAIR, 0:2, :]
            link(nc.scalar.activation(lnb, lgx, ACT.Abs))
            link(nc.scalar.activation(lnb, lnb, ACT.Exp, scale=-1.0))
            nc.scalar.activation(lnb, lnb, ACT.Ln, bias=1.0).then_inc(S("gate log ready"), 1)
            for t in range(LT):
                wait_product(act, f"lru{t}")
                nc.scalar.activation(rg[:, t, :], bank(f"lru{t}")[:, 0:T], ACT.Sigmoid, bias=col("lru_ba", t))
                nc.scalar.activation(ig[:, t, :], bank(f"lru{t}")[:, T:2 * T], ACT.Sigmoid,
                                     bias=col("lru_bi", t)).then_inc(gone(f"lru{t}"), 1)
            wait_taken(act, "lru2")
            act.wait_ge(S("softplus ready"), 1)
            for t in range(LT):
                nc.scalar.activation(ag[:, t, :], rg[:, t, :], ACT.Exp, scale=lru_neg(t))
            for t in range(LT):
                nc.scalar.activation(rg[:, t, :], rg[:, t, :], ACT.Tanh, scale=lru_pos(t)).then_inc(S("lru decay"), 1)
            act.wait_ge(S("gate sums ready"), 2)
            nc.scalar.activation(eb, bcum, ACT.Exp, scale=1.0 / 16.0)
            nc.scalar.activation(kin, bcum, ACT.Exp, scale=-1.0 / 16.0)
            nc.scalar.activation(diff, diff, ACT.Exp, scale=1.0 / 16.0)
            nc.scalar.activation(gdec[:, :, :], bcum.rearrange("p a (c s) -> p a c s", s=GCH)[:, :, :, GCH - 1],
                                 ACT.Exp, scale=1.0 / 16.0).then_inc(S("gate powers ready"), 1)
            act.wait_ge(S("lru root arg"), 1)
            nc.scalar.activation(xc, xc, ACT.Sqrt, scale=2.0).then_inc(S("lru root ready"), 1)
            for n, h in (("og01", 0), ("og23", 2)):
                wait_product(act, n)
                nc.scalar.activation(sog[0:GDV, h:h + 2, :], bank(n)[0:GDV, :].rearrange("p (a b) -> p a b", a=2),
                                     ACT.Silu).then_inc(gone(n), 1)
            for n, h in (("o01", 0), ("o23", 2)):
                wait_product(act, n)
                nc.scalar.activation(W[0:GDV, 4 + h:6 + h, :], bank(n)[0:GDV, :].rearrange("p (a b) -> p a b", a=2),
                                     ACT.Square).then_inc(S("gla squared"), 1)
            for n, h in (("os01", 0), ("os23", 2)):
                wait_product(act, n)
                nc.scalar.activation(gla_root[:, h:h + 2, :], bank(n)[0:GDV, :].rearrange("p (a b) -> p a b", a=2),
                                     ACT.Sqrt, scale=1.0 / GDV, bias=col("eps", rows=slice(0, GDV))).then_inc(gone(n), 1)
            wait_taken(act, "mu")
            nc.scalar.activation(W[:, 2:4, :], u2, ACT.Square).then_inc(S("conv squared"), 1)
            wait_product(act, "var")
            nc.scalar.activation(root[:, :], bank("var")[:, 0:T], ACT.Sqrt, scale=1.0 / CONV_W,
                                 bias=col("eps")).then_inc(gone("var"), 1)
            act.wait_ge(S("conv scaled"), 1)
            for t in range(CT):
                nc.scalar.activation(u2[:, t, :], u2[:, t, :], ACT.Silu, scale=col("ln_g", t),
                                     bias=col("ln_b", t)).then_inc(S("mix u ready"), 1)

            for n in X1:
                wait_taken(act, n)
            act.dma_start(HC, a["ctxT"]).then_inc(S("ctx loaded"), 16)
            act.dma_start(view(61, 1920), a["lpack"]).then_inc(S("late pack loaded"), 16)
            act.dma_start(brow, a["brow"]).then_inc(S("late pack loaded"), 16)
            squares("n2", X)
            norm_root("n2")
            modulate("n2", H, lambda k: gs[:, 1, k:k + 1], lambda k: mod1[:, 24 + k:25 + k], "h2 ready")
            act.wait_ge(S("ctx loaded"), 16)
            squares("nc", HC)
            norm_root("nc")
            modulate("nc", HC, lambda k: gs[:, 2, k:k + 1], lambda k: mod2[:, k, 1:2], "ctx ready")

            def routing(m):
                act.wait_ge(S("route group arg"), m + 1)
                nc.scalar.activation(rv["gexp"], rv["gexp"], ACT.Exp).then_inc(S("route group exp"), 1)
                act.wait_ge(S("route pair arg"), m + 1)
                nc.scalar.activation(rv["pexp"], rv["pexp"], ACT.Exp).then_inc(S("route pair exp"), 1)

            def experts_act(m, count):
                with act.Fori(0, count // 2) as i:
                    for j in range(8):
                        act.wait_ge(S(f"moe{m} product"), i * 8 + j + 1)
                        nc.scalar.activation(act_g[:, j % 2, :], psum[4 + j % 2][:, 0:T],
                                             ACT.Silu).then_inc(S(f"moe{m} silu ready"), 1)

            routing(0)
            experts_act(1, E1)

            for b in range(4):
                wait_taken(act, f"moe1_{b}")
            squares("nf", X)
            norm_root("nf")
            modulate("nf", X, lambda k: col("g_final", k), None, "x3 ready")
            act.wait_ge(S("x3 ready"), 8)
            squares("m1", X)
            norm_root("m1")
            modulate("m1", H, lambda k: gs[:, 3, k:k + 1], lambda k: mod2[:, k, 0:1], "h3 ready")

            def two(n, h, dst, func, bias=None, scale=1.0):
                wait_product(act, n)
                for t in range(2):
                    ins = nc.scalar.activation(dst[:, h + t, :], bank(n)[:, t * T:t * T + T], func,
                                               bias=col("b_in", bias + t), scale=scale)
                ins.then_inc(gone(n), 1)

            link(nc.scalar.activation(lgs[:, 0, :], col("decay", 0, 8), ACT.Abs))
            nc.scalar.activation(lgs[:, 0, :], lgs[:, 0, :], ACT.Exp, scale=-1.0).then_inc(S("decay exp"), 1)
            act.wait_ge(S("decay arg"), 1)
            nc.scalar.activation(lgs[:, 2, :], lgs[:, 1, :], ACT.Ln).then_inc(S("decay log"), 1)
            two("kT01", 0, kraw, ACT.Identity, 4)
            two("kT23", 2, kraw, ACT.Identity, 6)
            for tt in range(TT):
                wait_product(act, f"kc{tt}")
                nc.scalar.activation(KC[:, tt, :], bank(f"kc{tt}")[:, :], ACT.Copy).then_inc(gone(f"kc{tt}"), 1)
            for half in range(2):
                for what, dst in (("vx", V), ("vc", VC)):
                    for tt in range(TT):
                        n = f"{what}{half}{tt}"
                        wait_product(act, n)
                        nc.scalar.activation(dst[:, tt, 512 * half:512 * half + 512], bank(n)[:, :],
                                             ACT.Copy).then_inc(gone(n), 1)
            act.wait_ge(S("log decay ready"), 1)
            for tt in range(TT):
                nc.scalar.activation(ctxdec[:, 0, :, tt], lgs[:, 3, 0:4], ACT.Exp, scale=col("rpos", tt))
                nc.scalar.activation(ctxdec[:, 1, :, tt], lgs[:, 3, 4:8], ACT.Exp,
                                     scale=col("pos", tt)).then_inc(S("ctx decay ready"), 1)
            for h in range(RH):
                wait_product(act, f"st{h}")
                nc.scalar.activation(S0[:, h, :, :], bank(f"st{h}")[:, :].rearrange("p (a b) -> p a b", a=2),
                                     ACT.Copy).then_inc(gone(f"st{h}"), 1)
            two("q2_01", 0, qraw, ACT.Identity, 0)
            two("q2_23", 2, qraw, ACT.Identity, 2)
            for j in range(4):
                two(f"g{2 * j}{2 * j + 1}", 2 * j, sg, ACT.Silu, 16 + 2 * j)
            for h in range(RH):
                act.wait_ge(S("decay matrix arg"), h + 1)
                act.wait_ge(S("ctx queries ready"), h) if h else None
                nc.scalar.activation(Dm, Dm, ACT.Exp)
                nc.scalar.activation(Ef, irow, ACT.Exp, scale=lgs[:, 3, h:h + 1])
                nc.scalar.activation(Eb, irow, ACT.Exp, scale=lgs[:, 4, 4 + h:5 + h],
                                     bias=backb[:, h:h + 1]).then_inc(S("decay matrix ready"), 1)
                if h:
                    readout_act(act, h - 1)
            readout_act(act, RH - 1)
            act.wait_ge(S("hyena pads zero"), 1)
            for j in range(6):
                wait_product(act, f"hy{2 * j}")
                for t in range(2):
                    ins = nc.scalar.activation(hypad[:, 2 * j + t, 1:T + 1], bank(f"hy{2 * j}")[:, t * T:t * T + T],
                                               ACT.Identity, bias=col("b_in", 24 + 2 * j + t))
                ins.then_inc(gone(f"hy{2 * j}"), 1)
            act.wait_ge(S("readout ready"), RH)
            for j in range(4):
                two(f"gr{2 * j}", 2 * j, sigR, ACT.Sigmoid, 36 + 2 * j)
            for j in range(4):
                two(f"gh{2 * j}", 2 * j, sigH, ACT.Sigmoid, 44 + 2 * j)
            for tt in range(TT):
                wait_product(act, f"zt{tt}")
                nc.scalar.activation(ztok[:, tt, :], bank(f"zt{tt}")[:, :], ACT.Copy).then_inc(gone(f"zt{tt}"), 1)

            for n in X4:
                wait_taken(act, n)
            squares("m2", X)
            norm_root("m2")
            modulate("m2", H, lambda k: gs[:, 4, k:k + 1], lambda k: mod2[:, 24 + k, 0:1], "h4 ready")
            routing(1)
            experts_act(2, E2)
            for b in range(4):
                wait_taken(act, f"moe2_{b}")
            squares("mf", X)
            norm_root("mf")
            modulate("mf", X, lambda k: col("g_out", k), None, "y ready")
            for j in range(2):
                act.wait_ge(S("y ready"), 4 * j + 4)
                act.dma_start(out[:, 4 * j:4 * j + 4, :], X[:, 4 * j:4 * j + 4, :]).then_inc(S("stored"), 16)
            act.wait_ge(S("stored"), 32)

        @block.vector
        def _(dve):
            steps = [0]

            def link(ins):
                steps[0] += 1
                ins.then_inc(S("vector step"), 1)
                dve.wait_ge(S("vector step"), steps[0])

            def take(ins, name):
                ins.then_inc(gone(name), 1)
                wait_taken(dve, name)

            V_ = nc.vector

            def log1p(y, w, lnw, tmp, out):
                link(V_.tensor_scalar(tmp, w, 1.0, None, ALU.subtract))
                link(V_.tensor_scalar(out, tmp, 0.0, None, ALU.is_equal))
                link(V_.tensor_tensor(tmp, tmp, out, ALU.add))
                link(V_.reciprocal(tmp, tmp))
                link(V_.tensor_tensor(tmp, tmp, lnw, ALU.mult))
                link(V_.tensor_tensor(tmp, tmp, out, ALU.add))
                link(V_.tensor_tensor(out, tmp, y, ALU.mult))

            dve.wait_ge(S("softplus exp"), 1)
            V_.tensor_scalar(sml[:, 3:6], sml[:, 0:3], 1.0, None, ALU.add).then_inc(S("softplus arg"), 1)
            dve.wait_ge(S("softplus log"), 1)
            log1p(sml[:, 0:3], sml[:, 3:6], sml[:, 6:9], sml[:, 9:12], sml[:, 12:15])
            link(V_.tensor_scalar(sml[:, 15:18], col("lam", 0, 3), -1.0, 0.0, ALU.mult, ALU.max))
            link(V_.tensor_tensor(sml[:, 15:18], sml[:, 15:18], sml[:, 12:15], ALU.add))
            V_.tensor_scalar(lru_scale[:, 0, :], sml[:, 15:18], -8.0, None, ALU.mult)
            V_.tensor_scalar(lru_scale[:, 1, :], sml[:, 15:18], 8.0, None, ALU.mult).then_inc(S("softplus ready"), 1)

            TWO_PI = 2.0 * np.pi
            C1 = 6.28125
            C2 = float(np.float32(np.round((TWO_PI - C1) * 2 ** 20) / 2 ** 20))
            C3 = float(np.float32(TWO_PI - C1 - C2))
            MAGIC = 12582912.0
            PI_BELOW = 3.1415925

            def sine_argument(name, bias):
                wait_product(dve, name)
                take(V_.tensor_scalar(arg, bank(name)[0:64, 0:T], col(bias, rows=slice(0, 64)),
                                      col("f_freq", rows=slice(0, 64)), ALU.add, ALU.mult), name)
                link(V_.tensor_scalar(rnd, arg, float(1.0 / TWO_PI), MAGIC, ALU.mult, ALU.add))
                link(V_.tensor_scalar(rnd, rnd, MAGIC, None, ALU.subtract))
                for c in (C1, C2, C3):
                    link(V_.scalar_tensor_tensor(arg, rnd, -c, arg, ALU.mult, ALU.add))
                V_.tensor_scalar(arg, arg, PI_BELOW, -PI_BELOW, ALU.min, ALU.max).then_inc(S("sine argument"), 1)

            def ada1(p):
                wait_product(dve, f"a1_{p}")
                take(V_.tensor_tensor(mod1[:, 8 * p:8 * p + 8], bank(f"a1_{p}")[:, 0:8], col("b_ada", 8 * p, 8),
                                      ALU.add), f"a1_{p}")

            def ada2(p):
                wait_product(dve, f"a2_{p}")
                take(V_.tensor_tensor(mod2[:, 8 * p:8 * p + 8, :],
                                      bank(f"a2_{p}")[:, 0:16].rearrange("p (a b) -> p a b", b=2),
                                      bc(col("b_ada2", 8 * p, 8).unsqueeze(2), [P, 8, 2]), ALU.add), f"a2_{p}")

            def gain(i, g, scale):
                V_.scalar_tensor_tensor(gs[:, i, :], scale, 1.0, col(g, 0, 8), ALU.add, ALU.mult)

            def norm_scale(key, src, dst):
                wait_taken(dve, key + "_ss")
                link(V_.reciprocal(rstd[:, :], root[:, :]))
                V_.tensor_tensor(dst[:, :, :], src[:, :, :], bc(rstd[:, :].unsqueeze(1), [P, DK, T]),
                                 ALU.mult).then_inc(S("norm scaled"), 1)

            sine_argument("f1", "f_b1")
            ada1(0)
            sine_argument("f2", "f_b2")
            for n in range(4):
                name = f"f3_{n // 2}{n % 2}"
                wait_product(dve, name)
                dve.wait_ge(S("decay ready"), n // 2 + 1)
                V_.tensor_tensor(filt[:, n // 2, n % 2, :], bank(name)[:, :], decay[:, n // 2, :],
                                 ALU.mult).then_inc(gone(name), 1)
            ada1(1)
            gain(0, "g_mix", mod1[:, 8:16])
            norm_scale("n1", X, H)
            for half in range(2):
                wait_product(dve, f"f4_{half}")
                take(V_.reciprocal(decay[:, half, :], bank(f"f4_{half}")[:, :]), f"f4_{half}")
            for tt in range(TT):
                ins = V_.tensor_tensor(filt[:, tt, :, :], filt[:, tt, :, :], decay[:, :, :], ALU.mult)
            link(ins)
            V_.tensor_tensor(absf[:, :, 0, :], filt[:, :, 0, :], filt[:, :, 1, :], ALU.add)
            V_.tensor_tensor(absf[:, :, 1, :], filt[:, :, 0, :], filt[:, :, 1, :],
                             ALU.subtract).then_inc(S("filter pair ready"), 1)

            wait_taken(dve, "cvg")
            wait_product(dve, "cvv")
            take(V_.tensor_tensor(upad[:, :, CONV_K - 1:], cvsg, bank("cvv")[:, :].rearrange("p (a b) -> p a b", a=2),
                                  ALU.mult), "cvv")
            dve.wait_ge(S("pads zero"), 1)
            wait_taken(dve, "lrx01")
            wait_taken(dve, "lrx2")
            for j in range(LRU_K):
                for t in range(LT):
                    tap = col("lru_w", t * LRU_K + j)
                    if j == 0:
                        ins = V_.tensor_scalar(xc[:, t, :], lxpad[:, t, 0:T], tap, col("lru_b", t), ALU.mult, ALU.add)
                    else:
                        ins = V_.scalar_tensor_tensor(xc[:, t, :], lxpad[:, t, j:j + T], tap, xc[:, t, :],
                                                      ALU.mult, ALU.add)
                link(ins) if j < LRU_K - 1 else ins.then_inc(S("lru conv ready"), 1)

            def long_conv(taps):
                for j in taps:
                    for t in range(CT):
                        tap = col("conv_w", t * CONV_K + j)
                        if j == 0:
                            ins = V_.tensor_scalar(u2[:, t, :], upad[:, t, 0:T], tap, col("conv_b", t),
                                                   ALU.mult, ALU.add)
                        else:
                            ins = V_.scalar_tensor_tensor(u2[:, t, :], upad[:, t, j:j + T], tap, u2[:, t, :],
                                                          ALU.mult, ALU.add)
                    link(ins) if j < CONV_K - 1 else ins.then_inc(S("conv ready"), 1)

            long_conv(range(0, 10))
            dve.wait_ge(S("gate log ready"), 1)
            link(V_.scalar_tensor_tensor(lgx, lgx, 0.0, W[0:PAIR, 0:2, :], ALU.min, ALU.subtract))
            for pr in range(2):
                ins = V_.tensor_tensor_scan(bcum[:, pr, :], segm, lgx[:, pr, :], 0.0, ALU.mult, ALU.add)
            link(ins)
            for pr in range(2):
                b4 = bcum[:, pr, :].rearrange("p (c s) -> p c s", s=GCH)
                V_.tensor_tensor(diff[:, pr, :].rearrange("p (c s) -> p c s", s=GCH),
                                 bc(b4[:, :, GCH - 1:GCH], [PAIR, T // GCH, GCH]), b4,
                                 ALU.subtract).then_inc(S("gate sums ready"), 1)
            ada1(2)
            wait_taken(dve, "lru2")
            link(V_.tensor_tensor(ig, ig, xc, ALU.mult))
            dve.wait_ge(S("lru decay"), 3)
            link(V_.tensor_scalar(xc, rg, 1.0, None, ALU.add))
            link(V_.reciprocal(xc, xc))
            V_.tensor_tensor(xc, xc, rg, ALU.mult).then_inc(S("lru root arg"), 1)
            dve.wait_ge(S("gate powers ready"), 1)
            dve.wait_ge(S("heads zero"), 1)
            wait_taken(dve, "q01")
            wait_taken(dve, "k01")
            V_.tensor_tensor(diff, diff, kT1, ALU.mult).then_inc(S("gla keys ready"), 1)
            V_.tensor_tensor(kin, kin, kT1, ALU.mult)
            for h in range(GH):
                ins = V_.scalar_tensor_tensor(qz[:, h, :], qT[:, h // 2, :], col("head", h % 2, rows=slice(0, PAIR)),
                                              eb[:, h // 2, :], ALU.mult, ALU.mult)
            ins.then_inc(S("gla queries ready"), 1)
            dve.wait_ge(S("lru root ready"), 1)
            link(V_.tensor_tensor(ig, ig, xc, ALU.mult))
            for t in range(LT):
                ins = V_.tensor_tensor_scan(rg[:, t, :], ag[:, t, :], ig[:, t, :], 0.0, ALU.mult, ALU.add)
            link(ins)
            wait_taken(dve, "lry01")
            wait_taken(dve, "lry2")
            V_.tensor_tensor(gy, gy, rg, ALU.mult).then_inc(S("mix r ready"), 1)
            ada1(3)
            wait_product(dve, "k2t")
            for ch in range(2):
                r = slice(64 * ch, 64 * ch + 64)
                ins = V_.tensor_copy(k2z[r, :, ch, :, :].rearrange("p a b c -> p a (b c)"),
                                     bank("k2t")[r, 0:4 * PAIR].rearrange("p (a b) -> p a b", a=TT))
            ins.then_inc(gone("k2t"), 1)
            for n, h in (("sc01", 0), ("sc23", 2)):
                wait_product(dve, n)
                V_.tensor_tensor(sm[:, h:h + 2, :, :].rearrange("p a b c -> p (a b) c"),
                                 bank(n)[:, :].rearrange("p (a b) -> p a b", a=4),
                                 bc(gmask.unsqueeze(1), [P, 4, P]), ALU.mult).then_inc(gone(n), 1)
            for c in range(3):
                wait_product(dve, f"kv{c}")
                kv = bank(f"kv{c}")[0:PAIR, 0:4 * GDV].rearrange("p (a b) -> p a b", a=2)
                if c == 0:
                    ins = V_.tensor_copy(states[:, 0, :, :], kv)
                else:
                    for pr in range(2):
                        ins = V_.scalar_tensor_tensor(states[:, c, pr, :], states[:, c - 1, pr, :],
                                                      gdec[:, pr, c:c + 1], kv[:, pr, :], ALU.mult, ALU.add)
                take(ins, f"kv{c}")
            long_conv(range(10, CONV_K))
            for n, o, h in (("os01", "o01", 0), ("os23", "o23", 2)):
                wait_taken(dve, n)
                link(V_.reciprocal(gla_root[:, h:h + 2, :], gla_root[:, h:h + 2, :]))
                tmp = W[0:GDV, 4 + h:6 + h, :]
                take(V_.tensor_tensor(tmp, bank(o)[0:GDV, :].rearrange("p (a b) -> p a b", a=2),
                                      gla_root[:, h:h + 2, :], ALU.mult), o)
            wait_taken(dve, "og23")
            for h in range(GH):
                V_.scalar_tensor_tensor(sog[0:GDV, h, :], W[0:GDV, 4 + h, :], col("gla_g", h, rows=slice(0, GDV)),
                                        sog[0:GDV, h, :], ALU.mult, ALU.mult).then_inc(S("mix o ready"), 1)
            ada1(4)
            ada1(5)
            ada2(0)
            ada2(1)
            wait_product(dve, "mu")
            for t in range(CT):
                ins = V_.scalar_tensor_tensor(u2[:, t, :], bank("mu")[:, 0:T], -1.0 / CONV_W, u2[:, t, :],
                                              ALU.mult, ALU.add)
            ins.then_inc(gone("mu"), 1)
            gain(1, "g_ffn", mod1[:, 32:40])
            gain(2, "g1", mod2[:, 8:16, 1])
            gain(3, "g1", mod2[:, 8:16, 0])
            wait_taken(dve, "var")
            link(V_.reciprocal(rstd[:, :], root[:, :]))
            V_.tensor_tensor(u2, u2, bc(rstd[:, :].unsqueeze(1), [P, CT, T]), ALU.mult).then_inc(S("conv scaled"), 1)

            def add_to_x(names, gate, width=2):
                for j, n in enumerate(names):
                    wait_product(dve, n)
                    for t in range(2):
                        k = 2 * j + t
                        ins = V_.scalar_tensor_tensor(X[:, k, :], bank(n)[:, t * T:t * T + T], gate(k), X[:, k, :],
                                                      ALU.mult, ALU.add)
                    ins.then_inc(gone(n), 1)

            add_to_x(X1, lambda k: mod1[:, 16 + k:17 + k])
            norm_scale("n2", X, H)
            ada2(2)
            norm_scale("nc", HC, HC)
            ada2(3)

            def R(lo, n):
                return route[:, lo:lo + n]

            def R2(lo, m):
                return route[:, lo:lo + TT * m].rearrange("p (t m) -> p t m", t=TT)

            def routing(m, n, bias, tie):
                w = 4 + 4 * n
                L = R2(0, w)
                wait_product(dve, f"rt{m + 1}")
                take(V_.tensor_tensor(L, bank(f"rt{m + 1}")[:, 0:TT * w].rearrange("p (t m) -> p t m", t=TT),
                                      bc(col(bias, 0, w).unsqueeze(1), [P, TT, w]), ALU.add), f"rt{m + 1}")
                gmax, gexp, gsum = R(72, 2), rv["gexp"], R(90, 2)
                first, tmp, best = R2(104, 4), R2(280, n), R(94, 2)

                def one_hot(dst, src, top, names_, k):
                    link(V_.tensor_tensor(dst, src, bc(top.unsqueeze(2), [P, TT, k]), ALU.is_equal))
                    link(V_.tensor_tensor(dst, dst, bc(col(names_, 0, k).unsqueeze(1), [P, TT, k]), ALU.mult))
                    link(V_.tensor_reduce(best, dst, AX.X, ALU.max))
                    link(V_.tensor_tensor(dst, dst, bc(best.unsqueeze(2), [P, TT, k]), ALU.is_equal))

                link(V_.tensor_reduce(gmax, L[:, :, 0:4], AX.X, ALU.max))
                V_.tensor_tensor(gexp, L[:, :, 0:4], bc(gmax.unsqueeze(2), [P, TT, 4]),
                                 ALU.subtract).then_inc(S("route group arg"), 1)
                one_hot(first, L[:, :, 0:4], gmax, "tie4", 4)
                es, m1, oh1, e2, m2, oh2 = R2(176, n), R(192, 2), R2(200, n), R2(216, n), R(232, 2), R2(240, n)
                for t in range(TT):
                    prod = route[:, 112:112 + 4 * n].rearrange("p (e g) -> p e g", g=4)
                    link(V_.tensor_tensor(prod, L[:, t, 4:].rearrange("p (g e) -> p e g", g=4),
                                          bc(first[:, t, :].unsqueeze(1), [P, n, 4]), ALU.mult))
                    link(V_.tensor_reduce(es[:, t, :], prod, AX.X, ALU.add))
                link(V_.tensor_reduce(m1, es, AX.X, ALU.max))
                one_hot(oh1, es, m1, f"tie{n}", n)
                link(V_.scalar_tensor_tensor(e2, oh1, -3.0e38, es, ALU.mult, ALU.add))
                link(V_.tensor_reduce(m2, e2, AX.X, ALU.max))
                one_hot(oh2, e2, m2, f"tie{n}", n)
                V_.tensor_tensor(rv["pexp"], m2, m1, ALU.subtract).then_inc(S("route pair arg"), 1)
                dve.wait_ge(S("route group exp"), m + 1)
                link(V_.tensor_reduce(gsum, gexp, AX.X, ALU.add))
                dve.wait_ge(S("route pair exp"), m + 1)
                w1, w2 = R(258, 2), R(260, 2)
                link(V_.tensor_scalar(w1, rv["pexp"], 1.0, None, ALU.add))
                link(V_.tensor_tensor(w1, w1, gsum, ALU.mult))
                link(V_.reciprocal(w1, w1))
                link(V_.tensor_tensor(w2, w1, rv["pexp"], ALU.mult))
                link(V_.tensor_tensor(oh1, oh1, bc(w1.unsqueeze(2), [P, TT, n]), ALU.mult))
                link(V_.tensor_tensor(oh2, oh2, bc(w2.unsqueeze(2), [P, TT, n]), ALU.mult))
                link(V_.tensor_tensor(oh1, oh1, oh2, ALU.add))
                for t in range(TT):
                    link(V_.tensor_tensor(comb[:, t, 0:4 * n].rearrange("p (g e) -> p g e", g=4),
                                          bc(first[:, t, :].unsqueeze(2), [P, 4, n]),
                                          bc(oh1[:, t, :].unsqueeze(1), [P, 4, n]), ALU.mult))

            def experts_dve(m, count):
                V_.memset(zeros, 0.0).then_inc(S("zeros set"), 1)
                dve.sem_inc(S(f"moe{m} hidden"), 2)
                with dve.Fori(0, count // 2) as i:
                    for e in range(2):
                        for t in range(TT):
                            ins = V_.tensor_scalar(diag[:, e, t, :], ident[:, :], comb[:, t, bass.ds(i * 2 + e, 1)],
                                                   None, ALU.mult)
                        ins.then_inc(S(f"moe{m} diagonal ready"), 1)
                        dve.wait_ge(S(f"moe{m} weights spread"), i * 2 + e + 1)
                        for f in range(4):
                            j = 4 * e + f
                            dve.wait_ge(S(f"moe{m} silu ready"), i * 8 + j + 1)
                            V_.tensor_tensor(act_w[:, j % 2, :], act_g[:, j % 2, :],
                                             psum[6][:, e * T:e * T + T], ALU.mult).then_inc(S(f"moe{m} weighed"), 1)
                            dve.wait_ge(S(f"moe{m} weighed"), i * 8 + j + 1)
                            V_.tensor_tensor(hid[:, e, f, :], act_w[:, j % 2, :], psum[4 + j % 2][:, T:2 * T],
                                             ALU.mult).then_inc(S(f"moe{m} hidden"), 1)
                for b in range(4, BANKS):
                    wait_product(dve, f"moe{m}_{b}")
                    dve.sem_inc(drained[b], 1)

            routing(0, 4, "br1", "tie4")
            ada2(4)
            ada2(5)
            link(V_.tensor_scalar(gs[:, 4, :], mod2[:, 32:40, 0], 1.0, None, ALU.add))
            link(V_.tensor_tensor(gs[:, 4, :], gs[:, 4, :], col("g2", 0, 8), ALU.mult))
            experts_dve(1, E1)
            add_to_x([f"moe1_{b}" for b in range(4)], lambda k: mod1[:, 40 + k:41 + k])
            norm_scale("nf", X, X)
            norm_scale("m1", X, H)

            dve.wait_ge(S("decay exp"), 1)
            V_.tensor_scalar(lgs[:, 1, :], lgs[:, 0, :], 1.0, None, ALU.add).then_inc(S("decay arg"), 1)
            dve.wait_ge(S("decay log"), 1)
            log1p(lgs[:, 0, :], lgs[:, 1, :], lgs[:, 2, :], lgs[:, 4, :], lgs[:, 3, :])
            link(V_.scalar_tensor_tensor(lgs[:, 3, :], col("decay", 0, 8), 0.0, lgs[:, 3, :], ALU.min, ALU.subtract))
            V_.tensor_scalar(lgs[:, 4, :], lgs[:, 3, :], -1.0, None, ALU.mult)
            V_.tensor_scalar(backb[:, :], lgs[:, 3, 4:8], float(T + 1), None, ALU.mult).then_inc(S("log decay ready"), 1)
            dve.wait_ge(S("log decay ready"), 1)

            def rotate(name, h, raw, dst, scale):
                wait_product(dve, name)
                cos, sin = (bc(rope[:, i:i + 1, :], [P, 2, T]) for i in range(2))
                link(V_.scalar_tensor_tensor(dst[:, h:h + 2, :], raw[:, h:h + 2, :], scale, cos, ALU.mult, ALU.mult))
                take(V_.scalar_tensor_tensor(raw[:, h:h + 2, :], bank(name)[:, :].rearrange("p (a b) -> p a b", a=2),
                                             scale, sin, ALU.mult, ALU.mult), name)
                V_.tensor_tensor(dst[:, h:h + 2, :], dst[:, h:h + 2, :], raw[:, h:h + 2, :],
                                 ALU.add).then_inc(S("rotated"), 1)

            dve.wait_ge(S("ctx decay ready"), 2)
            wait_product(dve, "vc11")
            wait_taken(dve, "kc1")
            for tt in range(TT):
                for way in range(2):
                    V_.tensor_tensor(kdec[:, :, way, tt, :], KC[:, tt, :].rearrange("p (h d) -> p h d", h=RH),
                                     bc(ctxdec[:, way, :, tt:tt + 1], [P, RH, P]),
                                     ALU.mult).then_inc(S("ctx keys ready"), 1)
            rotate("rk01", 0, kraw, kr, 1.0)
            rotate("rk23", 2, kraw, kr, 1.0)
            rotate("rq01", 0, qraw, qr, float(RDK) ** -0.5)
            rotate("rq23", 2, qraw, qr, float(RDK) ** -0.5)

            def readout(h):
                wait_taken(dve, f"rs{h}")
                link(V_.reciprocal(rstd[:, :], root[:, :]))
                take(V_.tensor_tensor(rtmp, bank(f"o{h}")[:, :].rearrange("p (a b) -> p a b", a=2),
                                      bc(rstd[:, :].unsqueeze(1), [P, 2, T]), ALU.mult), f"o{h}")
                V_.tensor_tensor(sg[:, 2 * h:2 * h + 2, :], sg[:, 2 * h:2 * h + 2, :], rtmp,
                                 ALU.mult).then_inc(S("readout ready"), 1)

            wait_taken(dve, "g67")
            for h in range(RH):
                for jt in range(TT):
                    V_.tensor_scalar(Dm[:, jt, :], irow, col("pos1", jt), lgs[:, 4, 4 + h:5 + h],
                                     ALU.subtract, ALU.mult)
                    ins = V_.tensor_scalar(dtmp[:, jt, :], irow, col("pos1", jt), lgs[:, 3, h:h + 1],
                                           ALU.subtract, ALU.mult)
                link(ins)
                V_.tensor_tensor(Dm, Dm, dtmp, ALU.min).then_inc(S("decay matrix arg"), 1)
                dve.wait_ge(S("decay matrix ready"), h + 1)
                V_.tensor_tensor(qf[:, h % 2, :], qr[:, h, :], Ef, ALU.mult)
                V_.tensor_tensor(qb[:, h % 2, :], qr[:, h, :], Eb, ALU.mult).then_inc(S("ctx queries ready"), 1)
                wait_product(dve, f"s{h}")
                take(V_.tensor_tensor(Pm[h % 2], bank(f"s{h}")[:, :].rearrange("p (a b) -> p a b", a=2), Dm,
                                      ALU.mult), f"s{h}")
                if h:
                    readout(h - 1)
            readout(RH - 1)

            for n in range(6):
                wait_taken(dve, f"hy{2 * n}")
            for c in range(HYT):
                for j in range(3):
                    for dst, t in ((x0[:, c, :], c), (cv1, HYT + c), (cv2, 2 * HYT + c)):
                        tap = col("hy_w", 3 * t + j)
                        if j == 0:
                            ins = V_.tensor_scalar(dst, hypad[:, t, 0:T], tap, col("hy_b", t), ALU.mult, ALU.add)
                        else:
                            ins = V_.scalar_tensor_tensor(dst, hypad[:, t, j:j + T], tap, dst, ALU.mult, ALU.add)
                    link(ins)
                V_.tensor_tensor(zT[:, c, :], cv1, cv2, ALU.mult).then_inc(S("z ready"), 1)
                dve.wait_ge(S("z ready"), c + 1)
            for kt in range(2):
                zr, zi = f"zr{kt}", f"zi{kt}"
                wait_product(dve, zi)
                V_.tensor_tensor(Y[:, 0, kt, :], bank(zr)[:, :], HF[:, 0, kt, :], ALU.mult)
                V_.tensor_tensor(Y[:, 1, kt, :], bank(zr)[:, :], HF[:, 1, kt, :], ALU.mult).then_inc(gone(zr), 1)
                V_.tensor_tensor(ztmp[:, 0, :], bank(zi)[:, :], HF[:, 1, kt, :], ALU.mult)
                take(V_.tensor_tensor(ztmp[:, 1, :], bank(zi)[:, :], HF[:, 0, kt, :], ALU.mult), zi)
                V_.tensor_tensor(Y[:, 0, kt, :], Y[:, 0, kt, :], ztmp[:, 0, :], ALU.subtract)
                V_.tensor_tensor(Y[:, 1, kt, :], Y[:, 1, kt, :], ztmp[:, 1, :], ALU.add).then_inc(S("spectrum ready"), 1)
                dve.wait_ge(S("spectrum ready"), kt + 1)
            for c in range(HYT):
                n = f"yt{c // 2 * 2}"
                wait_product(dve, n)
                ins = V_.scalar_tensor_tensor(zT[:, c, :], zT[:, c, :], col("skip", c),
                                              bank(n)[:, (c % 2) * T:(c % 2) * T + T], ALU.mult, ALU.add)
                if c % 2:
                    take(ins, n)
                    V_.tensor_tensor(hyo[:, c - 1:c + 1, :], zT[:, c - 1:c + 1, :], x0[:, c - 1:c + 1, :],
                                     ALU.mult).then_inc(S("hyena ready"), 1)
            for j in range(4):
                wait_taken(dve, f"gr{2 * j}")
                wait_taken(dve, f"gh{2 * j}")
            for j in range(4):
                n = f"ro{2 * j}"
                wait_product(dve, n)
                V_.tensor_tensor(H[:, 2 * j:2 * j + 2, :], bank(n)[:, :].rearrange("p (a b) -> p a b", a=2),
                                 sigR[:, 2 * j:2 * j + 2, :], ALU.mult).then_inc(gone(n), 1)
            for j in range(4):
                n = f"ho{2 * j}"
                wait_product(dve, n)
                take(V_.tensor_tensor(sigH[:, 2 * j:2 * j + 2, :], bank(n)[:, :].rearrange("p (a b) -> p a b", a=2),
                                      sigH[:, 2 * j:2 * j + 2, :], ALU.mult), n)
                V_.tensor_tensor(H[:, 2 * j:2 * j + 2, :], H[:, 2 * j:2 * j + 2, :], sigH[:, 2 * j:2 * j + 2, :],
                                 ALU.add).then_inc(S("merged"), 1)
            add_to_x(X4, lambda k: mod2[:, 16 + k, 0:1])
            norm_scale("m2", X, H)
            routing(1, 8, "br2", "tie8")
            experts_dve(2, E2)
            add_to_x([f"moe2_{b}" for b in range(4)], lambda k: mod2[:, 40 + k, 0:1])
            norm_scale("mf", X, X)

        @block.tensor
        def _(pe):
            order = list(place)
            done = [0]

            def begin(name):
                while order[done[0]] != name:
                    assert order[done[0]].startswith("a"), (order[done[0]], name)
                    done[0] += 1
                done[0] += 1
                b, use = place[name]
                if use:
                    pe.wait_ge(drained[b], use)
                return psum[b]

            def end(ins, name):
                ins.then_inc(filled[place[name][0]], 1)

            def mm(out_, lhsT, rhs, start, stop):
                return nc.tensor.matmul(out_, lhsT, rhs, start=start, stop=stop)

            def ss(name, src_tiles, signal, base, per):
                b = begin(name)
                n = len(src_tiles)
                for k, t in enumerate(src_tiles):
                    if k % per == 0:
                        pe.wait_ge(S(signal), base + k // per + 1)
                    rows = t.shape[0]
                    ins = mm(b[0:rows, 0:T], ones[0:rows, 0:rows], t, k == 0, k == n - 1)
                end(ins, name)

            def norm(key):
                ss(key + "_ss", [W[:, k, :] for k in range(DK)], "squared", 4 * NORM[key], 2)

            def ada(which, p):
                name = f"a{which}_{p}"
                b = begin(name)
                n = which
                for j in (2 * p, 2 * p + 1):
                    key = (f"ada{which}", j)
                    wait_slab(pe, slab_no[key])
                    w = slab(key, 8, 512)
                    for f in range(4):
                        o = (4 * (j % 2) + f) * n
                        for k in range(DK):
                            rhs = cact[:, k:k + 1] if which == 1 else cact[:, 8 + 2 * k:10 + 2 * k]
                            ins = mm(b[:, o:o + n], w[:, k, f * P:f * P + P], rhs, k == 0, k == DK - 1)
                    if j % 2:
                        free_and_end(ins, key, name)
                    else:
                        ins.then_inc(freed[slab_no[key] % SLOTS], 1)

            def free_and_end(ins, key, name):
                end(ins, name)
                pe.wait_ge(filled[place[name][0]], place[name][1] + 1)
                pe.sem_inc(freed[slab_no[key] % SLOTS], 1)

            def proj(name, w, c0, src, tiles, m=P, free=None, nk=DK):
                b = begin(name)
                for t in range(tiles):
                    for k in range(nk):
                        ins = mm(b[0:m, t * T:t * T + T], w[:, k, c0 + t * m:c0 + t * m + m], src[:, k, :],
                                 k == 0, k == nk - 1)
                if free:
                    free_and_end(ins, free, name)
                else:
                    end(ins, name)

            def by_token(name, w, c0, width, src, tt, free=None, bias=None):
                b = begin(name)
                for k in range(DK):
                    ins = mm(b[:, 0:width], src[:, k, tt * P:tt * P + P], w[:, k, c0:c0 + width], k == 0,
                             k == DK - 1 and bias is None)
                if bias is not None:
                    ins = mm(b[:, 0:width], ones[0:1, :], bias, False, True)
                if free:
                    free_and_end(ins, free, name)
                else:
                    end(ins, name)

            pe.wait_ge(S("ones set"), 1)
            norm("n1")
            pe.wait_ge(S("filter pack loaded"), 16)
            b = begin("f1")
            end(mm(b[0:64, 0:T], fw1, feats, True, True), "f1")
            pe.wait_ge(S("c ready"), 1)
            ada(1, 0)
            pe.wait_ge(S("sine ready"), 1)
            b = begin("f2")
            end(mm(b[0:64, 0:T], fw2, hid1, True, True), "f2")
            pe.wait_ge(S("sine ready"), 2)
            for tt in range(TT):
                for half in range(2):
                    b = begin(f"f3_{tt}{half}")
                    end(mm(b[:, :], hid2[:, tt * P:tt * P + P], fw3[:, half * HYW:half * HYW + HYW], True, True),
                        f"f3_{tt}{half}")
            ada(1, 1)
            pe.wait_ge(S("filter abs"), 4)
            for half in range(2):
                b = begin(f"f4_{half}")
                for tt in range(TT):
                    ins = mm(b[:, :], ones[:, :], absf[:, tt, half, :], tt == 0, tt == TT - 1)
                end(ins, f"f4_{half}")
            pe.wait_ge(S("filter pair ready"), 1)
            for n in range(4):
                ri, kt = n // 2, n % 2
                b = begin(f"f5_{n}")
                for tt in range(TT):
                    ins = mm(b[:, :], basis[:, ri, tt, kt * P:kt * P + P], absf[:, tt, ri, :], tt == 0, tt == TT - 1)
                end(ins, f"f5_{n}")

            pe.wait_ge(S("h1 ready"), DK)
            keys = [("win", j) for j in range(6)]
            ws = [slab(k, 8, c1 - c0) for k, (c0, c1) in zip(keys, WIN_CUTS)]

            def arrived(key):
                wait_slab(pe, slab_no[key])

            arrived(keys[0])
            proj("cvg", ws[0], CONV_W, H, 2)
            proj("cvv", ws[0], 0, H, 2, free=keys[0])
            arrived(keys[1])
            proj("lrx01", ws[1], 0, H, 2)
            proj("lrx2", ws[1], 2 * P, H, 1, free=keys[1])
            arrived(keys[2])
            proj("lry01", ws[2], 0, H, 2)
            proj("lry2", ws[2], 2 * P, H, 1, free=keys[2])
            arrived(keys[3])
            proj("q01", ws[3], 0, H, 2, m=PAIR)
            proj("k01", ws[3], GH * GDK, H, 2, m=PAIR, free=keys[3])
            arrived(keys[4])
            for tt in range(TT):
                by_token(f"v{tt}", ws[4], 0, GH * GDV, H, tt)
            proj("glr", ws[4], GH * GDV, H, 1, m=16, free=keys[4])
            pe.wait_ge(S("mixer pack loaded"), 48)
            wait_taken(pe, "glr")
            b = begin("lgp")
            for pr in range(2):
                ins = mm(b[0:PAIR, pr * T:pr * T + T], glaw[:, pr, :], glr, True, True)
            end(ins, "lgp")
            arrived(keys[5])
            proj("og01", ws[5], 0, H, 2, m=GDV)
            proj("og23", ws[5], 2 * GDV, H, 2, m=GDV, free=keys[5])
            ada(1, 2)
            pe.wait_ge(S("lru conv ready"), 1)
            for t in range(LT):
                b = begin(f"lru{t}")
                for g in range(2):
                    ins = mm(b[:, g * T:g * T + T], lruw[:, g, t, :], xc[:, t, :], True, True)
                end(ins, f"lru{t}")
            ada(1, 3)
            pe.wait_ge(S("gla keys ready"), 1)
            b = begin("k2t")
            for tt in range(TT):
                for pr in range(2):
                    o = (2 * tt + pr) * PAIR
                    ins = nc.tensor.transpose(b[:, o:o + PAIR], diff[:, pr, tt * P:tt * P + P],
                                              ident[0:PAIR, 0:PAIR])
            end(ins, "k2t")
            pe.wait_ge(S("gla queries ready"), 1)
            for h in range(GH):
                if h % 2 == 0:
                    b = begin(f"sc{h}{h + 1}")
                for tt in range(TT):
                    o = (2 * (h % 2) + tt) * P
                    s = slice(tt * P, tt * P + P)
                    ins = mm(b[:, o:o + P], kin[:, h // 2, s], qz[:, h, s], True, True)
                if h % 2:
                    end(ins, f"sc{h - 1}{h}")
            wait_taken(pe, "k2t")
            wait_taken(pe, "v1")
            for c in range(3):
                b = begin(f"kv{c}")
                for pr in range(2):
                    ins = mm(b[0:PAIR, pr * 192:pr * 192 + 192], k2z[:, c // 2, c % 2, pr, :],
                             vtok[:, c // 2, pr * 192:pr * 192 + 192], True, True)
                end(ins, f"kv{c}")
            wait_taken(pe, "sc23")
            wait_taken(pe, "kv2")
            for h in range(GH):
                if h % 2 == 0:
                    b = begin(f"o{h}{h + 1}")
                for tt in range(TT):
                    o = (h % 2) * T + tt * P
                    mm(b[0:GDV, o:o + P], vtok[:, tt, h * GDV:h * GDV + GDV], sm[:, h, tt, :], True, False)
                    for c in (2 * tt, 2 * tt + 1):
                        if c:
                            e = (h % 2) * GDV
                            ins = mm(b[0:GDV, (h % 2) * T + c * GCH:(h % 2) * T + c * GCH + GCH],
                                     states[:, c - 1, h // 2, e:e + GDV], qz[:, h, c * GCH:c * GCH + GCH],
                                     False, c % 2 == 1)
                if h % 2:
                    end(ins, f"o{h - 1}{h}")
            for h in range(GH):
                if h % 2 == 0:
                    pe.wait_ge(S("gla squared"), h // 2 + 1)
                    b = begin(f"os{h}{h + 1}")
                ins = mm(b[0:GDV, (h % 2) * T:(h % 2) * T + T], ones[0:GDV, 0:GDV], W[0:GDV, 4 + h, :], True, True)
                if h % 2:
                    end(ins, f"os{h - 1}{h}")
            ada(1, 4)
            ada(1, 5)
            ada(2, 0)
            ada(2, 1)
            ss("mu", [u2[:, t, :] for t in range(CT)], "conv ready", 0, CT)
            ss("var", [W[:, 2 + t, :] for t in range(CT)], "conv squared", 0, CT)

            pe.wait_ge(S("mix u ready"), 2)
            pe.wait_ge(S("mix r ready"), 1)
            pe.wait_ge(S("mix o ready"), GH)
            mix = ([u2[:, t, :] for t in range(CT)] + [gy[:, t, :] for t in range(LT)]
                   + [sog[0:GDV, h, :] for h in range(GH)])
            for k in range(8):
                j = min(k // 3, 2)
                key = ("wout", j)
                c0, c1 = WOUT_CUTS[j]
                w = c1 - c0
                if k % 3 == 0:
                    arrived(key)
                if k % 2 == 0:
                    b = begin(f"wo{k}{k + 1}")
                for n, src in enumerate(mix):
                    rows = src.shape[0]
                    o = n * w + k * P - c0
                    ins = mm(b[:, (k % 2) * T:(k % 2) * T + T],
                             ring[0:rows, slab_no[key] % SLOTS, o:o + P], src, n == 0, n == len(mix) - 1)
                if k in (2, 7):
                    if k == 7:
                        free_and_end(ins, key, "wo67")
                    else:
                        ins.then_inc(freed[slab_no[key] % SLOTS], 1)
                elif k == 5:
                    free_and_end(ins, key, "wo45")
                elif k % 2:
                    end(ins, f"wo{k - 1}{k}")
            norm("n2")
            ada(2, 2)
            norm("nc")
            ada(2, 3)

            def router(m, n):
                w = 4 + 4 * n
                base = 0 if m == 0 else DK * 20
                v = wr[:, base:base + DK * w].rearrange("p (k w) -> p k w", k=DK)
                pe.wait_ge(S(f"h{2 * m + 2} ready"), DK)
                b = begin(f"rt{m + 1}")
                for tt in range(TT):
                    for k in range(DK):
                        ins = mm(b[:, tt * w:tt * w + w], H[:, k, tt * P:tt * P + P], v[:, k, :], k == 0, k == DK - 1)
                end(ins, f"rt{m + 1}")

            def experts_pe(m, n0, count):
                for b in range(BANKS):
                    begin(f"moe{m}_{b}")
                pe.wait_ge(S("zeros set"), m)
                for b in range(4):
                    nc.tensor.matmul(psum[b][:, :], ident[:, :], zeros, start=True, stop=False, skip_group_check=True)
                with pe.Fori(0, count // 2) as i:
                    for e in range(2):
                        pe.wait_ge(S(f"moe{m} diagonal ready"), i * 2 + e + 1)
                        for t in range(TT):
                            ins = mm(psum[6][:, e * T + t * P:e * T + t * P + P], ones[:, :], diag[:, e, t, :],
                                     True, True)
                        ins.then_inc(S(f"moe{m} weights spread"), 1)
                        w = []
                        for j in range(3):
                            n = n0 + 3 * e + j
                            w.append(ring[:, n % SLOTS, :].rearrange("p (k w) -> p k w", k=8 if j < 2 else 4))
                        for j in range(2):
                            n = n0 + 3 * e + j
                            pe.wait_ge(landed[n % SLOTS], i * 32 + 32 * (n // SLOTS + 1))
                        for f in range(4):
                            j = 4 * e + f
                            pe.wait_ge(S(f"moe{m} hidden"), i * 8 + j + 1)
                            for half in range(2):
                                for k in range(DK):
                                    ins = mm(psum[4 + j % 2][:, half * T:half * T + T],
                                             w[half][:, k, f * P:f * P + P], H[:, k, :], k == 0, k == DK - 1)
                                if f == 3 and half == 0:
                                    ins.then_inc(freed[(n0 + 3 * e) % SLOTS], 1)
                            ins.then_inc(S(f"moe{m} product"), 1)
                        pe.wait_ge(S(f"moe{m} product"), i * 8 + 4 * e + 4)
                        pe.sem_inc(freed[(n0 + 3 * e + 1) % SLOTS], 1)
                        n = n0 + 3 * e + 2
                        pe.wait_ge(landed[n % SLOTS], i * 32 + 32 * (n // SLOTS + 1))
                        for f in range(4):
                            pe.wait_ge(S(f"moe{m} hidden"), i * 8 + 4 * e + f + 3)
                            for k in range(DK):
                                ins = nc.tensor.matmul(psum[k // 2][:, (k % 2) * T:(k % 2) * T + T],
                                                       w[2][:, f, k * P:k * P + P], hid[:, e, f, :], start=False,
                                                       stop=False, skip_group_check=True)
                        ins.then_inc(freed[n % SLOTS], 1)
                pe.wait_ge(freed[(n0 + 5) % SLOTS], (n0 + 3 * count - 1) // SLOTS + 1)
                for b in range(BANKS):
                    pe.sem_inc(filled[b], 1)

            router(0, 4)
            ada(2, 4)
            ada(2, 5)
            experts_pe(1, N1, E1)
            norm("nf")
            norm("m1")

            pe.wait_ge(S("h3 ready"), DK)
            pe.wait_ge(S("ctx ready"), DK)
            pe.wait_ge(S("late pack loaded"), 32)
            key = ("win2", 0)
            w = slab(key, 8, 512)
            arrived(key)
            proj("kT01", w, 0, H, 2)
            proj("kT23", w, 2 * P, H, 2)
            by_token("kc0", w, 0, 512, HC, 0, bias=brow[:, 0:512])
            by_token("kc1", w, 0, 512, HC, 1, free=key, bias=brow[:, 0:512])
            for half in range(2):
                key = ("win2", 1 + half)
                w = slab(key, 8, 512)
                arrived(key)
                bias = brow[:, 512 + 512 * half:1024 + 512 * half]
                for what, src in (("vx", H), ("vc", HC)):
                    for tt in range(TT):
                        last = what == "vc" and tt == 1
                        by_token(f"{what}{half}{tt}", w, 0, 512, src, tt, free=key if last else None, bias=bias)
            pe.wait_ge(S("ctx keys ready"), 4)
            wait_taken(pe, "vc11")
            for h in range(RH):
                b = begin(f"st{h}")
                for way in range(2):
                    for tt in range(TT):
                        ins = mm(b[:, way * RDV:way * RDV + RDV], kdec[:, h, way, tt, :],
                                 VC[:, tt, h * RDV:h * RDV + RDV], tt == 0, tt == TT - 1)
                end(ins, f"st{h}")

            def swap(name, raw, h):
                b = begin(name)
                for t in range(2):
                    ins = mm(b[:, t * T:t * T + T], perm, raw[:, h + t, :], True, True)
                end(ins, name)

            wait_taken(pe, "kT23")
            swap("rk01", kraw, 0)
            swap("rk23", kraw, 2)
            key = ("win2", 3)
            w = slab(key, 8, 512)
            arrived(key)
            proj("q2_01", w, 0, H, 2)
            proj("q2_23", w, 2 * P, H, 2, free=key)
            wait_taken(pe, "q2_23")
            swap("rq01", qraw, 0)
            swap("rq23", qraw, 2)
            for j in range(2):
                key = ("win2", 4 + j)
                w = slab(key, 8, 512)
                arrived(key)
                proj(f"g{4 * j}{4 * j + 1}", w, 0, H, 2)
                proj(f"g{4 * j + 2}{4 * j + 3}", w, 2 * P, H, 2, free=key)
            pe.wait_ge(S("rotated"), 4)
            for h in range(RH):
                b = begin(f"s{h}")
                for jt in range(TT):
                    ins = mm(b[:, jt * T:jt * T + T], kr[:, h, jt * P:jt * P + P], qr[:, h, :], True, True)
                end(ins, f"s{h}")

            def attend(h):
                wait_taken(pe, f"s{h}")
                b = begin(f"o{h}")
                for vt in range(2):
                    o = b[:, vt * T:vt * T + T]
                    e = vt * P
                    for jt in range(TT):
                        mm(o, V[:, jt, h * RDV + e:h * RDV + e + P], Pm[h % 2][:, jt, :], jt == 0, False)
                    mm(o, S0[:, h, 0, e:e + P], qf[:, h % 2, :], False, False)
                    ins = mm(o, S0[:, h, 1, e:e + P], qb[:, h % 2, :], False, True)
                end(ins, f"o{h}")

            def readout_sum(h):
                ss(f"rs{h}", [osq[:, t, :] for t in range(2)], "readout squared", h, 2)

            wait_taken(pe, "st3")
            attend(0)
            attend(1)
            readout_sum(0)
            attend(2)
            readout_sum(1)
            attend(3)
            readout_sum(2)
            readout_sum(3)
            for j in range(3):
                key = ("win2", 6 + j)
                w = slab(key, 8, 512)
                arrived(key)
                proj(f"hy{4 * j}", w, 0, H, 2)
                proj(f"hy{4 * j + 2}", w, 2 * P, H, 2, free=key)
            for g, j0 in (("gr", 9), ("gh", 11)):
                for j in range(2):
                    key = ("win2", j0 + j)
                    w = slab(key, 8, 512)
                    arrived(key)
                    proj(f"{g}{4 * j}", w, 0, H, 2)
                    proj(f"{g}{4 * j + 2}", w, 2 * P, H, 2, free=key)
            pe.wait_ge(S("z ready"), HYT)
            for tt in range(TT):
                b = begin(f"zt{tt}")
                for c in range(HYT):
                    ins = nc.tensor.transpose(b[:, c * P:c * P + P], zT[:, c, tt * P:tt * P + P], ident[:, :])
                end(ins, f"zt{tt}")
            for tt in range(TT):
                wait_taken(pe, f"zt{tt}")
            for kt in range(2):
                for ri, n in enumerate((f"zr{kt}", f"zi{kt}")):
                    b = begin(n)
                    for tt in range(TT):
                        ins = mm(b[:, :], mcs[:, ri, tt, kt * P:kt * P + P], ztok[:, tt, :], tt == 0, tt == TT - 1)
                    end(ins, n)
            pe.wait_ge(S("spectrum ready"), 2)
            for c in range(HYT):
                if c % 2 == 0:
                    b = begin(f"yt{c}")
                for n in range(4):
                    ri, kt = n // 2, n % 2
                    ins = mm(b[:, (c % 2) * T:(c % 2) * T + T], Y[:, ri, kt, c * P:c * P + P], mcs[:, ri, kt, :],
                             n == 0, n == 3)
                if c % 2:
                    end(ins, f"yt{c - 1}")
            pe.wait_ge(S("readout ready"), RH)
            for j in range(2):
                key = ("ret_o", j)
                w = slab(key, 8, 512)
                arrived(key)
                proj(f"ro{4 * j}", w, 0, sg, 2)
                proj(f"ro{4 * j + 2}", w, 2 * P, sg, 2, free=key)
            pe.wait_ge(S("hyena ready"), 2)
            key = ("hy_o", 0)
            w = slab(key, 4, 1024)
            arrived(key)
            for j in range(4):
                proj(f"ho{2 * j}", w, 2 * P * j, hyo, 2, nk=HYT, free=key if j == 3 else None)
            pe.wait_ge(S("merged"), 4)
            for j in range(2):
                key = ("wout2", j)
                w = slab(key, 8, 512)
                arrived(key)
                proj(f"w2_{4 * j}", w, 0, H, 2)
                proj(f"w2_{4 * j + 2}", w, 2 * P, H, 2, free=key)
            norm("m2")
            router(1, 8)
            experts_pe(2, N3, E2)
            norm("mf")


_WHOLE = ["w_ada", "w_in", "w_out", "w_gate", "w_up", "w_down", "ada_w_2", "w_in_2", "ret_w_o_2", "hy_w_o_2",
          "w_out_2", "expert_w1_2", "expert_w3_2", "expert_w2_2"]


def packs(i):
    f = np.float32

    def cols_of(v, n):
        return np.ascontiguousarray(np.asarray(v).reshape(n, P).T)

    def padded(v, rows=P):
        v = np.asarray(v)
        out = np.zeros((rows,) + v.shape[1:], f)
        out[:v.shape[0]] = v
        return out

    def taps(w, tiles):
        k = w.shape[0]
        return w.reshape(k, tiles, P).transpose(2, 1, 0).reshape(P, tiles * k)

    def spread(v):
        return np.broadcast_to(np.asarray(v).reshape(1, -1), (P, np.asarray(v).size))

    p = np.arange(P)
    t = np.arange(T)
    c = np.zeros((P, NCOL), f)

    def put(name, v):
        c[:, AT[name]:AT[name] + v.shape[1]] = v

    put("c", cols_of(i["c"], 8))
    both = np.stack([i["c_2"].reshape(8, P), i["c_ctx_2"].reshape(8, P)], 1)
    put("c2", both.reshape(16, P).T)
    put("b_ada", cols_of(i["b_ada"], 48))
    put("b_ada2", cols_of(i["ada_b_2"], 48))
    put("g_mix", cols_of(i["g_mix"], 8))
    put("conv_w", taps(i["conv_dw_w"][0], CT))
    put("conv_b", cols_of(i["conv_dw_b"], 2))
    put("ln_g", cols_of(i["conv_ln_g"], 2))
    put("ln_b", cols_of(i["conv_ln_b"], 2))
    put("lru_w", taps(i["lru_conv_w"][0], LT))
    for name, key in (("lru_b", "lru_conv_b"), ("lru_ba", "lru_b_a"), ("lru_bi", "lru_b_i"), ("lam", "lru_lam")):
        put(name, cols_of(i[key], 3))
    put("gla_b", padded(i["gla_b_gate"][0].reshape(2, PAIR).T))
    put("gla_g", padded(i["gla_norm_g"][0].reshape(GH, GDV).T))
    for name, key in (("g_ffn", "g_ffn"), ("g_final", "g_final"), ("g1", "norm1_g_2"), ("g2", "norm2_g_2"),
                      ("g_out", "final_norm_g_2")):
        put(name, cols_of(i[key], 8))
    put("b_in", cols_of(i["b_in_2"], 52))
    put("decay", spread(i["ret_decay_logit_2"][0]))
    put("hy_w", taps(i["hy_conv_w_2"][0], 12))
    put("hy_b", cols_of(i["hy_conv_b_2"], 12))
    for name, key in (("f_b1", "hy_ffn_b1_2"), ("f_freq", "hy_ffn_freq_2"), ("f_b2", "hy_ffn_b2_2")):
        put(name, padded(i[key].reshape(64, 1)))
    put("skip", cols_of(i["hy_skip_2"], 4))
    put("br1", spread(np.concatenate([i["b_route_group"].reshape(-1), i["b_route_expert"].reshape(-1)])))
    put("br2", spread(np.concatenate([i["router_group_b_2"].reshape(-1), i["router_expert_b_2"].reshape(-1)])))
    times = (np.arange(T, dtype=f) / T).astype(f)
    put("neg_t", -times.reshape(TT, P).T)
    pos = (p[:, None] + P * np.arange(TT)[None, :]).astype(f)
    put("pos", pos)
    put("rpos", T - 1 - pos)
    put("pos1", pos + 1)
    put("tie4", spread(np.arange(4, 0, -1).astype(f)))
    put("tie8", spread(np.arange(8, 0, -1).astype(f)))
    rows = np.arange(P)[:, None]
    put("head", (((rows // GDK == 0) | (rows // GDK == 1)) * (rows // GDK == np.arange(2)[None, :])
                 * float(GDK) ** -0.5).astype(f))
    put("eps", np.full((P, 1), EPS, f))

    def by_feature(x):
        return np.ascontiguousarray(x.reshape(T, DK, P).transpose(2, 1, 0))

    bands = np.linspace(1e-4, 15, 16, dtype=f)
    phase = (f(2.0 * np.pi) * times[:, None] * bands[None, :]).astype(f)
    feats = np.concatenate([times[:, None], np.cos(phase), -np.sin(phase)], -1).astype(f)
    slow, fast = abs(np.log(1e-2)) / 1.5, abs(np.log(1e-2)) / 0.3
    deltas = np.linspace(slow, fast, HYW, dtype=f)

    def tiles(m):
        return m.reshape(TT, P, T).transpose(1, 0, 2)

    w_tau = np.pi * np.outer(t, t + 0.5) / T
    w_mid = np.pi * np.outer(t + 0.5, t + 0.5) / T
    basis = np.stack([tiles(np.cos(w_tau)), tiles(-np.sin(w_tau))], 1).astype(f)
    mcs = np.stack([tiles(np.cos(w_mid)), tiles(-np.sin(w_mid))], 1).astype(f)
    fpack = np.zeros((P, 12 * T), f)
    fpack[:33, 0:T] = feats.T
    fpack[:33, T:T + 64] = i["hy_ffn_w1_2"][0]
    fpack[:64, T + 64:T + 128] = i["hy_ffn_w2_2"][0]
    fpack[:, 2 * T:4 * T] = deltas[None, :]
    fpack[:, 4 * T:8 * T] = basis.reshape(P, -1)
    fpack[:64, 8 * T:12 * T] = i["hy_ffn_w3_2"][0]

    mpack = np.zeros((P, 1408), f)
    lw = mpack[:, 0:768].reshape(P, 2, LT, P)
    for g, key in enumerate(("lru_w_a", "lru_w_i")):
        for b in range(6):
            s = slice(64 * (b % 2), 64 * (b % 2) + 64)
            lw[s, g, b // 2, s] = i[key][0, b]
    j, q = p[:, None], p[None, :]
    mpack[:, 768:896] = (j <= q) & (j // GCH == q // GCH)
    mpack[:, 896:1152] = (t % GCH != 0)[None, :]
    mpack[:16, 1152:1344] = i["gla_w_gate"][0]

    inv = (f(10000.0) ** (-np.arange(32, dtype=f) / f(32))).astype(f)
    ang = np.zeros((P, T), f)
    for blk in range(4):
        where = (t // 64 if blk < 2 else t % 64).astype(f)
        ang[32 * blk:32 * blk + 32] = (inv[:, None] * where[None, :]).astype(f)
    sign = np.where((p // 32) % 2 == 0, -1.0, 1.0)[:, None]
    perm = np.zeros((P, P), f)
    perm[p ^ 32, p] = 1.0
    lpack = np.concatenate([mcs.reshape(P, -1), np.cos(ang), sign * np.sin(ang), perm,
                            np.broadcast_to(t[None, :] + 1, (P, T))], 1).astype(f)

    def router(g, e):
        w = np.concatenate([g, e], 1)
        return w.reshape(DK, P, -1).transpose(1, 0, 2).reshape(P, -1)

    e1 = i["w_route_expert"][0].transpose(1, 0, 2).reshape(D, 16)
    wr = np.concatenate([router(i["w_route_group"][0], e1),
                         router(i["router_group_w_2"][0], i["router_expert_w_2"][0])], 1)
    return {"cols": c, "xT": by_feature(i["x"][0]), "ctxT": by_feature(i["ctx_2"][0]), "fpack": fpack,
            "mpack": mpack, "lpack": lpack, "wr": np.ascontiguousarray(wr), "ident": np.eye(P, dtype=f),
            "brow": np.ascontiguousarray(i["b_in_2"][:, 512:2048])}


def kernel(**inputs):
    import concourse.bacc as bacc
    from concourse.bass_utils import run_bass_kernel_spmd

    i = {k: np.asarray(v) for k, v in inputs.items()}
    nc = bacc.Bacc("TRN2", target_bir_lowering=False, num_devices=1)
    arrays = packs(i)
    for name in _WHOLE:
        v = i[name]
        v = v.reshape((-1,) + v.shape[-2:])
        arrays[name] = np.ascontiguousarray(v[0] if v.shape[0] == 1 else v)
    aps = {name: nc.dram_tensor(f"in_{name}", v.shape, F32, kind="ExternalInput").ap() for name, v in arrays.items()}
    out = nc.dram_tensor("out_y", [P, DK, T], F32, kind="ExternalOutput").ap()
    build(nc, aps, out)
    r = run_bass_kernel_spmd(nc, [{f"in_{name}": v for name, v in arrays.items()}], core_ids=[0])
    y = r.results[0]["out_y"]
    return np.ascontiguousarray(y.transpose(2, 1, 0)).reshape(1, T, D)
```

```python
from contextlib import ExitStack

import concourse.bass as bass
import numpy as np
from concourse import mybir

F32 = mybir.dt.float32
ALU = mybir.AluOpType
ACT = mybir.ActivationFunctionType
AX = mybir.AxisListType

P = 128
T = 256
TT = T // P
D = 1024
DK = D // P
EPS = 1e-6

CONV_W, CONV_K = 256, 31
LRU_W, LRU_K = 384, 4
GH, GDK, GDV, GCH = 4, 48, 96, 64
PAIR = 2 * GDK
CT, LT = CONV_W // P, LRU_W // P

RH, RDK, RDV = 4, 128, 256
HYW = 512
HYT = HYW // P

SLOTS = 6
SLAB = 4096
BANKS = 8
CAP = 64

WIN_CUTS = [(0, 512), (512, 896), (896, 1280), (1280, 1664), (1664, 2064), (2064, 2448)]
WOUT_CUTS = [(0, 384), (384, 768), (768, 1024)]
WIN2_ORDER = [512, 1024, 1536, 0, 2048, 2560, 3072, 3584, 4096, 4608, 5120, 5632, 6144]

COLS = [("c", 8), ("c2", 16), ("b_ada", 48), ("b_ada2", 48), ("g_mix", 8), ("conv_w", 62), ("conv_b", 2), ("ln_g", 2),
        ("ln_b", 2), ("lru_w", 12), ("lru_b", 3), ("lru_ba", 3), ("lru_bi", 3), ("lam", 3), ("gla_b", 2), ("gla_g", 4),
        ("g_ffn", 8), ("g_final", 8), ("g1", 8), ("g2", 8), ("b_in", 52), ("decay", 8), ("hy_w", 36), ("hy_b", 12),
        ("f_b1", 1), ("f_freq", 1), ("f_b2", 1), ("skip", 4), ("g_out", 8), ("br1", 20), ("br2", 36),
        ("eps", 1), ("head", 2), ("neg_t", 2), ("pos", 2), ("rpos", 2), ("pos1", 2), ("tie4", 4), ("tie8", 8)]
AT, n_ = {}, 0
for name_, w_ in COLS:
    AT[name_] = n_
    n_ += w_
NCOL = n_


def stream_plan():
    ada1 = [("ada1", j) for j in range(12)]
    ada2 = [("ada2", j) for j in range(12)]
    first = (ada1[0:4] + [("win", j) for j in range(6)] + ada1[4:12] + ada2[0:4] + [("wout", j) for j in range(3)]
             + ada2[4:12])
    second = ([("win2", j) for j in range(13)] + [("ret_o", 0), ("ret_o", 1), ("hy_o", 0), ("wout2", 0), ("wout2", 1)])
    return first, second


def bank_plan():
    names = ["n1_ss", "f1", "a1_0", "f2", "f3_00", "f3_01", "f3_10", "f3_11", "a1_1", "f4_0", "f4_1",
             "f5_0", "f5_1", "f5_2", "f5_3",
             "cvg", "cvv", "lrx01", "lrx2", "lry01", "lry2", "q01", "k01", "v0", "v1", "glr", "lgp", "og01", "og23",
             "a1_2", "lru0", "lru1", "lru2", "a1_3", "k2t", "sc01", "sc23", "kv0", "kv1", "kv2", "o01", "o23",
             "os01", "os23", "a1_4", "a1_5", "a2_0", "a2_1", "mu", "var",
             "wo01", "wo23", "wo45", "wo67", "n2_ss", "a2_2", "nc_ss", "a2_3", "rt1", "ht1_0", "ht1_1", "ht1_2",
             "ht1_3", "a2_4", "a2_5", "rk1", "fl1"]
    names += [f"moe1_{b}" for b in range(BANKS)]
    names += ["nf_ss", "m1_ss"]
    names += ["kT01", "kT23", "kc0", "kc1", "vx00", "vx01", "vc00", "vc01", "vx10", "vx11", "vc10", "vc11",
              "st0", "st1", "st2", "st3", "rk01", "rk23", "q2_01", "q2_23", "rq01", "rq23",
              "g01", "g23", "g45", "g67", "s0", "s1", "s2", "s3", "o0", "o1", "rs0", "o2", "rs1", "o3", "rs2", "rs3"]
    names += [f"hy{2 * j}" for j in range(6)] + [f"gr{2 * j}" for j in range(4)] + [f"gh{2 * j}" for j in range(4)]
    names += ["zt0", "zt1", "zr0", "zi0", "zr1", "zi1", "yt0", "yt2"]
    names += [f"ro{2 * j}" for j in range(4)] + [f"ho{2 * j}" for j in range(4)] + [f"w2_{2 * j}" for j in range(4)]
    names += ["m2_ss", "rt2", "ht2_0", "ht2_1", "ht2_2", "ht2_3", "rk2", "fl2"] + [f"moe2_{b}" for b in range(BANKS)] + ["mf_ss"]
    place = {}
    used = [0] * BANKS
    at = 0
    for n in names:
        b = int(n[-1]) if n.startswith("moe") else at % BANKS
        at += not n.startswith("moe")
        place[n] = (b, used[b])
        used[b] += 1
    return place


def build(nc, a, out):
    first, second = stream_plan()
    place = bank_plan()
    N1 = len(first)
    E1, E2 = 16, 32
    N2 = N1 + 3 * E1
    N3 = N2 + len(second)
    slab_no = {key: n for n, key in enumerate(first)}
    slab_no.update({key: N2 + n for n, key in enumerate(second)})

    with ExitStack() as ctx:
        def sb(name, shape):
            return ctx.enter_context(nc.sbuf_tensor(name, shape, F32))

        sems = {}

        def S(name):
            if name not in sems:
                sems[name] = ctx.enter_context(nc.semaphore(name.replace(" ", "_")))
            return sems[name]

        psum = [ctx.enter_context(nc.psum_tensor(f"bank{b}", [P, 512], F32)) for b in range(BANKS)]
        filled = [S(f"filled{b}") for b in range(BANKS)]
        drained = [S(f"drained{b}") for b in range(BANKS)]
        landed = [S(f"landed{s}") for s in range(SLOTS)]
        freed = [S(f"freed{s}") for s in range(SLOTS)]

        ring = sb("ring", [P, SLOTS, SLAB])
        cols = sb("cols_sb", [P, NCOL])
        X = sb("X", [P, DK, T])
        H = sb("H", [P, DK, T])
        W = sb("W", [P, DK, T])
        HF = sb("HF", [P, 2, 2, HYW])
        marks = sb("marks", [P, 2 * P + CAP])
        ident = marks[:, 0:P]
        before = marks[:, P:2 * P]
        places = marks[:, 2 * P:2 * P + CAP]
        ones = sb("ones", [P, P])
        wr = sb("wr", [P, DK * 20 + DK * 36])
        root = sb("root", [P, T])
        rstd = sb("rstd", [P, T])
        mod1 = sb("mod1", [P, 48])
        mod2 = sb("mod2", [P, 48, 2])
        gs = sb("gs", [P, 5, DK])
        cact = sb("cact", [P, 24])
        lgs = sb("lgs", [P, 5, 8])
        sml = sb("sml", [P, 24])
        lru_scale = sb("lru_scale", [P, 2, LT])
        gdec = sb("gdec", [PAIR, 2, 4])
        ctxdec = sb("ctxdec", [P, 2, RH, TT])
        backb = sb("backb", [P, RH])
        route = sb("route", [P, 304])
        comb = sb("comb", [P, TT, 32])
        rank = sb("rank", [P, TT, 32])
        over = sb("over", [P, TT, 32])
        n_over = sb("n_over", [P, 2])
        flag = ctx.enter_context(nc.sbuf_tensor("flag", [P, 1], mybir.dt.int32))
        pool = sb("pool", [P, 69 * T])

        def view(tile, *shape, rows=P):
            n = int(np.prod(shape))
            v = pool[0:rows, int(tile * T):int(tile * T) + n]
            if len(shape) == 1:
                return v
            names = "abcd"[:len(shape)]
            return v.rearrange(f"p ({' '.join(names)}) -> p {' '.join(names)}",
                               **{k: s for k, s in zip(names[1:], shape[1:])})

        def col(name, i=0, n=1, rows=slice(0, P)):
            return cols[rows, AT[name] + i:AT[name] + i + n]

        upad = view(0, CT, CONV_K - 1 + T)
        u2 = view(3, CT, T)
        lxpad = view(5, LT, LRU_K - 1 + T)
        xc = view(9, LT, T)
        rg = view(12, LT, T)
        ig = view(15, LT, T)
        ag = view(18, LT, T)
        gy = view(21, LT, T)
        cvsg = view(12, CT, T)
        qT = view(24, 2, T, rows=PAIR)
        kT1 = view(26, 2, T, rows=PAIR)
        vtok = view(28, TT, GH * GDV)
        glr = view(31, T, rows=16)
        lgx = view(32, 2, T, rows=PAIR)
        bcum = view(34, 2, T, rows=PAIR)
        diff = view(36, 2, T, rows=PAIR)
        eb = view(38, 2, T, rows=PAIR)
        lruw = view(40, 2, LT, P)
        gmask = view(43, P)
        segm = view(43.5, T, rows=PAIR)
        glaw = view(44.5, 2, PAIR, rows=16)
        qz = view(46, GH, T, rows=PAIR)
        kin = view(50, 2, T, rows=PAIR)
        k2z = view(52, TT, 2, 2, PAIR)
        sm = view(56, GH, TT, P)
        states = view(60, 3, 2, 2 * GDV, rows=PAIR)
        sog = view(65, GH, T)
        feats = view(12, T, rows=33)
        fw1 = view(13, 64, rows=33)
        fw2 = view(13.25, 64, rows=64)
        deltas = view(14, HYW)
        basis = view(16, 2, TT, T)
        fw3 = view(20, 1024, rows=64)
        arg = view(24, T, rows=64)
        rnd = view(25, T, rows=64)
        hid1 = view(26, T, rows=64)
        hid2 = view(27, T, rows=64)
        filt = view(46, TT, 2, HYW)
        absf = view(54, TT, 2, HYW)
        decay = view(62, TT, HYW)
        htok = view(8, TT, D)
        hexp = view(16, 2, DK, CAP)
        pick = view(20, 2, TT, CAP)
        pickw = view(21, TT, 2 * CAP)
        put = view(22, T)
        sact = view(23, 4, CAP)
        yexp = view(30, D)
        hid = view(34, 4, CAP)
        ogate, oup, odown = view(35, DK, P), view(39, DK, P), view(45, D)
        ohid, oact, oweigh = view(49, T), view(50, T), view(51, T)
        odiag = view(52, TT, P)
        HC = view(0, DK, T)
        sigR = view(0, DK, T)
        VC = view(8, TT, 1024)
        sigH = view(8, DK, T)
        Ef, Eb = view(8, T), view(9, T)
        qf, qb = view(10, 2, T), view(12, 2, T)
        S0 = view(16, RH, 2, RDV)
        x0 = view(16, HYT, T)
        zT = view(20, HYT, T)
        brow = view(24, 1536, rows=1)
        kdec = view(24, RH, 2, TT, P)
        sg = view(24, DK, T)
        hypad = view(32, 12, T + 2)
        kr = view(45, RH, T)
        qr = view(49, RH, T)
        hyo = view(45, HYT, T)
        cv1, cv2 = view(49, T), view(50, T)
        V = view(53, TT, 1024)
        ztok = view(53, TT, HYW)
        ztmp = view(57, TT, HYW)
        mcs = view(61, 2, TT, T)
        rope = view(65, 2, T)
        perm = view(67, P)
        irow = view(67.5, T)
        W4 = W[:, 0:4, :]
        kraw, qraw = W[:, 0:4, :], W[:, 4:8, :]
        KC = W[:, 4:8, :].rearrange("p (t a) b -> p t (a b)", t=TT)
        Dm = W[:, 0:2, :]
        Pm = [W[:, 2:4, :], W[:, 4:6, :]]
        osq = W[:, 6:8, :]
        Y = W[:, :, :].rearrange("p (r t a) b -> p r t (a b)", r=2, t=TT)

        zeros = view(59, 512)
        dtmp, rtmp = view(0, 2, T), view(2, 2, T)
        gla_root = view(56, GH, T, rows=GDV)
        X1 = ["wo01", "wo23", "wo45", "wo67"]
        X4 = ["w2_0", "w2_2", "w2_4", "w2_6"]
        NORM = {key: n for n, key in enumerate(["n1", "n2", "nc", "nf", "m1", "m2", "mf"])}
        rv = {"gexp": route[:, 80:88].rearrange("p (t g) -> p t g", t=TT), "pexp": route[:, 256:258]}

        def lru_neg(t):
            return lru_scale[:, 0, t:t + 1]

        def lru_pos(t):
            return lru_scale[:, 1, t:t + 1]

        def bank(name):
            return psum[place[name][0]]

        def wait_product(eng, name):
            b, use = place[name]
            eng.wait_ge(filled[b], use + 1)

        def gone(name):
            return drained[place[name][0]]

        def wait_taken(eng, name):
            b, use = place[name]
            eng.wait_ge(drained[b], use + 1)

        def wait_slab(eng, n):
            eng.wait_ge(landed[n % SLOTS], 32 * (n // SLOTS + 1))

        def used_up(eng, i, j, n0):
            n = n0 + j
            eng.wait_ge(freed[n % SLOTS], i + n // SLOTS + 1)

        def slab(key, k, w, base=0):
            s = slab_no[key] % SLOTS
            return ring[:, s, base:base + k * w].rearrange("p (k w) -> p k w", k=k)

        def bc(ap, shape):
            return ap.broadcast_to(shape)

        block = ctx.enter_context(nc.Block())

        def experts(sp, m, w_gate, w_up, w_down, n0, count):
            by_expert = [w.rearrange("e (k p) f -> e p k f", p=P) for w in (w_gate, w_up, w_down)]
            with sp.Fori(0, count // 2) as i:
                for j in range(6):
                    n, w = n0 + j, by_expert[j % 3]
                    k = w.shape[2]
                    s = n % SLOTS
                    src = w[bass.ds(i * 2 + j // 3, 1)].rearrange("o p k f -> p (o k) f")
                    dst = ring[:, s, :].rearrange("p (k w) -> p k w", k=k)
                    sp.wait_ge(freed[s], i + n // SLOTS)
                    sp.dma_start(dst[:, 0:k // 2], src[:, 0:k // 2]).then_inc(landed[s], 16)
                    sp.dma_start(dst[:, k // 2:k], src[:, k // 2:k]).then_inc(landed[s], 16)
            sp.wait_ge(S(f"moe{m} flag ready"), 1)
            crowded = sp.value_load(flag[0:1, 0:1], min_val=0, max_val=TT * P * 2)
            with sp.If(crowded > 0):
                with sp.Fori(0, count) as e:
                    g, u, d = (w[bass.ds(e, 1)].rearrange("o p k f -> p (o k) f") for w in by_expert)
                    for f in range(4):
                        c = slice(f * P, f * P + P)
                        sp.wait_ge(S(f"over{m} used"), e * 4 + f + 1)
                        sp.dma_start(ogate, g[:, :, c]).then_inc(S(f"over{m} landed"), 16)
                        sp.dma_start(oup, u[:, :, c]).then_inc(S(f"over{m} landed"), 16)
                        sp.dma_start(odown, d[:, f, :]).then_inc(S(f"over{m} landed"), 16)

        @block.sync
        def _(sp):
            def load(n, halves):
                s = n % SLOTS
                if n >= SLOTS:
                    sp.wait_ge(freed[s], n // SLOTS)
                for dst, src in halves:
                    sp.dma_start(dst, src).then_inc(landed[s], 16)

            def columns(n, w, c0, c1):
                v = w.rearrange("(k p) f -> p k f", p=P)[:, :, c0:c1]
                d = ring[:, n % SLOTS, 0:8 * (c1 - c0)].rearrange("p (k w) -> p k w", k=8)
                load(n, [(d[:, 0:4], v[:, 0:4]), (d[:, 4:8], v[:, 4:8])])

            for key in first + second:
                n = slab_no[key]
                kind, j = key
                if n == N2:
                    experts(sp, 1, a["w_gate"], a["w_up"], a["w_down"], N1, E1)
                if kind == "ada1":
                    columns(n, a["w_ada"], 512 * j, 512 * j + 512)
                elif kind == "ada2":
                    columns(n, a["ada_w_2"], 512 * j, 512 * j + 512)
                elif kind == "win":
                    columns(n, a["w_in"], *WIN_CUTS[j])
                elif kind == "wout":
                    c0, c1 = WOUT_CUTS[j]
                    w = c1 - c0
                    top = a["w_out"][0:640, c0:c1].rearrange("(k p) f -> p k f", p=P)
                    low = a["w_out"][640:1024, c0:c1].rearrange("(k p) f -> p k f", p=GDV)
                    load(n, [(ring[:, n % SLOTS, 0:5 * w].rearrange("p (k w) -> p k w", k=5), top),
                             (ring[0:GDV, n % SLOTS, 5 * w:9 * w].rearrange("p (k w) -> p k w", k=4), low)])
                elif kind == "win2":
                    columns(n, a["w_in_2"], WIN2_ORDER[j], WIN2_ORDER[j] + 512)
                elif kind == "ret_o":
                    columns(n, a["ret_w_o_2"], 512 * j, 512 * j + 512)
                elif kind == "wout2":
                    columns(n, a["w_out_2"], 512 * j, 512 * j + 512)
                elif kind == "hy_o":
                    v = a["hy_w_o_2"].rearrange("(k p) f -> p k f", p=P)
                    d = ring[:, n % SLOTS, :].rearrange("p (k w) -> p k w", k=4)
                    load(n, [(d[:, 0:2], v[:, 0:2]), (d[:, 2:4], v[:, 2:4])])
            experts(sp, 2, a["expert_w1_2"], a["expert_w3_2"], a["expert_w2_2"], N3, E2)

        @block.gpsimd
        def _(pool_e):
            pool_e.memset(ones[:, :], 1.0).then_inc(S("ones set"), 1)
            pool_e.memset(upad[:, :, 0:CONV_K - 1], 0.0)
            pool_e.memset(lxpad[:, :, 0:LRU_K - 1], 0.0).then_inc(S("pads zero"), 1)
            for n in range(4):
                wait_taken(pool_e, f"f5_{n}")
            pool_e.memset(k2z[:, :, :, :, :], 0.0).then_inc(S("heads zero"), 1)
            wait_taken(pool_e, "m1_ss")
            pool_e.memset(hypad[:, :, 0:1], 0.0)
            pool_e.memset(hypad[:, :, T + 1:T + 2], 0.0).then_inc(S("hyena pads zero"), 1)

        def readout_act(act, h):
            wait_product(act, f"o{h}")
            nc.scalar.activation(osq, bank(f"o{h}")[:, :].rearrange("p (a b) -> p a b", a=2),
                                 ACT.Square).then_inc(S("readout squared"), 1)
            wait_product(act, f"rs{h}")
            if h:
                act.wait_ge(S("readout ready"), h)
            nc.scalar.activation(root[:, :], bank(f"rs{h}")[:, 0:T], ACT.Sqrt, scale=1.0 / RDV,
                                 bias=col("eps")).then_inc(gone(f"rs{h}"), 1)

        @block.scalar
        def _(act):
            steps = [0]

            def link(ins):
                steps[0] += 1
                ins.then_inc(S("scalar step"), 1)
                act.wait_ge(S("scalar step"), steps[0])

            def squares(key, src):
                for j in range(4):
                    nc.scalar.activation(W[:, 2 * j:2 * j + 2, :], src[:, 2 * j:2 * j + 2, :],
                                         ACT.Square).then_inc(S("squared"), 1)

            def norm_root(key):
                wait_product(act, key + "_ss")
                nc.scalar.activation(root[:, :], bank(key + "_ss")[:, 0:T], ACT.Sqrt, scale=1.0 / D,
                                     bias=col("eps")).then_inc(gone(key + "_ss"), 1)

            def modulate(key, dst, scales, shifts, ready):
                act.wait_ge(S("norm scaled"), NORM[key] + 1)
                for k in range(DK):
                    if shifts is None:
                        ins = nc.scalar.activation(dst[:, k, :], dst[:, k, :], ACT.Copy, scale=scales(k))
                    else:
                        ins = nc.scalar.activation(dst[:, k, :], dst[:, k, :], ACT.Identity, scale=scales(k),
                                                   bias=shifts(k))
                    ins.then_inc(S(ready), 1)

            act.dma_start(cols[:, :], a["cols"]).then_inc(S("cols loaded"), 16)
            act.dma_start(X[:, :, :], a["xT"]).then_inc(S("x loaded"), 16)
            act.dma_start(view(12, 12 * T), a["fpack"]).then_inc(S("filter pack loaded"), 16)
            act.dma_start(marks[:, :], a["marks"]).then_inc(S("mixer pack loaded"), 16)
            act.dma_start(view(40, 1408), a["mpack"]).then_inc(S("mixer pack loaded"), 16)
            act.dma_start(wr[:, :], a["wr"]).then_inc(S("mixer pack loaded"), 16)

            act.wait_ge(S("cols loaded"), 16)
            nc.scalar.activation(cact[:, :], col("c", 0, 24), ACT.Silu).then_inc(S("c ready"), 1)
            link(nc.scalar.activation(sml[:, 0:3], col("lam", 0, 3), ACT.Abs))
            nc.scalar.activation(sml[:, 0:3], sml[:, 0:3], ACT.Exp, scale=-1.0).then_inc(S("softplus exp"), 1)
            act.wait_ge(S("softplus arg"), 1)
            nc.scalar.activation(sml[:, 6:9], sml[:, 3:6], ACT.Ln).then_inc(S("softplus log"), 1)
            act.wait_ge(S("x loaded"), 16)
            squares("n1", X)
            norm_root("n1")
            act.wait_ge(S("filter pack loaded"), 16)
            for tt in range(TT):
                nc.scalar.activation(decay[:, tt, :], deltas, ACT.Exp,
                                     scale=col("neg_t", tt)).then_inc(S("decay ready"), 1)
            for h, dst in enumerate((hid1, hid2)):
                act.wait_ge(S("sine argument"), h + 1)
                nc.scalar.activation(dst, arg, ACT.Sin).then_inc(S("sine ready"), 1)
            for n in range(4):
                wait_taken(act, f"f3_{n // 2}{n % 2}")
                nc.scalar.activation(absf[:, n // 2, n % 2, :], filt[:, n // 2, n % 2, :],
                                     ACT.Abs).then_inc(S("filter abs"), 1)
            modulate("n1", H, lambda k: gs[:, 0, k:k + 1], lambda k: mod1[:, k:k + 1], "h1 ready")
            for n in range(4):
                wait_product(act, f"f5_{n}")
                nc.scalar.activation(HF[:, n // 2, n % 2, :], bank(f"f5_{n}")[:, :], ACT.Copy,
                                     scale=1.0 / T).then_inc(gone(f"f5_{n}"), 1)

            wait_product(act, "cvg")
            nc.scalar.activation(cvsg, bank("cvg")[:, :].rearrange("p (a b) -> p a b", a=2),
                                 ACT.Sigmoid).then_inc(gone("cvg"), 1)
            for n, (t0, m) in {"lrx01": (0, 2), "lrx2": (2, 1)}.items():
                wait_product(act, n)
                nc.scalar.activation(lxpad[:, t0:t0 + m, LRU_K - 1:],
                                     bank(n)[:, 0:m * T].rearrange("p (a b) -> p a b", a=m),
                                     ACT.Copy).then_inc(gone(n), 1)
            for n, (t0, m) in {"lry01": (0, 2), "lry2": (2, 1)}.items():
                wait_product(act, n)
                nc.scalar.activation(gy[:, t0:t0 + m, :], bank(n)[:, 0:m * T].rearrange("p (a b) -> p a b", a=m),
                                     ACT.Gelu_apprx_tanh).then_inc(gone(n), 1)
            for n, dst in (("q01", qT), ("k01", kT1)):
                wait_product(act, n)
                nc.scalar.activation(dst, bank(n)[0:PAIR, :].rearrange("p (a b) -> p a b", a=2),
                                     ACT.Copy).then_inc(gone(n), 1)
            for tt in range(TT):
                wait_product(act, f"v{tt}")
                nc.scalar.activation(vtok[:, tt, :], bank(f"v{tt}")[:, 0:GH * GDV],
                                     ACT.Copy).then_inc(gone(f"v{tt}"), 1)
            wait_product(act, "glr")
            nc.scalar.activation(glr, bank("glr")[0:16, 0:T], ACT.Copy).then_inc(gone("glr"), 1)
            wait_product(act, "lgp")
            for pr in range(2):
                ins = nc.scalar.activation(lgx[:, pr, :], bank("lgp")[0:PAIR, pr * T:pr * T + T], ACT.Identity,
                                           bias=col("gla_b", pr, rows=slice(0, PAIR)))
            ins.then_inc(gone("lgp"), 1)
            wait_taken(act, "lgp")
            lnb = W[0:PAIR, 0:2, :]
            link(nc.scalar.activation(lnb, lgx, ACT.Abs))
            link(nc.scalar.activation(lnb, lnb, ACT.Exp, scale=-1.0))
            nc.scalar.activation(lnb, lnb, ACT.Ln, bias=1.0).then_inc(S("gate log ready"), 1)
            for t in range(LT):
                wait_product(act, f"lru{t}")
                nc.scalar.activation(rg[:, t, :], bank(f"lru{t}")[:, 0:T], ACT.Sigmoid, bias=col("lru_ba", t))
                nc.scalar.activation(ig[:, t, :], bank(f"lru{t}")[:, T:2 * T], ACT.Sigmoid,
                                     bias=col("lru_bi", t)).then_inc(gone(f"lru{t}"), 1)
            wait_taken(act, "lru2")
            act.wait_ge(S("softplus ready"), 1)
            for t in range(LT):
                nc.scalar.activation(ag[:, t, :], rg[:, t, :], ACT.Exp, scale=lru_neg(t))
            for t in range(LT):
                nc.scalar.activation(rg[:, t, :], rg[:, t, :], ACT.Tanh, scale=lru_pos(t)).then_inc(S("lru decay"), 1)
            act.wait_ge(S("gate sums ready"), 2)
            nc.scalar.activation(eb, bcum, ACT.Exp, scale=1.0 / 16.0)
            nc.scalar.activation(kin, bcum, ACT.Exp, scale=-1.0 / 16.0)
            nc.scalar.activation(diff, diff, ACT.Exp, scale=1.0 / 16.0)
            nc.scalar.activation(gdec[:, :, :], bcum.rearrange("p a (c s) -> p a c s", s=GCH)[:, :, :, GCH - 1],
                                 ACT.Exp, scale=1.0 / 16.0).then_inc(S("gate powers ready"), 1)
            act.wait_ge(S("lru root arg"), 1)
            nc.scalar.activation(xc, xc, ACT.Sqrt, scale=2.0).then_inc(S("lru root ready"), 1)
            for n, h in (("og01", 0), ("og23", 2)):
                wait_product(act, n)
                nc.scalar.activation(sog[0:GDV, h:h + 2, :], bank(n)[0:GDV, :].rearrange("p (a b) -> p a b", a=2),
                                     ACT.Silu).then_inc(gone(n), 1)
            for n, h in (("o01", 0), ("o23", 2)):
                wait_product(act, n)
                nc.scalar.activation(W[0:GDV, 4 + h:6 + h, :], bank(n)[0:GDV, :].rearrange("p (a b) -> p a b", a=2),
                                     ACT.Square).then_inc(S("gla squared"), 1)
            for n, h in (("os01", 0), ("os23", 2)):
                wait_product(act, n)
                nc.scalar.activation(gla_root[:, h:h + 2, :], bank(n)[0:GDV, :].rearrange("p (a b) -> p a b", a=2),
                                     ACT.Sqrt, scale=1.0 / GDV, bias=col("eps", rows=slice(0, GDV))).then_inc(gone(n), 1)
            wait_taken(act, "mu")
            nc.scalar.activation(W[:, 2:4, :], u2, ACT.Square).then_inc(S("conv squared"), 1)
            wait_product(act, "var")
            nc.scalar.activation(root[:, :], bank("var")[:, 0:T], ACT.Sqrt, scale=1.0 / CONV_W,
                                 bias=col("eps")).then_inc(gone("var"), 1)
            act.wait_ge(S("conv scaled"), 1)
            for t in range(CT):
                nc.scalar.activation(u2[:, t, :], u2[:, t, :], ACT.Silu, scale=col("ln_g", t),
                                     bias=col("ln_b", t)).then_inc(S("mix u ready"), 1)

            for n in X1:
                wait_taken(act, n)
            act.dma_start(HC, a["ctxT"]).then_inc(S("ctx loaded"), 16)
            act.dma_start(view(61, 1920), a["lpack"]).then_inc(S("late pack loaded"), 16)
            act.dma_start(brow, a["brow"]).then_inc(S("late pack loaded"), 16)
            squares("n2", X)
            norm_root("n2")
            modulate("n2", H, lambda k: gs[:, 1, k:k + 1], lambda k: mod1[:, 24 + k:25 + k], "h2 ready")
            act.wait_ge(S("ctx loaded"), 16)
            squares("nc", HC)
            norm_root("nc")
            modulate("nc", HC, lambda k: gs[:, 2, k:k + 1], lambda k: mod2[:, k, 1:2], "ctx ready")

            def routing(m):
                act.wait_ge(S("route group arg"), m + 1)
                nc.scalar.activation(rv["gexp"], rv["gexp"], ACT.Exp).then_inc(S("route group exp"), 1)
                act.wait_ge(S("route pair arg"), m + 1)
                nc.scalar.activation(rv["pexp"], rv["pexp"], ACT.Exp).then_inc(S("route pair exp"), 1)

            def by_token_copies(m):
                for n in range(4):
                    name = f"ht{m}_{n}"
                    wait_product(act, name)
                    nc.scalar.activation(htok[:, n // 2, 512 * (n % 2):512 * (n % 2) + 512], bank(name)[:, :],
                                         ACT.Copy).then_inc(gone(name), 1)

            def experts_act(m, n0, count):
                def gathered(i, e):
                    act.wait_ge(S(f"moe{m} gathered"), i * 2 + e + 1)
                    nc.scalar.activation(hexp[:, e % 2, :, :], psum[4][:, :].rearrange("p (a b) -> p a b", a=DK),
                                         ACT.Copy).then_inc(S(f"moe{m} tokens ready"), 1)

                def silu(i, e):
                    used_up(act, i, 3 * e + 1, n0)
                    nc.scalar.activation(sact, psum[5][:, 0:4 * CAP].rearrange("p (a b) -> p a b", a=4),
                                         ACT.Silu).then_inc(S(f"moe{m} silu ready"), 1)

                def turn(i, last=False):
                    for e in (0, 1):
                        if not (last and e):
                            gathered(i, e + 1)
                        r = slice(CAP * e, CAP * e + CAP)
                        used_up(act, i, 3 * e + 2, n0)
                        nc.scalar.activation(yexp[r, 0:512], psum[6][r, :],
                                             ACT.Copy).then_inc(S(f"moe{m} left half ready"), 1)
                        if not (last and e):
                            silu(i, e + 1)

                gathered(0, 0)
                silu(0, 0)
                with act.Fori(0, count // 2 - 1) as i:
                    turn(i)
                turn(count // 2 - 1, last=True)
                act.wait_ge(S(f"moe{m} flag ready"), 1)
                crowded = act.value_load(flag[0:1, 0:1], min_val=0, max_val=TT * P * 2)
                with act.If(crowded > 0):
                    with act.Fori(0, count) as e:
                        for f in range(4):
                            act.wait_ge(S(f"over{m} product"), e * 4 + f + 1)
                            nc.scalar.activation(oact, psum[4][:, 0:T], ACT.Silu).then_inc(S(f"over{m} silu"), 1)

            by_token_copies(1)
            routing(0)
            experts_act(1, N1, E1)

            for b in range(4):
                wait_taken(act, f"moe1_{b}")
            squares("nf", X)
            norm_root("nf")
            modulate("nf", X, lambda k: col("g_final", k), None, "x3 ready")
            act.wait_ge(S("x3 ready"), 8)
            squares("m1", X)
            norm_root("m1")
            modulate("m1", H, lambda k: gs[:, 3, k:k + 1], lambda k: mod2[:, k, 0:1], "h3 ready")

            def two(n, h, dst, func, bias=None, scale=1.0):
                wait_product(act, n)
                for t in range(2):
                    ins = nc.scalar.activation(dst[:, h + t, :], bank(n)[:, t * T:t * T + T], func,
                                               bias=col("b_in", bias + t), scale=scale)
                ins.then_inc(gone(n), 1)

            link(nc.scalar.activation(lgs[:, 0, :], col("decay", 0, 8), ACT.Abs))
            nc.scalar.activation(lgs[:, 0, :], lgs[:, 0, :], ACT.Exp, scale=-1.0).then_inc(S("decay exp"), 1)
            act.wait_ge(S("decay arg"), 1)
            nc.scalar.activation(lgs[:, 2, :], lgs[:, 1, :], ACT.Ln).then_inc(S("decay log"), 1)
            two("kT01", 0, kraw, ACT.Identity, 4)
            two("kT23", 2, kraw, ACT.Identity, 6)
            for tt in range(TT):
                wait_product(act, f"kc{tt}")
                nc.scalar.activation(KC[:, tt, :], bank(f"kc{tt}")[:, :], ACT.Copy).then_inc(gone(f"kc{tt}"), 1)
            for half in range(2):
                for what, dst in (("vx", V), ("vc", VC)):
                    for tt in range(TT):
                        n = f"{what}{half}{tt}"
                        wait_product(act, n)
                        nc.scalar.activation(dst[:, tt, 512 * half:512 * half + 512], bank(n)[:, :],
                                             ACT.Copy).then_inc(gone(n), 1)
            act.wait_ge(S("log decay ready"), 1)
            for tt in range(TT):
                nc.scalar.activation(ctxdec[:, 0, :, tt], lgs[:, 3, 0:4], ACT.Exp, scale=col("rpos", tt))
                nc.scalar.activation(ctxdec[:, 1, :, tt], lgs[:, 3, 4:8], ACT.Exp,
                                     scale=col("pos", tt)).then_inc(S("ctx decay ready"), 1)
            for h in range(RH):
                wait_product(act, f"st{h}")
                nc.scalar.activation(S0[:, h, :, :], bank(f"st{h}")[:, :].rearrange("p (a b) -> p a b", a=2),
                                     ACT.Copy).then_inc(gone(f"st{h}"), 1)
            two("q2_01", 0, qraw, ACT.Identity, 0)
            two("q2_23", 2, qraw, ACT.Identity, 2)
            for j in range(4):
                two(f"g{2 * j}{2 * j + 1}", 2 * j, sg, ACT.Silu, 16 + 2 * j)
            for h in range(RH):
                act.wait_ge(S("decay matrix arg"), h + 1)
                act.wait_ge(S("ctx queries ready"), h) if h else None
                nc.scalar.activation(Dm, Dm, ACT.Exp)
                nc.scalar.activation(Ef, irow, ACT.Exp, scale=lgs[:, 3, h:h + 1])
                nc.scalar.activation(Eb, irow, ACT.Exp, scale=lgs[:, 4, 4 + h:5 + h],
                                     bias=backb[:, h:h + 1]).then_inc(S("decay matrix ready"), 1)
                if h:
                    readout_act(act, h - 1)
            readout_act(act, RH - 1)
            act.wait_ge(S("hyena pads zero"), 1)
            for j in range(6):
                wait_product(act, f"hy{2 * j}")
                for t in range(2):
                    ins = nc.scalar.activation(hypad[:, 2 * j + t, 1:T + 1], bank(f"hy{2 * j}")[:, t * T:t * T + T],
                                               ACT.Identity, bias=col("b_in", 24 + 2 * j + t))
                ins.then_inc(gone(f"hy{2 * j}"), 1)
            act.wait_ge(S("readout ready"), RH)
            for j in range(4):
                two(f"gr{2 * j}", 2 * j, sigR, ACT.Sigmoid, 36 + 2 * j)
            for j in range(4):
                two(f"gh{2 * j}", 2 * j, sigH, ACT.Sigmoid, 44 + 2 * j)
            for tt in range(TT):
                wait_product(act, f"zt{tt}")
                nc.scalar.activation(ztok[:, tt, :], bank(f"zt{tt}")[:, :], ACT.Copy).then_inc(gone(f"zt{tt}"), 1)

            for n in X4:
                wait_taken(act, n)
            squares("m2", X)
            norm_root("m2")
            modulate("m2", H, lambda k: gs[:, 4, k:k + 1], lambda k: mod2[:, 24 + k, 0:1], "h4 ready")
            by_token_copies(2)
            routing(1)
            experts_act(2, N3, E2)
            for b in range(4):
                wait_taken(act, f"moe2_{b}")
            squares("mf", X)
            norm_root("mf")
            modulate("mf", X, lambda k: col("g_out", k), None, "y ready")
            for j in range(2):
                act.wait_ge(S("y ready"), 4 * j + 4)
                act.dma_start(out[:, 4 * j:4 * j + 4, :], X[:, 4 * j:4 * j + 4, :]).then_inc(S("stored"), 16)
            act.wait_ge(S("stored"), 32)

        @block.vector
        def _(dve):
            steps = [0]

            def link(ins):
                steps[0] += 1
                ins.then_inc(S("vector step"), 1)
                dve.wait_ge(S("vector step"), steps[0])

            def take(ins, name):
                ins.then_inc(gone(name), 1)
                wait_taken(dve, name)

            V_ = nc.vector

            def log1p(y, w, lnw, tmp, out):
                link(V_.tensor_scalar(tmp, w, 1.0, None, ALU.subtract))
                link(V_.tensor_scalar(out, tmp, 0.0, None, ALU.is_equal))
                link(V_.tensor_tensor(tmp, tmp, out, ALU.add))
                link(V_.reciprocal(tmp, tmp))
                link(V_.tensor_tensor(tmp, tmp, lnw, ALU.mult))
                link(V_.tensor_tensor(tmp, tmp, out, ALU.add))
                link(V_.tensor_tensor(out, tmp, y, ALU.mult))

            dve.wait_ge(S("softplus exp"), 1)
            V_.tensor_scalar(sml[:, 3:6], sml[:, 0:3], 1.0, None, ALU.add).then_inc(S("softplus arg"), 1)
            dve.wait_ge(S("softplus log"), 1)
            log1p(sml[:, 0:3], sml[:, 3:6], sml[:, 6:9], sml[:, 9:12], sml[:, 12:15])
            link(V_.tensor_scalar(sml[:, 15:18], col("lam", 0, 3), -1.0, 0.0, ALU.mult, ALU.max))
            link(V_.tensor_tensor(sml[:, 15:18], sml[:, 15:18], sml[:, 12:15], ALU.add))
            V_.tensor_scalar(lru_scale[:, 0, :], sml[:, 15:18], -8.0, None, ALU.mult)
            V_.tensor_scalar(lru_scale[:, 1, :], sml[:, 15:18], 8.0, None, ALU.mult).then_inc(S("softplus ready"), 1)

            TWO_PI = 2.0 * np.pi
            C1 = 6.28125
            C2 = float(np.float32(np.round((TWO_PI - C1) * 2 ** 20) / 2 ** 20))
            C3 = float(np.float32(TWO_PI - C1 - C2))
            MAGIC = 12582912.0
            PI_BELOW = 3.1415925

            def sine_argument(name, bias):
                wait_product(dve, name)
                take(V_.tensor_scalar(arg, bank(name)[0:64, 0:T], col(bias, rows=slice(0, 64)),
                                      col("f_freq", rows=slice(0, 64)), ALU.add, ALU.mult), name)
                link(V_.tensor_scalar(rnd, arg, float(1.0 / TWO_PI), MAGIC, ALU.mult, ALU.add))
                link(V_.tensor_scalar(rnd, rnd, MAGIC, None, ALU.subtract))
                for c in (C1, C2, C3):
                    link(V_.scalar_tensor_tensor(arg, rnd, -c, arg, ALU.mult, ALU.add))
                V_.tensor_scalar(arg, arg, PI_BELOW, -PI_BELOW, ALU.min, ALU.max).then_inc(S("sine argument"), 1)

            def ada1(p):
                wait_product(dve, f"a1_{p}")
                take(V_.tensor_tensor(mod1[:, 8 * p:8 * p + 8], bank(f"a1_{p}")[:, 0:8], col("b_ada", 8 * p, 8),
                                      ALU.add), f"a1_{p}")

            def ada2(p):
                wait_product(dve, f"a2_{p}")
                take(V_.tensor_tensor(mod2[:, 8 * p:8 * p + 8, :],
                                      bank(f"a2_{p}")[:, 0:16].rearrange("p (a b) -> p a b", b=2),
                                      bc(col("b_ada2", 8 * p, 8).unsqueeze(2), [P, 8, 2]), ALU.add), f"a2_{p}")

            def gain(i, g, scale):
                V_.scalar_tensor_tensor(gs[:, i, :], scale, 1.0, col(g, 0, 8), ALU.add, ALU.mult)

            def norm_scale(key, src, dst):
                wait_taken(dve, key + "_ss")
                link(V_.reciprocal(rstd[:, :], root[:, :]))
                V_.tensor_tensor(dst[:, :, :], src[:, :, :], bc(rstd[:, :].unsqueeze(1), [P, DK, T]),
                                 ALU.mult).then_inc(S("norm scaled"), 1)

            sine_argument("f1", "f_b1")
            ada1(0)
            sine_argument("f2", "f_b2")
            for n in range(4):
                name = f"f3_{n // 2}{n % 2}"
                wait_product(dve, name)
                dve.wait_ge(S("decay ready"), n // 2 + 1)
                V_.tensor_tensor(filt[:, n // 2, n % 2, :], bank(name)[:, :], decay[:, n // 2, :],
                                 ALU.mult).then_inc(gone(name), 1)
            ada1(1)
            gain(0, "g_mix", mod1[:, 8:16])
            norm_scale("n1", X, H)
            for half in range(2):
                wait_product(dve, f"f4_{half}")
                take(V_.reciprocal(decay[:, half, :], bank(f"f4_{half}")[:, :]), f"f4_{half}")
            for tt in range(TT):
                ins = V_.tensor_tensor(filt[:, tt, :, :], filt[:, tt, :, :], decay[:, :, :], ALU.mult)
            link(ins)
            V_.tensor_tensor(absf[:, :, 0, :], filt[:, :, 0, :], filt[:, :, 1, :], ALU.add)
            V_.tensor_tensor(absf[:, :, 1, :], filt[:, :, 0, :], filt[:, :, 1, :],
                             ALU.subtract).then_inc(S("filter pair ready"), 1)

            wait_taken(dve, "cvg")
            wait_product(dve, "cvv")
            take(V_.tensor_tensor(upad[:, :, CONV_K - 1:], cvsg, bank("cvv")[:, :].rearrange("p (a b) -> p a b", a=2),
                                  ALU.mult), "cvv")
            dve.wait_ge(S("pads zero"), 1)
            wait_taken(dve, "lrx01")
            wait_taken(dve, "lrx2")
            for j in range(LRU_K):
                for t in range(LT):
                    tap = col("lru_w", t * LRU_K + j)
                    if j == 0:
                        ins = V_.tensor_scalar(xc[:, t, :], lxpad[:, t, 0:T], tap, col("lru_b", t), ALU.mult, ALU.add)
                    else:
                        ins = V_.scalar_tensor_tensor(xc[:, t, :], lxpad[:, t, j:j + T], tap, xc[:, t, :],
                                                      ALU.mult, ALU.add)
                link(ins) if j < LRU_K - 1 else ins.then_inc(S("lru conv ready"), 1)

            def long_conv(taps):
                for j in taps:
                    for t in range(CT):
                        tap = col("conv_w", t * CONV_K + j)
                        if j == 0:
                            ins = V_.tensor_scalar(u2[:, t, :], upad[:, t, 0:T], tap, col("conv_b", t),
                                                   ALU.mult, ALU.add)
                        else:
                            ins = V_.scalar_tensor_tensor(u2[:, t, :], upad[:, t, j:j + T], tap, u2[:, t, :],
                                                          ALU.mult, ALU.add)
                    link(ins) if j < CONV_K - 1 else ins.then_inc(S("conv ready"), 1)

            long_conv(range(0, 10))
            dve.wait_ge(S("gate log ready"), 1)
            link(V_.scalar_tensor_tensor(lgx, lgx, 0.0, W[0:PAIR, 0:2, :], ALU.min, ALU.subtract))
            for pr in range(2):
                ins = V_.tensor_tensor_scan(bcum[:, pr, :], segm, lgx[:, pr, :], 0.0, ALU.mult, ALU.add)
            link(ins)
            for pr in range(2):
                b4 = bcum[:, pr, :].rearrange("p (c s) -> p c s", s=GCH)
                V_.tensor_tensor(diff[:, pr, :].rearrange("p (c s) -> p c s", s=GCH),
                                 bc(b4[:, :, GCH - 1:GCH], [PAIR, T // GCH, GCH]), b4,
                                 ALU.subtract).then_inc(S("gate sums ready"), 1)
            ada1(2)
            wait_taken(dve, "lru2")
            link(V_.tensor_tensor(ig, ig, xc, ALU.mult))
            dve.wait_ge(S("lru decay"), 3)
            link(V_.tensor_scalar(xc, rg, 1.0, None, ALU.add))
            link(V_.reciprocal(xc, xc))
            V_.tensor_tensor(xc, xc, rg, ALU.mult).then_inc(S("lru root arg"), 1)
            dve.wait_ge(S("gate powers ready"), 1)
            dve.wait_ge(S("heads zero"), 1)
            wait_taken(dve, "q01")
            wait_taken(dve, "k01")
            V_.tensor_tensor(diff, diff, kT1, ALU.mult).then_inc(S("gla keys ready"), 1)
            V_.tensor_tensor(kin, kin, kT1, ALU.mult)
            for h in range(GH):
                ins = V_.scalar_tensor_tensor(qz[:, h, :], qT[:, h // 2, :], col("head", h % 2, rows=slice(0, PAIR)),
                                              eb[:, h // 2, :], ALU.mult, ALU.mult)
            ins.then_inc(S("gla queries ready"), 1)
            dve.wait_ge(S("lru root ready"), 1)
            link(V_.tensor_tensor(ig, ig, xc, ALU.mult))
            for t in range(LT):
                ins = V_.tensor_tensor_scan(rg[:, t, :], ag[:, t, :], ig[:, t, :], 0.0, ALU.mult, ALU.add)
            link(ins)
            wait_taken(dve, "lry01")
            wait_taken(dve, "lry2")
            V_.tensor_tensor(gy, gy, rg, ALU.mult).then_inc(S("mix r ready"), 1)
            ada1(3)
            wait_product(dve, "k2t")
            for ch in range(2):
                r = slice(64 * ch, 64 * ch + 64)
                ins = V_.tensor_copy(k2z[r, :, ch, :, :].rearrange("p a b c -> p a (b c)"),
                                     bank("k2t")[r, 0:4 * PAIR].rearrange("p (a b) -> p a b", a=TT))
            ins.then_inc(gone("k2t"), 1)
            for n, h in (("sc01", 0), ("sc23", 2)):
                wait_product(dve, n)
                V_.tensor_tensor(sm[:, h:h + 2, :, :].rearrange("p a b c -> p (a b) c"),
                                 bank(n)[:, :].rearrange("p (a b) -> p a b", a=4),
                                 bc(gmask.unsqueeze(1), [P, 4, P]), ALU.mult).then_inc(gone(n), 1)
            for c in range(3):
                wait_product(dve, f"kv{c}")
                kv = bank(f"kv{c}")[0:PAIR, 0:4 * GDV].rearrange("p (a b) -> p a b", a=2)
                if c == 0:
                    ins = V_.tensor_copy(states[:, 0, :, :], kv)
                else:
                    for pr in range(2):
                        ins = V_.scalar_tensor_tensor(states[:, c, pr, :], states[:, c - 1, pr, :],
                                                      gdec[:, pr, c:c + 1], kv[:, pr, :], ALU.mult, ALU.add)
                take(ins, f"kv{c}")
            long_conv(range(10, CONV_K))
            for n, o, h in (("os01", "o01", 0), ("os23", "o23", 2)):
                wait_taken(dve, n)
                link(V_.reciprocal(gla_root[:, h:h + 2, :], gla_root[:, h:h + 2, :]))
                tmp = W[0:GDV, 4 + h:6 + h, :]
                take(V_.tensor_tensor(tmp, bank(o)[0:GDV, :].rearrange("p (a b) -> p a b", a=2),
                                      gla_root[:, h:h + 2, :], ALU.mult), o)
            wait_taken(dve, "og23")
            for h in range(GH):
                V_.scalar_tensor_tensor(sog[0:GDV, h, :], W[0:GDV, 4 + h, :], col("gla_g", h, rows=slice(0, GDV)),
                                        sog[0:GDV, h, :], ALU.mult, ALU.mult).then_inc(S("mix o ready"), 1)
            ada1(4)
            ada1(5)
            ada2(0)
            ada2(1)
            wait_product(dve, "mu")
            for t in range(CT):
                ins = V_.scalar_tensor_tensor(u2[:, t, :], bank("mu")[:, 0:T], -1.0 / CONV_W, u2[:, t, :],
                                              ALU.mult, ALU.add)
            ins.then_inc(gone("mu"), 1)
            gain(1, "g_ffn", mod1[:, 32:40])
            gain(2, "g1", mod2[:, 8:16, 1])
            gain(3, "g1", mod2[:, 8:16, 0])
            wait_taken(dve, "var")
            link(V_.reciprocal(rstd[:, :], root[:, :]))
            V_.tensor_tensor(u2, u2, bc(rstd[:, :].unsqueeze(1), [P, CT, T]), ALU.mult).then_inc(S("conv scaled"), 1)

            def add_to_x(names, gate, width=2):
                for j, n in enumerate(names):
                    wait_product(dve, n)
                    for t in range(2):
                        k = 2 * j + t
                        ins = V_.scalar_tensor_tensor(X[:, k, :], bank(n)[:, t * T:t * T + T], gate(k), X[:, k, :],
                                                      ALU.mult, ALU.add)
                    ins.then_inc(gone(n), 1)

            add_to_x(X1, lambda k: mod1[:, 16 + k:17 + k])
            norm_scale("n2", X, H)
            ada2(2)
            norm_scale("nc", HC, HC)
            ada2(3)

            def R(lo, n):
                return route[:, lo:lo + n]

            def R2(lo, m):
                return route[:, lo:lo + TT * m].rearrange("p (t m) -> p t m", t=TT)

            def routing(m, n, bias, tie):
                w = 4 + 4 * n
                L = R2(0, w)
                wait_product(dve, f"rt{m + 1}")
                take(V_.tensor_tensor(L, bank(f"rt{m + 1}")[:, 0:TT * w].rearrange("p (t m) -> p t m", t=TT),
                                      bc(col(bias, 0, w).unsqueeze(1), [P, TT, w]), ALU.add), f"rt{m + 1}")
                gmax, gexp, gsum = R(72, 2), rv["gexp"], R(90, 2)
                first, tmp, best = R2(104, 4), R2(280, n), R(94, 2)

                def one_hot(dst, src, top, names_, k):
                    link(V_.tensor_tensor(dst, src, bc(top.unsqueeze(2), [P, TT, k]), ALU.is_equal))
                    link(V_.tensor_tensor(dst, dst, bc(col(names_, 0, k).unsqueeze(1), [P, TT, k]), ALU.mult))
                    link(V_.tensor_reduce(best, dst, AX.X, ALU.max))
                    link(V_.tensor_tensor(dst, dst, bc(best.unsqueeze(2), [P, TT, k]), ALU.is_equal))

                link(V_.tensor_reduce(gmax, L[:, :, 0:4], AX.X, ALU.max))
                V_.tensor_tensor(gexp, L[:, :, 0:4], bc(gmax.unsqueeze(2), [P, TT, 4]),
                                 ALU.subtract).then_inc(S("route group arg"), 1)
                one_hot(first, L[:, :, 0:4], gmax, "tie4", 4)
                es, m1, oh1, e2, m2, oh2 = R2(176, n), R(192, 2), R2(200, n), R2(216, n), R(232, 2), R2(240, n)
                for t in range(TT):
                    prod = route[:, 112:112 + 4 * n].rearrange("p (e g) -> p e g", g=4)
                    link(V_.tensor_tensor(prod, L[:, t, 4:].rearrange("p (g e) -> p e g", g=4),
                                          bc(first[:, t, :].unsqueeze(1), [P, n, 4]), ALU.mult))
                    link(V_.tensor_reduce(es[:, t, :], prod, AX.X, ALU.add))
                link(V_.tensor_reduce(m1, es, AX.X, ALU.max))
                one_hot(oh1, es, m1, f"tie{n}", n)
                link(V_.scalar_tensor_tensor(e2, oh1, -3.0e38, es, ALU.mult, ALU.add))
                link(V_.tensor_reduce(m2, e2, AX.X, ALU.max))
                one_hot(oh2, e2, m2, f"tie{n}", n)
                V_.tensor_tensor(rv["pexp"], m2, m1, ALU.subtract).then_inc(S("route pair arg"), 1)
                dve.wait_ge(S("route group exp"), m + 1)
                E = 4 * n
                both = R2(280, n)
                link(V_.tensor_tensor(both, oh1, oh2, ALU.add))
                for t in range(TT):
                    ins = V_.tensor_tensor(over[:, t, 0:E].rearrange("p (g e) -> p g e", g=4),
                                           bc(first[:, t, :].unsqueeze(2), [P, 4, n]),
                                           bc(both[:, t, :].unsqueeze(1), [P, 4, n]), ALU.mult)
                ins.then_inc(S("chosen"), 1)
                link(V_.tensor_reduce(gsum, gexp, AX.X, ALU.add))
                dve.wait_ge(S("route pair exp"), m + 1)
                w1, w2 = R(258, 2), R(260, 2)
                link(V_.tensor_scalar(w1, rv["pexp"], 1.0, None, ALU.add))
                link(V_.tensor_tensor(w1, w1, gsum, ALU.mult))
                link(V_.reciprocal(w1, w1))
                link(V_.tensor_tensor(w2, w1, rv["pexp"], ALU.mult))
                link(V_.tensor_tensor(oh1, oh1, bc(w1.unsqueeze(2), [P, TT, n]), ALU.mult))
                link(V_.tensor_tensor(oh2, oh2, bc(w2.unsqueeze(2), [P, TT, n]), ALU.mult))
                link(V_.tensor_tensor(oh1, oh1, oh2, ALU.add))
                for t in range(TT):
                    link(V_.tensor_tensor(comb[:, t, 0:4 * n].rearrange("p (g e) -> p g e", g=4),
                                          bc(first[:, t, :].unsqueeze(2), [P, 4, n]),
                                          bc(oh1[:, t, :].unsqueeze(1), [P, 4, n]), ALU.mult))

            def places_and_overflow(m, E):
                name = f"rk{m}"
                wait_product(dve, name)
                take(V_.scalar_tensor_tensor(rank[:, :, 0:E], bank(name)[:, 0:TT * E].rearrange("p (t e) -> p t e", t=TT),
                                             1.0, over[:, :, 0:E], ALU.add, ALU.mult), name)
                link(V_.tensor_scalar(rank[:, :, 0:E], rank[:, :, 0:E], 1.0, None, ALU.subtract))
                link(V_.tensor_scalar(over[:, :, 0:E], rank[:, :, 0:E], float(CAP), None, ALU.is_ge))
                V_.tensor_reduce(n_over[:, 0:1], over[:, :, 0:E], AX.XY, ALU.add).then_inc(S("overflow counted"), 1)
                dve.wait_ge(S("overflow counted"), m)
                V_.tensor_tensor(over[:, :, 0:E], over[:, :, 0:E], comb[:, :, 0:E], ALU.mult)
                wait_product(dve, f"fl{m}")
                take(V_.tensor_copy(flag[:, :], bank(f"fl{m}")[:, 0:1]), f"fl{m}")
                dve.sem_inc(S(f"moe{m} flag ready"), 1)

            def experts_dve(m, n0, count):
                def picks(i, e):
                    for t in range(TT):
                        ins = V_.tensor_scalar(pick[:, e % 2, t, :], places, rank[:, t, bass.ds(i * 2 + e, 1)], None,
                                               ALU.is_equal)
                    ins.then_inc(S(f"moe{m} picks ready"), 1)

                def hidden(i, e):
                    dve.wait_ge(S(f"moe{m} silu ready"), i * 2 + e + 1)
                    V_.tensor_tensor(hid, sact, psum[5][:, 4 * CAP:8 * CAP].rearrange("p (a b) -> p a b", a=4),
                                     ALU.mult).then_inc(S(f"moe{m} hidden"), 1)

                def turn(i, last=False):
                    for e in (0, 1):
                        if not last:
                            picks(i, e + 2)
                        if e == 0:
                            for t in range(TT):
                                for h in (0, 1):
                                    at_e = bass.ds(i * 2 + h, 1)
                                    ins = V_.tensor_scalar(pickw[:, t, CAP * h:CAP * h + CAP], places,
                                                           rank[:, t, at_e], comb[:, t, at_e],
                                                           ALU.is_equal, ALU.mult)
                            ins.then_inc(S(f"moe{m} weighted picks ready"), 1)
                        r = slice(CAP * e, CAP * e + CAP)
                        used_up(dve, i, 3 * e + 2, n0)
                        V_.tensor_copy(yexp[r, 512:1024], psum[7][r, :]).then_inc(S(f"moe{m} right half ready"), 1)
                        if e:
                            dve.wait_ge(S(f"moe{m} turned"), i + 1)
                            V_.tensor_copy(put, psum[4][:, 0:T]).then_inc(S(f"moe{m} put ready"), 1)
                        if not (last and e):
                            hidden(i, e + 1)

                V_.memset(zeros, 0.0).then_inc(S("zeros set"), 1)
                picks(0, 0)
                picks(0, 1)
                hidden(0, 0)
                with dve.Fori(0, count // 2 - 1) as i:
                    turn(i)
                turn(count // 2 - 1, last=True)
                crowded = dve.value_load(flag[0:1, 0:1], min_val=0, max_val=TT * P * 2)
                with dve.If(crowded > 0):
                    dve.sem_inc(S(f"over{m} hidden"), 1)
                    with dve.Fori(0, count) as e:
                        for t in range(TT):
                            ins = V_.tensor_scalar(odiag[:, t, :], ident, over[:, t, bass.ds(e, 1)], None, ALU.mult)
                        ins.then_inc(S(f"over{m} diagonal"), 1)
                        dve.wait_ge(S(f"over{m} weights spread"), e + 1)
                        for f in range(4):
                            dve.wait_ge(S(f"over{m} silu"), e * 4 + f + 1)
                            V_.tensor_tensor(oweigh, oact, psum[6][:, 0:T], ALU.mult).then_inc(S(f"over{m} weighed"), 1)
                            dve.wait_ge(S(f"over{m} weighed"), e * 4 + f + 1)
                            V_.tensor_tensor(ohid, oweigh, psum[4][:, T:2 * T],
                                             ALU.mult).then_inc(S(f"over{m} hidden"), 1)
                for b in range(4, BANKS):
                    wait_product(dve, f"moe{m}_{b}")
                    dve.sem_inc(drained[b], 1)

            routing(0, 4, "br1", "tie4")
            ada2(4)
            ada2(5)
            link(V_.tensor_scalar(gs[:, 4, :], mod2[:, 32:40, 0], 1.0, None, ALU.add))
            link(V_.tensor_tensor(gs[:, 4, :], gs[:, 4, :], col("g2", 0, 8), ALU.mult))
            places_and_overflow(1, E1)
            experts_dve(1, N1, E1)
            add_to_x([f"moe1_{b}" for b in range(4)], lambda k: mod1[:, 40 + k:41 + k])
            norm_scale("nf", X, X)
            norm_scale("m1", X, H)

            dve.wait_ge(S("decay exp"), 1)
            V_.tensor_scalar(lgs[:, 1, :], lgs[:, 0, :], 1.0, None, ALU.add).then_inc(S("decay arg"), 1)
            dve.wait_ge(S("decay log"), 1)
            log1p(lgs[:, 0, :], lgs[:, 1, :], lgs[:, 2, :], lgs[:, 4, :], lgs[:, 3, :])
            link(V_.scalar_tensor_tensor(lgs[:, 3, :], col("decay", 0, 8), 0.0, lgs[:, 3, :], ALU.min, ALU.subtract))
            V_.tensor_scalar(lgs[:, 4, :], lgs[:, 3, :], -1.0, None, ALU.mult)
            V_.tensor_scalar(backb[:, :], lgs[:, 3, 4:8], float(T + 1), None, ALU.mult).then_inc(S("log decay ready"), 1)
            dve.wait_ge(S("log decay ready"), 1)

            def rotate(name, h, raw, dst, scale):
                wait_product(dve, name)
                cos, sin = (bc(rope[:, i:i + 1, :], [P, 2, T]) for i in range(2))
                link(V_.scalar_tensor_tensor(dst[:, h:h + 2, :], raw[:, h:h + 2, :], scale, cos, ALU.mult, ALU.mult))
                take(V_.scalar_tensor_tensor(raw[:, h:h + 2, :], bank(name)[:, :].rearrange("p (a b) -> p a b", a=2),
                                             scale, sin, ALU.mult, ALU.mult), name)
                V_.tensor_tensor(dst[:, h:h + 2, :], dst[:, h:h + 2, :], raw[:, h:h + 2, :],
                                 ALU.add).then_inc(S("rotated"), 1)

            dve.wait_ge(S("ctx decay ready"), 2)
            wait_product(dve, "vc11")
            wait_taken(dve, "kc1")
            for tt in range(TT):
                for way in range(2):
                    V_.tensor_tensor(kdec[:, :, way, tt, :], KC[:, tt, :].rearrange("p (h d) -> p h d", h=RH),
                                     bc(ctxdec[:, way, :, tt:tt + 1], [P, RH, P]),
                                     ALU.mult).then_inc(S("ctx keys ready"), 1)
            rotate("rk01", 0, kraw, kr, 1.0)
            rotate("rk23", 2, kraw, kr, 1.0)
            rotate("rq01", 0, qraw, qr, float(RDK) ** -0.5)
            rotate("rq23", 2, qraw, qr, float(RDK) ** -0.5)

            def readout(h):
                wait_taken(dve, f"rs{h}")
                link(V_.reciprocal(rstd[:, :], root[:, :]))
                take(V_.tensor_tensor(rtmp, bank(f"o{h}")[:, :].rearrange("p (a b) -> p a b", a=2),
                                      bc(rstd[:, :].unsqueeze(1), [P, 2, T]), ALU.mult), f"o{h}")
                V_.tensor_tensor(sg[:, 2 * h:2 * h + 2, :], sg[:, 2 * h:2 * h + 2, :], rtmp,
                                 ALU.mult).then_inc(S("readout ready"), 1)

            wait_taken(dve, "g67")
            for h in range(RH):
                for jt in range(TT):
                    V_.tensor_scalar(Dm[:, jt, :], irow, col("pos1", jt), lgs[:, 4, 4 + h:5 + h],
                                     ALU.subtract, ALU.mult)
                    ins = V_.tensor_scalar(dtmp[:, jt, :], irow, col("pos1", jt), lgs[:, 3, h:h + 1],
                                           ALU.subtract, ALU.mult)
                link(ins)
                V_.tensor_tensor(Dm, Dm, dtmp, ALU.min).then_inc(S("decay matrix arg"), 1)
                dve.wait_ge(S("decay matrix ready"), h + 1)
                V_.tensor_tensor(qf[:, h % 2, :], qr[:, h, :], Ef, ALU.mult)
                V_.tensor_tensor(qb[:, h % 2, :], qr[:, h, :], Eb, ALU.mult).then_inc(S("ctx queries ready"), 1)
                wait_product(dve, f"s{h}")
                take(V_.tensor_tensor(Pm[h % 2], bank(f"s{h}")[:, :].rearrange("p (a b) -> p a b", a=2), Dm,
                                      ALU.mult), f"s{h}")
                if h:
                    readout(h - 1)
            readout(RH - 1)

            for n in range(6):
                wait_taken(dve, f"hy{2 * n}")
            for c in range(HYT):
                for j in range(3):
                    for dst, t in ((x0[:, c, :], c), (cv1, HYT + c), (cv2, 2 * HYT + c)):
                        tap = col("hy_w", 3 * t + j)
                        if j == 0:
                            ins = V_.tensor_scalar(dst, hypad[:, t, 0:T], tap, col("hy_b", t), ALU.mult, ALU.add)
                        else:
                            ins = V_.scalar_tensor_tensor(dst, hypad[:, t, j:j + T], tap, dst, ALU.mult, ALU.add)
                    link(ins)
                V_.tensor_tensor(zT[:, c, :], cv1, cv2, ALU.mult).then_inc(S("z ready"), 1)
                dve.wait_ge(S("z ready"), c + 1)
            for kt in range(2):
                zr, zi = f"zr{kt}", f"zi{kt}"
                wait_product(dve, zi)
                V_.tensor_tensor(Y[:, 0, kt, :], bank(zr)[:, :], HF[:, 0, kt, :], ALU.mult)
                V_.tensor_tensor(Y[:, 1, kt, :], bank(zr)[:, :], HF[:, 1, kt, :], ALU.mult).then_inc(gone(zr), 1)
                V_.tensor_tensor(ztmp[:, 0, :], bank(zi)[:, :], HF[:, 1, kt, :], ALU.mult)
                take(V_.tensor_tensor(ztmp[:, 1, :], bank(zi)[:, :], HF[:, 0, kt, :], ALU.mult), zi)
                V_.tensor_tensor(Y[:, 0, kt, :], Y[:, 0, kt, :], ztmp[:, 0, :], ALU.subtract)
                V_.tensor_tensor(Y[:, 1, kt, :], Y[:, 1, kt, :], ztmp[:, 1, :], ALU.add).then_inc(S("spectrum ready"), 1)
                dve.wait_ge(S("spectrum ready"), kt + 1)
            for c in range(HYT):
                n = f"yt{c // 2 * 2}"
                wait_product(dve, n)
                ins = V_.scalar_tensor_tensor(zT[:, c, :], zT[:, c, :], col("skip", c),
                                              bank(n)[:, (c % 2) * T:(c % 2) * T + T], ALU.mult, ALU.add)
                if c % 2:
                    take(ins, n)
                    V_.tensor_tensor(hyo[:, c - 1:c + 1, :], zT[:, c - 1:c + 1, :], x0[:, c - 1:c + 1, :],
                                     ALU.mult).then_inc(S("hyena ready"), 1)
            for j in range(4):
                wait_taken(dve, f"gr{2 * j}")
                wait_taken(dve, f"gh{2 * j}")
            for j in range(4):
                n = f"ro{2 * j}"
                wait_product(dve, n)
                V_.tensor_tensor(H[:, 2 * j:2 * j + 2, :], bank(n)[:, :].rearrange("p (a b) -> p a b", a=2),
                                 sigR[:, 2 * j:2 * j + 2, :], ALU.mult).then_inc(gone(n), 1)
            for j in range(4):
                n = f"ho{2 * j}"
                wait_product(dve, n)
                take(V_.tensor_tensor(sigH[:, 2 * j:2 * j + 2, :], bank(n)[:, :].rearrange("p (a b) -> p a b", a=2),
                                      sigH[:, 2 * j:2 * j + 2, :], ALU.mult), n)
                V_.tensor_tensor(H[:, 2 * j:2 * j + 2, :], H[:, 2 * j:2 * j + 2, :], sigH[:, 2 * j:2 * j + 2, :],
                                 ALU.add).then_inc(S("merged"), 1)
            add_to_x(X4, lambda k: mod2[:, 16 + k, 0:1])
            norm_scale("m2", X, H)
            routing(1, 8, "br2", "tie8")
            places_and_overflow(2, E2)
            experts_dve(2, N3, E2)
            add_to_x([f"moe2_{b}" for b in range(4)], lambda k: mod2[:, 40 + k, 0:1])
            norm_scale("mf", X, X)

        @block.tensor
        def _(pe):
            order = list(place)
            done = [0]

            def begin(name):
                while order[done[0]] != name:
                    assert order[done[0]].startswith("a"), (order[done[0]], name)
                    done[0] += 1
                done[0] += 1
                b, use = place[name]
                if use:
                    pe.wait_ge(drained[b], use)
                return psum[b]

            def end(ins, name):
                ins.then_inc(filled[place[name][0]], 1)

            def mm(out_, lhsT, rhs, start, stop):
                return nc.tensor.matmul(out_, lhsT, rhs, start=start, stop=stop)

            def ss(name, src_tiles, signal, base, per):
                b = begin(name)
                n = len(src_tiles)
                for k, t in enumerate(src_tiles):
                    if k % per == 0:
                        pe.wait_ge(S(signal), base + k // per + 1)
                    rows = t.shape[0]
                    ins = mm(b[0:rows, 0:T], ones[0:rows, 0:rows], t, k == 0, k == n - 1)
                end(ins, name)

            def norm(key):
                ss(key + "_ss", [W[:, k, :] for k in range(DK)], "squared", 4 * NORM[key], 2)

            def ada(which, p):
                name = f"a{which}_{p}"
                b = begin(name)
                n = which
                for j in (2 * p, 2 * p + 1):
                    key = (f"ada{which}", j)
                    wait_slab(pe, slab_no[key])
                    w = slab(key, 8, 512)
                    for f in range(4):
                        o = (4 * (j % 2) + f) * n
                        for k in range(DK):
                            rhs = cact[:, k:k + 1] if which == 1 else cact[:, 8 + 2 * k:10 + 2 * k]
                            ins = mm(b[:, o:o + n], w[:, k, f * P:f * P + P], rhs, k == 0, k == DK - 1)
                    if j % 2:
                        free_and_end(ins, key, name)
                    else:
                        ins.then_inc(freed[slab_no[key] % SLOTS], 1)

            def free_and_end(ins, key, name):
                end(ins, name)
                pe.wait_ge(filled[place[name][0]], place[name][1] + 1)
                pe.sem_inc(freed[slab_no[key] % SLOTS], 1)

            def proj(name, w, c0, src, tiles, m=P, free=None, nk=DK):
                b = begin(name)
                for t in range(tiles):
                    for k in range(nk):
                        ins = mm(b[0:m, t * T:t * T + T], w[:, k, c0 + t * m:c0 + t * m + m], src[:, k, :],
                                 k == 0, k == nk - 1)
                if free:
                    free_and_end(ins, free, name)
                else:
                    end(ins, name)

            def by_token(name, w, c0, width, src, tt, free=None, bias=None):
                b = begin(name)
                for k in range(DK):
                    ins = mm(b[:, 0:width], src[:, k, tt * P:tt * P + P], w[:, k, c0:c0 + width], k == 0,
                             k == DK - 1 and bias is None)
                if bias is not None:
                    ins = mm(b[:, 0:width], ones[0:1, :], bias, False, True)
                if free:
                    free_and_end(ins, free, name)
                else:
                    end(ins, name)

            pe.wait_ge(S("ones set"), 1)
            norm("n1")
            pe.wait_ge(S("filter pack loaded"), 16)
            b = begin("f1")
            end(mm(b[0:64, 0:T], fw1, feats, True, True), "f1")
            pe.wait_ge(S("c ready"), 1)
            ada(1, 0)
            pe.wait_ge(S("sine ready"), 1)
            b = begin("f2")
            end(mm(b[0:64, 0:T], fw2, hid1, True, True), "f2")
            pe.wait_ge(S("sine ready"), 2)
            for tt in range(TT):
                for half in range(2):
                    b = begin(f"f3_{tt}{half}")
                    end(mm(b[:, :], hid2[:, tt * P:tt * P + P], fw3[:, half * HYW:half * HYW + HYW], True, True),
                        f"f3_{tt}{half}")
            ada(1, 1)
            pe.wait_ge(S("filter abs"), 4)
            for half in range(2):
                b = begin(f"f4_{half}")
                for tt in range(TT):
                    ins = mm(b[:, :], ones[:, :], absf[:, tt, half, :], tt == 0, tt == TT - 1)
                end(ins, f"f4_{half}")
            pe.wait_ge(S("filter pair ready"), 1)
            for n in range(4):
                ri, kt = n // 2, n % 2
                b = begin(f"f5_{n}")
                for tt in range(TT):
                    ins = mm(b[:, :], basis[:, ri, tt, kt * P:kt * P + P], absf[:, tt, ri, :], tt == 0, tt == TT - 1)
                end(ins, f"f5_{n}")

            pe.wait_ge(S("h1 ready"), DK)
            keys = [("win", j) for j in range(6)]
            ws = [slab(k, 8, c1 - c0) for k, (c0, c1) in zip(keys, WIN_CUTS)]

            def arrived(key):
                wait_slab(pe, slab_no[key])

            arrived(keys[0])
            proj("cvg", ws[0], CONV_W, H, 2)
            proj("cvv", ws[0], 0, H, 2, free=keys[0])
            arrived(keys[1])
            proj("lrx01", ws[1], 0, H, 2)
            proj("lrx2", ws[1], 2 * P, H, 1, free=keys[1])
            arrived(keys[2])
            proj("lry01", ws[2], 0, H, 2)
            proj("lry2", ws[2], 2 * P, H, 1, free=keys[2])
            arrived(keys[3])
            proj("q01", ws[3], 0, H, 2, m=PAIR)
            proj("k01", ws[3], GH * GDK, H, 2, m=PAIR, free=keys[3])
            arrived(keys[4])
            for tt in range(TT):
                by_token(f"v{tt}", ws[4], 0, GH * GDV, H, tt)
            proj("glr", ws[4], GH * GDV, H, 1, m=16, free=keys[4])
            pe.wait_ge(S("mixer pack loaded"), 48)
            wait_taken(pe, "glr")
            b = begin("lgp")
            for pr in range(2):
                ins = mm(b[0:PAIR, pr * T:pr * T + T], glaw[:, pr, :], glr, True, True)
            end(ins, "lgp")
            arrived(keys[5])
            proj("og01", ws[5], 0, H, 2, m=GDV)
            proj("og23", ws[5], 2 * GDV, H, 2, m=GDV, free=keys[5])
            ada(1, 2)
            pe.wait_ge(S("lru conv ready"), 1)
            for t in range(LT):
                b = begin(f"lru{t}")
                for g in range(2):
                    ins = mm(b[:, g * T:g * T + T], lruw[:, g, t, :], xc[:, t, :], True, True)
                end(ins, f"lru{t}")
            ada(1, 3)
            pe.wait_ge(S("gla keys ready"), 1)
            b = begin("k2t")
            for tt in range(TT):
                for pr in range(2):
                    o = (2 * tt + pr) * PAIR
                    ins = nc.tensor.transpose(b[:, o:o + PAIR], diff[:, pr, tt * P:tt * P + P],
                                              ident[0:PAIR, 0:PAIR])
            end(ins, "k2t")
            pe.wait_ge(S("gla queries ready"), 1)
            for h in range(GH):
                if h % 2 == 0:
                    b = begin(f"sc{h}{h + 1}")
                for tt in range(TT):
                    o = (2 * (h % 2) + tt) * P
                    s = slice(tt * P, tt * P + P)
                    ins = mm(b[:, o:o + P], kin[:, h // 2, s], qz[:, h, s], True, True)
                if h % 2:
                    end(ins, f"sc{h - 1}{h}")
            wait_taken(pe, "k2t")
            wait_taken(pe, "v1")
            for c in range(3):
                b = begin(f"kv{c}")
                for pr in range(2):
                    ins = mm(b[0:PAIR, pr * 192:pr * 192 + 192], k2z[:, c // 2, c % 2, pr, :],
                             vtok[:, c // 2, pr * 192:pr * 192 + 192], True, True)
                end(ins, f"kv{c}")
            wait_taken(pe, "sc23")
            wait_taken(pe, "kv2")
            for h in range(GH):
                if h % 2 == 0:
                    b = begin(f"o{h}{h + 1}")
                for tt in range(TT):
                    o = (h % 2) * T + tt * P
                    mm(b[0:GDV, o:o + P], vtok[:, tt, h * GDV:h * GDV + GDV], sm[:, h, tt, :], True, False)
                    for c in (2 * tt, 2 * tt + 1):
                        if c:
                            e = (h % 2) * GDV
                            ins = mm(b[0:GDV, (h % 2) * T + c * GCH:(h % 2) * T + c * GCH + GCH],
                                     states[:, c - 1, h // 2, e:e + GDV], qz[:, h, c * GCH:c * GCH + GCH],
                                     False, c % 2 == 1)
                if h % 2:
                    end(ins, f"o{h - 1}{h}")
            for h in range(GH):
                if h % 2 == 0:
                    pe.wait_ge(S("gla squared"), h // 2 + 1)
                    b = begin(f"os{h}{h + 1}")
                ins = mm(b[0:GDV, (h % 2) * T:(h % 2) * T + T], ones[0:GDV, 0:GDV], W[0:GDV, 4 + h, :], True, True)
                if h % 2:
                    end(ins, f"os{h - 1}{h}")
            ada(1, 4)
            ada(1, 5)
            ada(2, 0)
            ada(2, 1)
            ss("mu", [u2[:, t, :] for t in range(CT)], "conv ready", 0, CT)
            ss("var", [W[:, 2 + t, :] for t in range(CT)], "conv squared", 0, CT)

            pe.wait_ge(S("mix u ready"), 2)
            pe.wait_ge(S("mix r ready"), 1)
            pe.wait_ge(S("mix o ready"), GH)
            mix = ([u2[:, t, :] for t in range(CT)] + [gy[:, t, :] for t in range(LT)]
                   + [sog[0:GDV, h, :] for h in range(GH)])
            for k in range(8):
                j = min(k // 3, 2)
                key = ("wout", j)
                c0, c1 = WOUT_CUTS[j]
                w = c1 - c0
                if k % 3 == 0:
                    arrived(key)
                if k % 2 == 0:
                    b = begin(f"wo{k}{k + 1}")
                for n, src in enumerate(mix):
                    rows = src.shape[0]
                    o = n * w + k * P - c0
                    ins = mm(b[:, (k % 2) * T:(k % 2) * T + T],
                             ring[0:rows, slab_no[key] % SLOTS, o:o + P], src, n == 0, n == len(mix) - 1)
                if k in (2, 7):
                    if k == 7:
                        free_and_end(ins, key, "wo67")
                    else:
                        ins.then_inc(freed[slab_no[key] % SLOTS], 1)
                elif k == 5:
                    free_and_end(ins, key, "wo45")
                elif k % 2:
                    end(ins, f"wo{k - 1}{k}")
            norm("n2")
            ada(2, 2)
            norm("nc")
            ada(2, 3)

            def router(m, n):
                w = 4 + 4 * n
                base = 0 if m == 0 else DK * 20
                v = wr[:, base:base + DK * w].rearrange("p (k w) -> p k w", k=DK)
                pe.wait_ge(S(f"h{2 * m + 2} ready"), DK)
                b = begin(f"rt{m + 1}")
                for tt in range(TT):
                    for k in range(DK):
                        ins = mm(b[:, tt * w:tt * w + w], H[:, k, tt * P:tt * P + P], v[:, k, :], k == 0, k == DK - 1)
                end(ins, f"rt{m + 1}")

            def turn_h(m):
                for n in range(4):
                    tt, half = n // 2, n % 2
                    b = begin(f"ht{m}_{n}")
                    for k in range(4):
                        ins = nc.tensor.transpose(b[:, k * P:k * P + P], H[:, 4 * half + k, tt * P:tt * P + P], ident)
                    end(ins, f"ht{m}_{n}")

            def ranks(m, E):
                pe.wait_ge(S("chosen"), m)
                b = begin(f"rk{m}")
                mm(b[:, 0:E], before, over[:, 0, 0:E], True, True)
                mm(b[:, E:2 * E], before, over[:, 1, 0:E], True, False)
                end(mm(b[:, E:2 * E], ones[:, :], over[:, 0, 0:E], False, True), f"rk{m}")
                pe.wait_ge(S("overflow counted"), m)
                b = begin(f"fl{m}")
                end(mm(b[:, 0:1], ones[:, :], n_over[:, 0:1], True, True), f"fl{m}")

            def experts_pe(m, n0, count):
                for b in range(BANKS):
                    begin(f"moe{m}_{b}")
                pe.wait_ge(S("zeros set"), m)
                for b in range(4):
                    nc.tensor.matmul(psum[b][:, :], ident, zeros, start=True, stop=False, skip_group_check=True)

                def weights(i, j, k):
                    n = n0 + j
                    pe.wait_ge(landed[n % SLOTS], i * 32 + 32 * (n // SLOTS + 1))
                    return ring[:, n % SLOTS, :].rearrange("p (k w) -> p k w", k=k)

                def gather(i, e):
                    pe.wait_ge(S(f"moe{m} picks ready"), i * 2 + e + 1)
                    for k in range(DK):
                        for t in range(TT):
                            ins = mm(psum[4][:, k * CAP:k * CAP + CAP], htok[:, t, k * P:k * P + P],
                                     pick[:, e % 2, t, :], t == 0, t == TT - 1)
                    ins.then_inc(S(f"moe{m} gathered"), 1)

                def gate_up(i, e):
                    pe.wait_ge(S(f"moe{m} tokens ready"), i * 2 + e + 1)
                    for half in range(2):
                        w = weights(i, 3 * e + half, DK)
                        for f in range(4):
                            o = (4 * half + f) * CAP
                            for k in range(DK):
                                ins = mm(psum[5][:, o:o + CAP], w[:, k, f * P:f * P + P], hexp[:, e % 2, k, :],
                                         k == 0, k == DK - 1)
                        ins.then_inc(freed[(n0 + 3 * e + half) % SLOTS], 1)

                def down(i, e):
                    w = weights(i, 3 * e + 2, 4)
                    pe.wait_ge(S(f"moe{m} hidden"), i * 2 + e + 1)
                    for half in range(2):
                        for f in range(4):
                            ins = mm(psum[6 + half][CAP * e:CAP * e + CAP, :], hid[:, f, :],
                                     w[:, f, half * 512:half * 512 + 512], f == 0, f == 3)
                    ins.then_inc(freed[(n0 + 3 * e + 2) % SLOTS], 1)

                def turn(i, last=False):
                    for e in (0, 1):
                        if not (last and e):
                            gather(i, e + 1)
                        down(i, e)
                        if e:
                            pe.wait_ge(S(f"moe{m} tokens ready"), i * 2 + 2 + (not last))
                            pe.wait_ge(S(f"moe{m} weighted picks ready"), i + 1)
                            for t in range(TT):
                                ins = nc.tensor.transpose(psum[4][:, t * P:t * P + P], pickw[:, t, :], ident)
                            ins.then_inc(S(f"moe{m} turned"), 1)
                        if not (last and e):
                            gate_up(i, e + 1)
                    pe.wait_ge(S(f"moe{m} left half ready"), i * 2 + 2)
                    pe.wait_ge(S(f"moe{m} right half ready"), i * 2 + 2)
                    pe.wait_ge(S(f"moe{m} put ready"), i + 1)
                    for k in range(DK):
                        ins = nc.tensor.matmul(psum[k // 2][:, (k % 2) * T:(k % 2) * T + T],
                                               yexp[:, k * P:k * P + P], put, start=False, stop=False,
                                               skip_group_check=True)
                    return ins

                gather(0, 0)
                gate_up(0, 0)
                with pe.Fori(0, count // 2 - 1) as i:
                    turn(i)
                turn(count // 2 - 1, last=True).then_inc(S(f"moe{m} summed"), 1)
                pe.wait_ge(S(f"moe{m} summed"), 1)

                pe.wait_ge(S(f"moe{m} flag ready"), 1)
                crowded = pe.value_load(flag[0:1, 0:1], min_val=0, max_val=TT * P * 2)
                with pe.If(crowded > 0):
                    pe.sem_inc(S(f"over{m} used"), 1)
                    with pe.Fori(0, count) as e:
                        pe.wait_ge(S(f"over{m} diagonal"), e + 1)
                        for t in range(TT):
                            ins = mm(psum[6][:, t * P:t * P + P], ones[:, :], odiag[:, t, :], True, True)
                        ins.then_inc(S(f"over{m} weights spread"), 1)
                        for f in range(4):
                            pe.wait_ge(S(f"over{m} landed"), e * 192 + 48 * (f + 1))
                            pe.wait_ge(S(f"over{m} hidden"), e * 4 + f + 1)
                            for half, w in enumerate((ogate, oup)):
                                for k in range(DK):
                                    ins = mm(psum[4][:, half * T:half * T + T], w[:, k, :], H[:, k, :],
                                             k == 0, k == DK - 1)
                            ins.then_inc(S(f"over{m} product"), 1)
                            pe.wait_ge(S(f"over{m} hidden"), e * 4 + f + 2)
                            for k in range(DK):
                                ins = nc.tensor.matmul(psum[k // 2][:, (k % 2) * T:(k % 2) * T + T],
                                                       odown[:, k * P:k * P + P], ohid, start=False, stop=False,
                                                       skip_group_check=True)
                            ins.then_inc(S(f"over{m} used"), 1)
                    pe.wait_ge(S(f"over{m} used"), 4 * count + 1)
                for b in range(BANKS):
                    pe.sem_inc(filled[b], 1)

            router(0, 4)
            turn_h(1)
            ada(2, 4)
            ada(2, 5)
            ranks(1, E1)
            experts_pe(1, N1, E1)
            norm("nf")
            norm("m1")

            pe.wait_ge(S("h3 ready"), DK)
            pe.wait_ge(S("ctx ready"), DK)
            pe.wait_ge(S("late pack loaded"), 32)
            key = ("win2", 0)
            w = slab(key, 8, 512)
            arrived(key)
            proj("kT01", w, 0, H, 2)
            proj("kT23", w, 2 * P, H, 2)
            by_token("kc0", w, 0, 512, HC, 0, bias=brow[:, 0:512])
            by_token("kc1", w, 0, 512, HC, 1, free=key, bias=brow[:, 0:512])
            for half in range(2):
                key = ("win2", 1 + half)
                w = slab(key, 8, 512)
                arrived(key)
                bias = brow[:, 512 + 512 * half:1024 + 512 * half]
                for what, src in (("vx", H), ("vc", HC)):
                    for tt in range(TT):
                        last = what == "vc" and tt == 1
                        by_token(f"{what}{half}{tt}", w, 0, 512, src, tt, free=key if last else None, bias=bias)
            pe.wait_ge(S("ctx keys ready"), 4)
            wait_taken(pe, "vc11")
            for h in range(RH):
                b = begin(f"st{h}")
                for way in range(2):
                    for tt in range(TT):
                        ins = mm(b[:, way * RDV:way * RDV + RDV], kdec[:, h, way, tt, :],
                                 VC[:, tt, h * RDV:h * RDV + RDV], tt == 0, tt == TT - 1)
                end(ins, f"st{h}")

            def swap(name, raw, h):
                b = begin(name)
                for t in range(2):
                    ins = mm(b[:, t * T:t * T + T], perm, raw[:, h + t, :], True, True)
                end(ins, name)

            wait_taken(pe, "kT23")
            swap("rk01", kraw, 0)
            swap("rk23", kraw, 2)
            key = ("win2", 3)
            w = slab(key, 8, 512)
            arrived(key)
            proj("q2_01", w, 0, H, 2)
            proj("q2_23", w, 2 * P, H, 2, free=key)
            wait_taken(pe, "q2_23")
            swap("rq01", qraw, 0)
            swap("rq23", qraw, 2)
            for j in range(2):
                key = ("win2", 4 + j)
                w = slab(key, 8, 512)
                arrived(key)
                proj(f"g{4 * j}{4 * j + 1}", w, 0, H, 2)
                proj(f"g{4 * j + 2}{4 * j + 3}", w, 2 * P, H, 2, free=key)
            pe.wait_ge(S("rotated"), 4)
            for h in range(RH):
                b = begin(f"s{h}")
                for jt in range(TT):
                    ins = mm(b[:, jt * T:jt * T + T], kr[:, h, jt * P:jt * P + P], qr[:, h, :], True, True)
                end(ins, f"s{h}")

            def attend(h):
                wait_taken(pe, f"s{h}")
                b = begin(f"o{h}")
                for vt in range(2):
                    o = b[:, vt * T:vt * T + T]
                    e = vt * P
                    for jt in range(TT):
                        mm(o, V[:, jt, h * RDV + e:h * RDV + e + P], Pm[h % 2][:, jt, :], jt == 0, False)
                    mm(o, S0[:, h, 0, e:e + P], qf[:, h % 2, :], False, False)
                    ins = mm(o, S0[:, h, 1, e:e + P], qb[:, h % 2, :], False, True)
                end(ins, f"o{h}")

            def readout_sum(h):
                ss(f"rs{h}", [osq[:, t, :] for t in range(2)], "readout squared", h, 2)

            wait_taken(pe, "st3")
            attend(0)
            attend(1)
            readout_sum(0)
            attend(2)
            readout_sum(1)
            attend(3)
            readout_sum(2)
            readout_sum(3)
            for j in range(3):
                key = ("win2", 6 + j)
                w = slab(key, 8, 512)
                arrived(key)
                proj(f"hy{4 * j}", w, 0, H, 2)
                proj(f"hy{4 * j + 2}", w, 2 * P, H, 2, free=key)
            for g, j0 in (("gr", 9), ("gh", 11)):
                for j in range(2):
                    key = ("win2", j0 + j)
                    w = slab(key, 8, 512)
                    arrived(key)
                    proj(f"{g}{4 * j}", w, 0, H, 2)
                    proj(f"{g}{4 * j + 2}", w, 2 * P, H, 2, free=key)
            pe.wait_ge(S("z ready"), HYT)
            for tt in range(TT):
                b = begin(f"zt{tt}")
                for c in range(HYT):
                    ins = nc.tensor.transpose(b[:, c * P:c * P + P], zT[:, c, tt * P:tt * P + P], ident)
                end(ins, f"zt{tt}")
            for tt in range(TT):
                wait_taken(pe, f"zt{tt}")
            for kt in range(2):
                for ri, n in enumerate((f"zr{kt}", f"zi{kt}")):
                    b = begin(n)
                    for tt in range(TT):
                        ins = mm(b[:, :], mcs[:, ri, tt, kt * P:kt * P + P], ztok[:, tt, :], tt == 0, tt == TT - 1)
                    end(ins, n)
            pe.wait_ge(S("spectrum ready"), 2)
            for c in range(HYT):
                if c % 2 == 0:
                    b = begin(f"yt{c}")
                for n in range(4):
                    ri, kt = n // 2, n % 2
                    ins = mm(b[:, (c % 2) * T:(c % 2) * T + T], Y[:, ri, kt, c * P:c * P + P], mcs[:, ri, kt, :],
                             n == 0, n == 3)
                if c % 2:
                    end(ins, f"yt{c - 1}")
            pe.wait_ge(S("readout ready"), RH)
            for j in range(2):
                key = ("ret_o", j)
                w = slab(key, 8, 512)
                arrived(key)
                proj(f"ro{4 * j}", w, 0, sg, 2)
                proj(f"ro{4 * j + 2}", w, 2 * P, sg, 2, free=key)
            pe.wait_ge(S("hyena ready"), 2)
            key = ("hy_o", 0)
            w = slab(key, 4, 1024)
            arrived(key)
            for j in range(4):
                proj(f"ho{2 * j}", w, 2 * P * j, hyo, 2, nk=HYT, free=key if j == 3 else None)
            pe.wait_ge(S("merged"), 4)
            for j in range(2):
                key = ("wout2", j)
                w = slab(key, 8, 512)
                arrived(key)
                proj(f"w2_{4 * j}", w, 0, H, 2)
                proj(f"w2_{4 * j + 2}", w, 2 * P, H, 2, free=key)
            norm("m2")
            router(1, 8)
            turn_h(2)
            ranks(2, E2)
            experts_pe(2, N3, E2)
            norm("mf")


_WHOLE = ["w_ada", "w_in", "w_out", "w_gate", "w_up", "w_down", "ada_w_2", "w_in_2", "ret_w_o_2", "hy_w_o_2",
          "w_out_2", "expert_w1_2", "expert_w3_2", "expert_w2_2"]


def packs(i):
    f = np.float32

    def cols_of(v, n):
        return np.ascontiguousarray(np.asarray(v).reshape(n, P).T)

    def padded(v, rows=P):
        v = np.asarray(v)
        out = np.zeros((rows,) + v.shape[1:], f)
        out[:v.shape[0]] = v
        return out

    def taps(w, tiles):
        k = w.shape[0]
        return w.reshape(k, tiles, P).transpose(2, 1, 0).reshape(P, tiles * k)

    def spread(v):
        return np.broadcast_to(np.asarray(v).reshape(1, -1), (P, np.asarray(v).size))

    p = np.arange(P)
    t = np.arange(T)
    c = np.zeros((P, NCOL), f)

    def put(name, v):
        c[:, AT[name]:AT[name] + v.shape[1]] = v

    put("c", cols_of(i["c"], 8))
    both = np.stack([i["c_2"].reshape(8, P), i["c_ctx_2"].reshape(8, P)], 1)
    put("c2", both.reshape(16, P).T)
    put("b_ada", cols_of(i["b_ada"], 48))
    put("b_ada2", cols_of(i["ada_b_2"], 48))
    put("g_mix", cols_of(i["g_mix"], 8))
    put("conv_w", taps(i["conv_dw_w"][0], CT))
    put("conv_b", cols_of(i["conv_dw_b"], 2))
    put("ln_g", cols_of(i["conv_ln_g"], 2))
    put("ln_b", cols_of(i["conv_ln_b"], 2))
    put("lru_w", taps(i["lru_conv_w"][0], LT))
    for name, key in (("lru_b", "lru_conv_b"), ("lru_ba", "lru_b_a"), ("lru_bi", "lru_b_i"), ("lam", "lru_lam")):
        put(name, cols_of(i[key], 3))
    put("gla_b", padded(i["gla_b_gate"][0].reshape(2, PAIR).T))
    put("gla_g", padded(i["gla_norm_g"][0].reshape(GH, GDV).T))
    for name, key in (("g_ffn", "g_ffn"), ("g_final", "g_final"), ("g1", "norm1_g_2"), ("g2", "norm2_g_2"),
                      ("g_out", "final_norm_g_2")):
        put(name, cols_of(i[key], 8))
    put("b_in", cols_of(i["b_in_2"], 52))
    put("decay", spread(i["ret_decay_logit_2"][0]))
    put("hy_w", taps(i["hy_conv_w_2"][0], 12))
    put("hy_b", cols_of(i["hy_conv_b_2"], 12))
    for name, key in (("f_b1", "hy_ffn_b1_2"), ("f_freq", "hy_ffn_freq_2"), ("f_b2", "hy_ffn_b2_2")):
        put(name, padded(i[key].reshape(64, 1)))
    put("skip", cols_of(i["hy_skip_2"], 4))
    put("br1", spread(np.concatenate([i["b_route_group"].reshape(-1), i["b_route_expert"].reshape(-1)])))
    put("br2", spread(np.concatenate([i["router_group_b_2"].reshape(-1), i["router_expert_b_2"].reshape(-1)])))
    times = (np.arange(T, dtype=f) / T).astype(f)
    put("neg_t", -times.reshape(TT, P).T)
    pos = (p[:, None] + P * np.arange(TT)[None, :]).astype(f)
    put("pos", pos)
    put("rpos", T - 1 - pos)
    put("pos1", pos + 1)
    put("tie4", spread(np.arange(4, 0, -1).astype(f)))
    put("tie8", spread(np.arange(8, 0, -1).astype(f)))
    rows = np.arange(P)[:, None]
    put("head", (((rows // GDK == 0) | (rows // GDK == 1)) * (rows // GDK == np.arange(2)[None, :])
                 * float(GDK) ** -0.5).astype(f))
    put("eps", np.full((P, 1), EPS, f))

    def by_feature(x):
        return np.ascontiguousarray(x.reshape(T, DK, P).transpose(2, 1, 0))

    bands = np.linspace(1e-4, 15, 16, dtype=f)
    phase = (f(2.0 * np.pi) * times[:, None] * bands[None, :]).astype(f)
    feats = np.concatenate([times[:, None], np.cos(phase), -np.sin(phase)], -1).astype(f)
    slow, fast = abs(np.log(1e-2)) / 1.5, abs(np.log(1e-2)) / 0.3
    deltas = np.linspace(slow, fast, HYW, dtype=f)

    def tiles(m):
        return m.reshape(TT, P, T).transpose(1, 0, 2)

    w_tau = np.pi * np.outer(t, t + 0.5) / T
    w_mid = np.pi * np.outer(t + 0.5, t + 0.5) / T
    basis = np.stack([tiles(np.cos(w_tau)), tiles(-np.sin(w_tau))], 1).astype(f)
    mcs = np.stack([tiles(np.cos(w_mid)), tiles(-np.sin(w_mid))], 1).astype(f)
    fpack = np.zeros((P, 12 * T), f)
    fpack[:33, 0:T] = feats.T
    fpack[:33, T:T + 64] = i["hy_ffn_w1_2"][0]
    fpack[:64, T + 64:T + 128] = i["hy_ffn_w2_2"][0]
    fpack[:, 2 * T:4 * T] = deltas[None, :]
    fpack[:, 4 * T:8 * T] = basis.reshape(P, -1)
    fpack[:64, 8 * T:12 * T] = i["hy_ffn_w3_2"][0]

    mpack = np.zeros((P, 1408), f)
    lw = mpack[:, 0:768].reshape(P, 2, LT, P)
    for g, key in enumerate(("lru_w_a", "lru_w_i")):
        for b in range(6):
            s = slice(64 * (b % 2), 64 * (b % 2) + 64)
            lw[s, g, b // 2, s] = i[key][0, b]
    j, q = p[:, None], p[None, :]
    mpack[:, 768:896] = (j <= q) & (j // GCH == q // GCH)
    mpack[:, 896:1152] = (t % GCH != 0)[None, :]
    mpack[:16, 1152:1344] = i["gla_w_gate"][0]

    inv = (f(10000.0) ** (-np.arange(32, dtype=f) / f(32))).astype(f)
    ang = np.zeros((P, T), f)
    for blk in range(4):
        where = (t // 64 if blk < 2 else t % 64).astype(f)
        ang[32 * blk:32 * blk + 32] = (inv[:, None] * where[None, :]).astype(f)
    sign = np.where((p // 32) % 2 == 0, -1.0, 1.0)[:, None]
    perm = np.zeros((P, P), f)
    perm[p ^ 32, p] = 1.0
    lpack = np.concatenate([mcs.reshape(P, -1), np.cos(ang), sign * np.sin(ang), perm,
                            np.broadcast_to(t[None, :] + 1, (P, T))], 1).astype(f)

    marks = np.concatenate([np.eye(P), p[:, None] < p[None, :], np.broadcast_to(np.arange(CAP), (P, CAP))],
                           1).astype(f)

    def router(g, e):
        w = np.concatenate([g, e], 1)
        return w.reshape(DK, P, -1).transpose(1, 0, 2).reshape(P, -1)

    e1 = i["w_route_expert"][0].transpose(1, 0, 2).reshape(D, 16)
    wr = np.concatenate([router(i["w_route_group"][0], e1),
                         router(i["router_group_w_2"][0], i["router_expert_w_2"][0])], 1)
    return {"cols": c, "xT": by_feature(i["x"][0]), "ctxT": by_feature(i["ctx_2"][0]), "fpack": fpack,
            "mpack": mpack, "lpack": lpack, "wr": np.ascontiguousarray(wr), "marks": marks,
            "brow": np.ascontiguousarray(i["b_in_2"][:, 512:2048])}


def kernel(**inputs):
    import concourse.bacc as bacc
    from concourse.bass_utils import run_bass_kernel_spmd

    i = {k: np.asarray(v) for k, v in inputs.items()}
    nc = bacc.Bacc("TRN2", target_bir_lowering=False, num_devices=1)
    arrays = packs(i)
    for name in _WHOLE:
        v = i[name]
        v = v.reshape((-1,) + v.shape[-2:])
        arrays[name] = np.ascontiguousarray(v[0] if v.shape[0] == 1 else v)
    aps = {name: nc.dram_tensor(f"in_{name}", v.shape, F32, kind="ExternalInput").ap() for name, v in arrays.items()}
    out = nc.dram_tensor("out_y", [P, DK, T], F32, kind="ExternalOutput").ap()
    build(nc, aps, out)
    r = run_bass_kernel_spmd(nc, [{f"in_{name}": v for name, v in arrays.items()}], core_ids=[0])
    y = r.results[0]["out_y"]
    return np.ascontiguousarray(y.transpose(2, 1, 0)).reshape(1, T, D)
```

```python
from contextlib import ExitStack

import concourse.bass as bass
import numpy as np
from concourse import mybir

F32 = mybir.dt.float32
ALU = mybir.AluOpType
ACT = mybir.ActivationFunctionType
AX = mybir.AxisListType

P = 128
T = 256
TT = T // P
D = 1024
DK = D // P
EPS = 1e-6

CONV_W, CONV_K = 256, 31
LRU_W, LRU_K = 384, 4
GH, GDK, GDV, GCH = 4, 48, 96, 64
PAIR = 2 * GDK
CT, LT = CONV_W // P, LRU_W // P

RH, RDK, RDV = 4, 128, 256
HYW = 512
HYT = HYW // P

SLOTS = 6
SLAB = 4096
BANKS = 8
CAP = 64

WIN_CUTS = [(0, 512), (512, 896), (896, 1280), (1280, 1664), (1664, 2064), (2064, 2448)]
WOUT_CUTS = [(0, 384), (384, 768), (768, 1024)]
WIN2_ORDER = [512, 1024, 1536, 0, 2048, 2560, 3072, 3584, 4096, 4608, 5120, 5632, 6144]

COLS = [("c", 8), ("c2", 16), ("b_ada", 48), ("b_ada2", 48), ("g_mix", 8), ("conv_w", 62), ("conv_b", 2), ("ln_g", 2),
        ("ln_b", 2), ("lru_w", 12), ("lru_b", 3), ("lru_ba", 3), ("lru_bi", 3), ("lam", 3), ("gla_b", 2), ("gla_g", 4),
        ("g_ffn", 8), ("g_final", 8), ("g1", 8), ("g2", 8), ("b_in", 52), ("decay", 8), ("hy_w", 36), ("hy_b", 12),
        ("f_b1", 1), ("f_freq", 1), ("f_b2", 1), ("skip", 4), ("g_out", 8), ("br1", 20), ("br2", 36),
        ("eps", 1), ("head", 2), ("neg_t", 2), ("pos", 2), ("rpos", 2), ("pos1", 2), ("tie4", 4), ("tie8", 8), ("sel", 3)]
AT, n_ = {}, 0
for name_, w_ in COLS:
    AT[name_] = n_
    n_ += w_
NCOL = n_


def stream_plan():
    ada1 = [("ada1", j) for j in range(12)]
    ada2 = [("ada2", j) for j in range(12)]
    win2 = [("win2", j) for j in range(13)]
    first = (ada1[0:4] + [("win", j) for j in range(6)] + ada1[4:12] + [("wout", j) for j in range(3)] + ada2[4:6])
    second = (ada2[0:4] + ada2[6:8] + win2 + ada2[8:10]
              + [("ret_o", 0), ("ret_o", 1), ("hy_o", 0), ("wout2", 0), ("wout2", 1)] + ada2[10:12])
    return first, second


def bank_plan():
    names = ["n1_ss", "a1_0", "a1_1", "cvg", "cvv", "f1", "lrx01", "f2", "lrx2", "f3_00", "f3_01", "f3_10", "f3_11",
             "lry01", "lry2", "f4_0", "f4_1", "q01", "k01", "f5_0", "f5_1", "f5_2", "f5_3", "v0", "v1", "glr", "lgp", "mu",
             "og01", "var", "og23", "lru0", "lru1", "lru2", "k2t", "sc01", "sc23", "a1_2", "kv0", "kv1", "kv2",
             "a1_3", "o01", "o23", "os01", "os23", "a1_4", "a1_5",
             "wo01", "wo23", "wo45", "wo67", "n2_ss", "a2_2", "rt1", "ht1_0", "ht1_1", "ht1_2", "ht1_3",
             "rk1", "fl1"]
    names += [f"moe1_{b}" for b in range(BANKS)]
    names += ["a2_0", "nf_ss", "a2_1", "m1_ss", "a2_3"]
    names += ["kT01", "nc_ss", "kT23", "kc0", "kc1", "vx00", "vx01", "vc00", "vc01", "vx10", "vx11", "vc10", "vc11",
              "q2_01", "q2_23", "rk01", "rk23", "st0", "st1", "st2", "st3", "rq01", "rq23",
              "g01", "g23", "s0", "s1", "g45", "g67", "o0", "hy0", "hy2", "s2", "o1", "rs0", "hy4", "hy6", "s3", "o2",
             "rs1", "hy8", "hy10", "o3", "rs2", "rs3"]
    names += [f"gr{2 * j}" for j in range(4)] + [f"gh{2 * j}" for j in range(4)]
    names += ["a2_4", "zt0", "zt1", "zr0", "zi0", "zr1", "zi1"] + [f"ro{2 * j}" for j in range(4)]
    names += ["yt0", "yt2"] + [f"ho{2 * j}" for j in range(4)] + [f"w2_{2 * j}" for j in range(4)]
    names += ["m2_ss", "a2_5", "rt2", "ht2_0", "ht2_1", "ht2_2", "ht2_3", "rk2", "fl2"] + [f"moe2_{b}" for b in range(BANKS)] + ["mf_ss"]
    names = [x for n in names for x in
             ([f"r{n[1]}_{2 * int(n[3])}", f"r{n[1]}_{2 * int(n[3]) + 1}", n] if n[:3] in ("a1_", "a2_") else [n])]
    place = {}
    used = [0] * BANKS
    at = 0
    for n in names:
        b = int(n[-1]) if n.startswith("moe") else at % BANKS
        at += not n.startswith("moe")
        place[n] = (b, used[b])
        used[b] += 1
    return place


def build(nc, a, out):
    first, second = stream_plan()
    place = bank_plan()
    N1 = len(first)
    E1, E2 = 16, 32
    N2 = N1 + 3 * E1
    N3 = N2 + len(second)
    slab_no = {key: n for n, key in enumerate(first)}
    slab_no.update({key: N2 + n for n, key in enumerate(second)})

    with ExitStack() as ctx:
        def sb(name, shape):
            return ctx.enter_context(nc.sbuf_tensor(name, shape, F32))

        sems = {}

        def S(name):
            if name not in sems:
                sems[name] = ctx.enter_context(nc.semaphore(name.replace(" ", "_")))
            return sems[name]

        psum = [ctx.enter_context(nc.psum_tensor(f"bank{b}", [P, 512], F32)) for b in range(BANKS)]
        filled = [S(f"filled{b}") for b in range(BANKS)]
        drained = [S(f"drained{b}") for b in range(BANKS)]
        landed = [S(f"landed{s}") for s in range(SLOTS)]
        freed = [S(f"freed{s}") for s in range(SLOTS)]

        ring = sb("ring", [P, SLOTS, SLAB])
        cols = sb("cols_sb", [P, NCOL])
        X = sb("X", [P, DK, T])
        H = sb("H", [P, DK, T])
        W = sb("W", [P, DK, T])
        HF = sb("HF", [P, 2, 2, HYW])
        marks = sb("marks", [P, 2 * P + CAP])
        ident = marks[:, 0:P]
        before = marks[:, P:2 * P]
        places = marks[:, 2 * P:2 * P + CAP]
        ones = sb("ones", [P, P])
        wr = sb("wr", [P, DK * 20 + DK * 36])
        root = sb("root", [P, T])
        rstd = sb("rstd", [P, T])
        mod1 = sb("mod1", [P, 48])
        mod2 = sb("mod2", [P, 48, 2])
        gs = sb("gs", [P, 5, DK])
        cact = sb("cact", [P, DK, 32])
        lgs = sb("lgs", [P, 5, 8])
        sml = sb("sml", [P, 24])
        lru_scale = sb("lru_scale", [P, 2, LT])
        gdec = sb("gdec", [PAIR, 2, 4])
        ctxdec = sb("ctxdec", [P, 2, RH, TT])
        backb = sb("backb", [P, RH])
        route = sb("route", [P, 280])
        comb = sb("comb", [P, TT, 32])
        rank = sb("rank", [P, TT, 32])
        over = sb("over", [P, TT, 32])
        n_over = sb("n_over", [P, 2])
        flag = ctx.enter_context(nc.sbuf_tensor("flag", [P, 1], mybir.dt.int32))
        pool = sb("pool", [P, 68 * T + T // 2])

        def view(tile, *shape, rows=P):
            n = int(np.prod(shape))
            v = pool[0:rows, int(tile * T):int(tile * T) + n]
            if len(shape) == 1:
                return v
            names = "abcd"[:len(shape)]
            return v.rearrange(f"p ({' '.join(names)}) -> p {' '.join(names)}",
                               **{k: s for k, s in zip(names[1:], shape[1:])})

        def col(name, i=0, n=1, rows=slice(0, P)):
            return cols[rows, AT[name] + i:AT[name] + i + n]

        upad = view(0, CT, CONV_K - 1 + T)
        u2 = view(3, CT, T)
        lxpad = view(5, LT, LRU_K - 1 + T)
        xc = view(9, LT, T)
        rg = view(12, LT, T)
        ig = view(15, LT, T)
        ag = view(18, LT, T)
        gy = view(21, LT, T)
        cvsg = W[:, 6:8, :]
        qT = view(24, 2, T, rows=PAIR)
        kT1 = view(26, 2, T, rows=PAIR)
        vtok = view(28, TT, GH * GDV)
        glr = view(31, T, rows=16)
        lgx = view(32, 2, T, rows=PAIR)
        bcum = view(34, 2, T, rows=PAIR)
        diff = view(36, 2, T, rows=PAIR)
        eb = view(38, 2, T, rows=PAIR)
        lruw = view(40, 2, LT, P)
        gmask = view(43, P)
        segm = view(43.5, T, rows=PAIR)
        glaw = view(44.5, 2, PAIR, rows=16)
        qz = view(46, GH, T, rows=PAIR)
        kin = view(50, 2, T, rows=PAIR)
        k2z = view(52, TT, 2, 2, PAIR)
        sm = view(56, GH, TT, P)
        states = view(60, 3, 2, 2 * GDV, rows=PAIR)
        sog = view(64.5, GH, T)
        feats = view(12, T, rows=33)
        fw1 = view(13, 64, rows=33)
        fw2 = view(13.25, 64, rows=64)
        deltas = view(14, HYW)
        basis = view(16, 2, TT, T)
        fw3 = view(20, 1024, rows=64)
        arg = view(24, T, rows=64)
        rnd = view(25, T, rows=64)
        hid1 = view(26, T, rows=64)
        hid2 = view(27, T, rows=64)
        filt = view(46, TT, 2, HYW)
        absf = view(54, TT, 2, HYW)
        decay = view(62, TT, HYW)
        htok = view(8, TT, D)
        hexp = view(16, 2, DK, CAP)
        pick = view(20, 2, TT, CAP)
        pickw = view(21, TT, 2 * CAP)
        put = view(22, T)
        sact = view(23, 512)
        hidt = view(25, 512)
        yexp = view(30, D)
        hid = view(34, 4, CAP)
        ogate, oup, odown = view(35, DK, P), view(39, DK, P), view(45, D)
        ohid, oact, oweigh = view(49, T), view(50, T), view(51, T)
        odiag = view(52, TT, P)
        HC = view(0, DK, T)
        sigR = view(0, DK, T)
        VC = view(8, TT, 1024)
        sigH = view(8, DK, T)
        Ef, Eb = view(8, T), view(9, T)
        qf, qb = view(10, 2, T), view(12, 2, T)
        S0 = view(16, RH, 2, RDV)
        x0 = view(16, HYT, T)
        zT = view(20, HYT, T)
        brow = view(45, 1536)
        kdec = view(24, RH, 2, TT, P)
        sg = view(24, DK, T)
        hypad = view(32, 12, T + 2)
        kr = view(45, RH, T)
        qr = view(49, RH, T)
        hyo = view(45, HYT, T)
        cv1, cv2 = view(49, T), view(50, T)
        V = view(53, TT, 1024)
        ztok = view(53, TT, HYW)
        ztmp = view(57, TT, HYW)
        mcs = view(61, 2, TT, T)
        rope = view(65, 2, T)
        perm = view(67, P)
        irow = view(67.5, T)
        W4 = W[:, 0:4, :]
        kraw, qraw = W[:, 0:4, :], W[:, 4:8, :]
        KC = W[:, 4:8, :].rearrange("p (t a) b -> p t (a b)", t=TT)
        Dm = W[:, 0:2, :]
        Pm = [W[:, 2:4, :], W[:, 4:6, :]]
        osq = W[:, 6:8, :]
        Y = W[:, :, :].rearrange("p (r t a) b -> p r t (a b)", r=2, t=TT)

        zeros = view(59, 512)
        dtmp, rtmp = view(0, 2, T), view(2, 2, T)
        gla_root = view(56, GH, T, rows=GDV)
        X1 = ["wo01", "wo23", "wo45", "wo67"]
        X4 = ["w2_0", "w2_2", "w2_4", "w2_6"]
        NORM = {key: n for n, key in enumerate(["n1", "n2", "nf", "m1", "nc", "m2", "mf"])}
        rv = {"gexp": route[:, 80:88].rearrange("p (t g) -> p t g", t=TT), "pexp": route[:, 256:258]}

        def lru_neg(t):
            return lru_scale[:, 0, t:t + 1]

        def lru_pos(t):
            return lru_scale[:, 1, t:t + 1]

        def bank(name):
            return psum[place[name][0]]

        def wait_product(eng, name):
            b, use = place[name]
            eng.wait_ge(filled[b], use + 1)

        def gone(name):
            return drained[place[name][0]]

        def wait_taken(eng, name):
            b, use = place[name]
            eng.wait_ge(drained[b], use + 1)

        def wait_slab(eng, n):
            eng.wait_ge(landed[n % SLOTS], 32 * (n // SLOTS + 1))

        def used_up(eng, i, j, n0):
            n = n0 + 2 + j
            eng.wait_ge(freed[n % SLOTS], i + n // SLOTS + 1)

        def up_slab(e):
            return 3 * e - 2 if e else -1

        def slab(key, k, w, base=0):
            s = slab_no[key] % SLOTS
            return ring[:, s, base:base + k * w].rearrange("p (k w) -> p k w", k=k)

        def bc(ap, shape):
            return ap.broadcast_to(shape)

        block = ctx.enter_context(nc.Block())

        def experts(sp, m, w_gate, w_up, w_down, n0, count):
            by_expert = [w.rearrange("e (k p) f -> e p k f", p=P) for w in (w_gate, w_up, w_down)]

            def one(n, kind, which, turns=None):
                w = by_expert[kind]
                k = w.shape[2]
                s = n % SLOTS
                src = w[which].rearrange("o p k f -> p (o k) f")
                dst = ring[:, s, :].rearrange("p (k w) -> p k w", k=k)
                if turns is None:
                    sp.wait_ge(freed[s], n // SLOTS)
                else:
                    sp.wait_ge(freed[s], turns + n // SLOTS)
                sp.dma_start(dst[:, 0:k // 2], src[:, 0:k // 2]).then_inc(landed[s], 16)
                sp.dma_start(dst[:, k // 2:k], src[:, k // 2:k]).then_inc(landed[s], 16)

            one(n0, 0, slice(0, 1))
            one(n0 + 1, 1, slice(0, 1))
            with sp.Fori(0, count // 2 - 1) as i:
                for j in range(6):
                    one(n0 + 2 + j, j % 3, bass.ds(i * 2 + (j // 3 + (j % 3 < 2)), 1), i)
            for j, (kind, e) in enumerate([(0, count - 1), (1, count - 1), (2, count - 2), (2, count - 1)]):
                one(n0 + 3 * count - 4 + j, kind, slice(e, e + 1))
            sp.wait_ge(S(f"moe{m} flag ready"), 1)
            crowded = sp.value_load(flag[0:1, 0:1], min_val=0, max_val=TT * P * 2)
            with sp.If(crowded > 0):
                with sp.Fori(0, count) as e:
                    g, u, d = (w[bass.ds(e, 1)].rearrange("o p k f -> p (o k) f") for w in by_expert)
                    for f in range(4):
                        c = slice(f * P, f * P + P)
                        sp.wait_ge(S(f"over{m} used"), e * 4 + f + 1)
                        sp.dma_start(ogate, g[:, :, c]).then_inc(S(f"over{m} landed"), 16)
                        sp.dma_start(oup, u[:, :, c]).then_inc(S(f"over{m} landed"), 16)
                        sp.dma_start(odown, d[:, f, :]).then_inc(S(f"over{m} landed"), 16)

        @block.sync
        def _(sp):
            def load(n, halves):
                s = n % SLOTS
                if n >= SLOTS:
                    sp.wait_ge(freed[s], n // SLOTS)
                for dst, src in halves:
                    sp.dma_start(dst, src).then_inc(landed[s], 16)

            def columns(n, w, c0, c1):
                v = w.rearrange("(k p) f -> p k f", p=P)[:, :, c0:c1]
                d = ring[:, n % SLOTS, 0:8 * (c1 - c0)].rearrange("p (k w) -> p k w", k=8)
                load(n, [(d[:, 0:4], v[:, 0:4]), (d[:, 4:8], v[:, 4:8])])

            for key in first + second:
                n = slab_no[key]
                kind, j = key
                if n == N2:
                    experts(sp, 1, a["w_gate"], a["w_up"], a["w_down"], N1, E1)
                if kind == "ada1":
                    columns(n, a["w_ada"], 512 * j, 512 * j + 512)
                elif kind == "ada2":
                    columns(n, a["ada_w_2"], 512 * j, 512 * j + 512)
                elif kind == "win":
                    columns(n, a["w_in"], *WIN_CUTS[j])
                elif kind == "wout":
                    c0, c1 = WOUT_CUTS[j]
                    w = c1 - c0
                    top = a["w_out"][0:640, c0:c1].rearrange("(k p) f -> p k f", p=P)
                    low = a["w_out"][640:1024, c0:c1].rearrange("(k p) f -> p k f", p=GDV)
                    load(n, [(ring[:, n % SLOTS, 0:5 * w].rearrange("p (k w) -> p k w", k=5), top),
                             (ring[0:GDV, n % SLOTS, 5 * w:9 * w].rearrange("p (k w) -> p k w", k=4), low)])
                elif kind == "win2":
                    columns(n, a["w_in_2"], WIN2_ORDER[j], WIN2_ORDER[j] + 512)
                elif kind == "ret_o":
                    columns(n, a["ret_w_o_2"], 512 * j, 512 * j + 512)
                elif kind == "wout2":
                    columns(n, a["w_out_2"], 512 * j, 512 * j + 512)
                elif kind == "hy_o":
                    v = a["hy_w_o_2"].rearrange("(k p) f -> p k f", p=P)
                    d = ring[:, n % SLOTS, :].rearrange("p (k w) -> p k w", k=4)
                    load(n, [(d[:, 0:2], v[:, 0:2]), (d[:, 2:4], v[:, 2:4])])
            experts(sp, 2, a["expert_w1_2"], a["expert_w3_2"], a["expert_w2_2"], N3, E2)

        @block.gpsimd
        def _(pool_e):
            pool_e.memset(ones[:, :], 1.0).then_inc(S("ones set"), 1)
            pool_e.memset(cact[:, :, :], 0.0).then_inc(S("c zero"), 1)
            pool_e.memset(upad[:, :, 0:CONV_K - 1], 0.0)
            pool_e.memset(lxpad[:, :, 0:LRU_K - 1], 0.0).then_inc(S("pads zero"), 1)
            for n in range(4):
                wait_taken(pool_e, f"f5_{n}")
            pool_e.memset(k2z[:, :, :, :, :], 0.0).then_inc(S("heads zero"), 1)
            wait_taken(pool_e, "m1_ss")
            pool_e.memset(hypad[:, :, 0:1], 0.0)
            pool_e.memset(hypad[:, :, T + 1:T + 2], 0.0).then_inc(S("hyena pads zero"), 1)

        def readout_act(act, h):
            wait_product(act, f"o{h}")
            nc.scalar.activation(osq, bank(f"o{h}")[:, :].rearrange("p (a b) -> p a b", a=2),
                                 ACT.Square).then_inc(S("readout squared"), 1)
            wait_product(act, f"rs{h}")
            if h:
                act.wait_ge(S("readout ready"), h)
            nc.scalar.activation(root[:, :], bank(f"rs{h}")[:, 0:T], ACT.Sqrt, scale=1.0 / RDV,
                                 bias=col("eps")).then_inc(gone(f"rs{h}"), 1)

        @block.scalar
        def _(act):
            steps = [0]

            def link(ins):
                steps[0] += 1
                ins.then_inc(S("scalar step"), 1)
                act.wait_ge(S("scalar step"), steps[0])

            def rows(which, *parts):
                for j in [2 * p + h for p in parts for h in (0, 1)]:
                    name = f"r{which}_{j}"
                    wait_product(act, name)
                    nc.scalar.activation(ring[:, slab_no[(f"ada{which}", j)] % SLOTS, 0:512], bank(name)[:, :],
                                         ACT.Copy).then_inc(gone(name), 1)

            def squares(key, src, after=None):
                for j in range(4):
                    if isinstance(after, str):
                        act.wait_ge(S("norm scaled"), DK * NORM[after] + 2 * j + 2)
                    elif after:
                        wait_taken(act, after[j])
                    nc.scalar.activation(W[:, 2 * j:2 * j + 2, :], src[:, 2 * j:2 * j + 2, :],
                                         ACT.Square).then_inc(S("squared"), 1)

            def norm_root(key):
                wait_product(act, key + "_ss")
                nc.scalar.activation(root[:, :], bank(key + "_ss")[:, 0:T], ACT.Sqrt, scale=1.0 / D,
                                     bias=col("eps")).then_inc(gone(key + "_ss"), 1)

            def shift(key, dst, shifts, ready):
                for k in range(DK):
                    act.wait_ge(S("norm scaled"), DK * NORM[key] + k + 1)
                    nc.scalar.activation(dst[:, k, :], dst[:, k, :], ACT.Identity,
                                         bias=shifts(k)).then_inc(S(ready), 1)

            act.dma_start(cols[:, :], a["cols"]).then_inc(S("cols loaded"), 16)
            act.dma_start(X[:, :, :], a["xT"]).then_inc(S("x loaded"), 16)

            act.wait_ge(S("cols loaded"), 16)
            act.wait_ge(S("c zero"), 1)
            nc.scalar.activation(cact[:, :, 0], col("c", 0, 8), ACT.Silu).then_inc(S("c ready"), 1)
            nc.scalar.activation(cact[:, :, 1:3], col("c2", 0, 16).rearrange("p (k n) -> p k n", k=DK),
                                 ACT.Silu).then_inc(S("c ready"), 1)
            link(nc.scalar.activation(sml[:, 0:3], col("lam", 0, 3), ACT.Abs))
            nc.scalar.activation(sml[:, 0:3], sml[:, 0:3], ACT.Exp, scale=-1.0).then_inc(S("softplus exp"), 1)
            act.wait_ge(S("softplus arg"), 1)
            nc.scalar.activation(sml[:, 6:9], sml[:, 3:6], ACT.Ln).then_inc(S("softplus log"), 1)
            act.wait_ge(S("x loaded"), 16)
            squares("n1", X)
            norm_root("n1")
            rows(1, 0)
            rows(1, 1)
            act.dma_start(view(12, 12 * T), a["fpack"]).then_inc(S("filter pack loaded"), 16)
            act.dma_start(marks[:, :], a["marks"]).then_inc(S("mixer pack loaded"), 16)
            act.dma_start(view(40, 1408), a["mpack"]).then_inc(S("mixer pack loaded"), 16)
            act.dma_start(wr[:, :], a["wr"]).then_inc(S("mixer pack loaded"), 16)
            shift("n1", H, lambda k: mod1[:, k:k + 1], "h1 ready")

            wait_product(act, "cvg")
            nc.scalar.activation(cvsg, bank("cvg")[:, :].rearrange("p (a b) -> p a b", a=2),
                                 ACT.Sigmoid).then_inc(gone("cvg"), 1)
            act.wait_ge(S("filter pack loaded"), 16)
            for tt in range(TT):
                nc.scalar.activation(decay[:, tt, :], deltas, ACT.Exp,
                                     scale=col("neg_t", tt)).then_inc(S("decay ready"), 1)

            def sine(h, dst):
                act.wait_ge(S("sine argument"), h + 1)
                nc.scalar.activation(dst, arg, ACT.Sin).then_inc(S("sine ready"), 1)

            def lru_input(n, t0, m):
                wait_product(act, n)
                nc.scalar.activation(lxpad[:, t0:t0 + m, LRU_K - 1:],
                                     bank(n)[:, 0:m * T].rearrange("p (a b) -> p a b", a=m),
                                     ACT.Copy).then_inc(gone(n), 1)

            sine(0, hid1)
            lru_input("lrx01", 0, 2)
            sine(1, hid2)
            lru_input("lrx2", 2, 1)
            for n in range(4):
                wait_taken(act, f"f3_{n // 2}{n % 2}")
                nc.scalar.activation(absf[:, n // 2, n % 2, :], filt[:, n // 2, n % 2, :],
                                     ACT.Abs).then_inc(S("filter abs"), 1)
            for n, (t0, m) in {"lry01": (0, 2), "lry2": (2, 1)}.items():
                wait_product(act, n)
                nc.scalar.activation(gy[:, t0:t0 + m, :], bank(n)[:, 0:m * T].rearrange("p (a b) -> p a b", a=m),
                                     ACT.Gelu_apprx_tanh).then_inc(gone(n), 1)
            for n, dst in (("q01", qT), ("k01", kT1)):
                wait_product(act, n)
                nc.scalar.activation(dst, bank(n)[0:PAIR, :].rearrange("p (a b) -> p a b", a=2),
                                     ACT.Copy).then_inc(gone(n), 1)
            for n in range(4):
                wait_product(act, f"f5_{n}")
                nc.scalar.activation(HF[:, n // 2, n % 2, :], bank(f"f5_{n}")[:, :], ACT.Copy,
                                     scale=1.0 / T).then_inc(gone(f"f5_{n}"), 1)
            for tt in range(TT):
                wait_product(act, f"v{tt}")
                nc.scalar.activation(vtok[:, tt, :], bank(f"v{tt}")[:, 0:GH * GDV],
                                     ACT.Copy).then_inc(gone(f"v{tt}"), 1)
            wait_product(act, "glr")
            nc.scalar.activation(glr, bank("glr")[0:16, 0:T], ACT.Copy).then_inc(gone("glr"), 1)
            wait_product(act, "lgp")
            for pr in range(2):
                ins = nc.scalar.activation(lgx[:, pr, :], bank("lgp")[0:PAIR, pr * T:pr * T + T], ACT.Identity,
                                           bias=col("gla_b", pr, rows=slice(0, PAIR)))
            ins.then_inc(gone("lgp"), 1)
            wait_taken(act, "lgp")
            lnb = W[0:PAIR, 0:2, :]
            link(nc.scalar.activation(lnb, lgx, ACT.Abs))
            link(nc.scalar.activation(lnb, lnb, ACT.Exp, scale=-1.0))
            nc.scalar.activation(lnb, lnb, ACT.Ln, bias=1.0).then_inc(S("gate log ready"), 1)
            wait_taken(act, "mu")
            nc.scalar.activation(W[:, 2:4, :], u2, ACT.Square).then_inc(S("conv squared"), 1)
            act.wait_ge(S("gate sums ready"), 2)
            nc.scalar.activation(eb, bcum, ACT.Exp, scale=1.0 / 16.0)
            nc.scalar.activation(kin, bcum, ACT.Exp, scale=-1.0 / 16.0)
            nc.scalar.activation(diff, diff, ACT.Exp, scale=1.0 / 16.0)
            nc.scalar.activation(gdec[:, :, :], bcum.rearrange("p a (c s) -> p a c s", s=GCH)[:, :, :, GCH - 1],
                                 ACT.Exp, scale=1.0 / 16.0).then_inc(S("gate powers ready"), 1)
            wait_product(act, "var")
            nc.scalar.activation(root[:, :], bank("var")[:, 0:T], ACT.Sqrt, scale=1.0 / CONV_W,
                                 bias=col("eps")).then_inc(gone("var"), 1)
            for n, h in (("og01", 0), ("og23", 2)):
                wait_product(act, n)
                nc.scalar.activation(sog[0:GDV, h:h + 2, :], bank(n)[0:GDV, :].rearrange("p (a b) -> p a b", a=2),
                                     ACT.Silu).then_inc(gone(n), 1)
            for t in range(LT):
                wait_product(act, f"lru{t}")
                nc.scalar.activation(rg[:, t, :], bank(f"lru{t}")[:, 0:T], ACT.Sigmoid, bias=col("lru_ba", t))
                nc.scalar.activation(ig[:, t, :], bank(f"lru{t}")[:, T:2 * T], ACT.Sigmoid,
                                     bias=col("lru_bi", t)).then_inc(gone(f"lru{t}"), 1)
            wait_taken(act, "lru2")
            act.wait_ge(S("softplus ready"), 1)
            for t in range(LT):
                nc.scalar.activation(ag[:, t, :], rg[:, t, :], ACT.Exp, scale=lru_neg(t))
            for t in range(LT):
                nc.scalar.activation(rg[:, t, :], rg[:, t, :], ACT.Tanh, scale=lru_pos(t)).then_inc(S("lru decay"), 1)
            act.wait_ge(S("conv scaled"), 1)
            for t in range(CT):
                nc.scalar.activation(u2[:, t, :], u2[:, t, :], ACT.Silu, scale=col("ln_g", t),
                                     bias=col("ln_b", t)).then_inc(S("mix u ready"), 1)

            rows(1, 2)
            act.wait_ge(S("lru root arg"), 1)
            nc.scalar.activation(xc, xc, ACT.Sqrt, scale=2.0).then_inc(S("lru root ready"), 1)
            rows(1, 3)
            for n, h in (("o01", 0), ("o23", 2)):
                wait_product(act, n)
                nc.scalar.activation(W[0:GDV, 4 + h:6 + h, :], bank(n)[0:GDV, :].rearrange("p (a b) -> p a b", a=2),
                                     ACT.Square).then_inc(S("gla squared"), 1)
            for n, h in (("os01", 0), ("os23", 2)):
                wait_product(act, n)
                nc.scalar.activation(gla_root[:, h:h + 2, :], bank(n)[0:GDV, :].rearrange("p (a b) -> p a b", a=2),
                                     ACT.Sqrt, scale=1.0 / GDV, bias=col("eps", rows=slice(0, GDV))).then_inc(gone(n), 1)
            rows(1, 4, 5)
            for n in X1:
                wait_taken(act, n)
            act.dma_start(HC, a["ctxT"]).then_inc(S("ctx loaded"), 16)
            act.dma_start(view(61, 1920), a["lpack"]).then_inc(S("late pack loaded"), 16)
            squares("n2", X)
            norm_root("n2")
            rows(2, 2)
            shift("n2", H, lambda k: mod1[:, 24 + k:25 + k], "h2 ready")

            def routing(m):
                act.wait_ge(S("route group arg"), m + 1)
                nc.scalar.activation(rv["gexp"], rv["gexp"], ACT.Exp).then_inc(S("route group exp"), 1)
                act.wait_ge(S("route pair arg"), m + 1)
                nc.scalar.activation(rv["pexp"], rv["pexp"], ACT.Exp).then_inc(S("route pair exp"), 1)

            def by_token_copies(m):
                for n in range(4):
                    name = f"ht{m}_{n}"
                    wait_product(act, name)
                    nc.scalar.activation(htok[:, n // 2, 512 * (n % 2):512 * (n % 2) + 512], bank(name)[:, :],
                                         ACT.Copy).then_inc(gone(name), 1)

            def experts_act(m, n0, count):
                def gathered(i, e):
                    act.wait_ge(S(f"moe{m} gathered"), i * 2 + e + 1)
                    nc.scalar.activation(hexp[:, e % 2, :, :], psum[4][:, :].rearrange("p (a b) -> p a b", a=DK),
                                         ACT.Copy).then_inc(S(f"moe{m} tokens ready"), 1)

                def silu(i, e):
                    used_up(act, i, up_slab(e), n0)
                    nc.scalar.activation(sact[CAP:P, :], psum[5][0:CAP, :],
                                         ACT.Silu).then_inc(S(f"moe{m} silu ready"), 1)

                def turn(i, last=False):
                    for e in (0, 1):
                        if not (last and e):
                            silu(i, e + 1)
                        used_up(act, i, 3 if last and e else 3 * e + 2, n0)
                        nc.scalar.activation(yexp[CAP * e:CAP * e + CAP, 0:512], psum[6][0:CAP, :],
                                             ACT.Copy).then_inc(S(f"moe{m} left half ready"), 1)
                        if not last:
                            gathered(i, e + 2)

                gathered(0, 0)
                silu(0, 0)
                gathered(0, 1)
                with act.Fori(0, count // 2 - 1) as i:
                    turn(i)
                turn(count // 2 - 1, last=True)
                act.wait_ge(S(f"moe{m} flag ready"), 1)
                crowded = act.value_load(flag[0:1, 0:1], min_val=0, max_val=TT * P * 2)
                with act.If(crowded > 0):
                    with act.Fori(0, count) as e:
                        for f in range(4):
                            act.wait_ge(S(f"over{m} product"), e * 4 + f + 1)
                            nc.scalar.activation(oact, psum[4][:, 0:T], ACT.Silu).then_inc(S(f"over{m} silu"), 1)

            by_token_copies(1)
            routing(0)
            experts_act(1, N1, E1)
            wait_product(act, "moe1_0")
            act.dma_start(brow, a["brow"]).then_inc(S("bias loaded"), 16)

            squares("nf", X, [f"moe1_{b}" for b in range(4)])
            rows(2, 0)
            norm_root("nf")
            rows(2, 1)
            squares("m1", X, "nf")
            norm_root("m1")
            rows(2, 3)
            shift("m1", H, lambda k: mod2[:, k, 0:1], "h3 ready")

            def two(n, h, dst, func, bias=None, scale=1.0):
                wait_product(act, n)
                for t in range(2):
                    ins = nc.scalar.activation(dst[:, h + t, :], bank(n)[:, t * T:t * T + T], func,
                                               bias=col("b_in", bias + t), scale=scale)
                ins.then_inc(gone(n), 1)

            link(nc.scalar.activation(lgs[:, 0, :], col("decay", 0, 8), ACT.Abs))
            nc.scalar.activation(lgs[:, 0, :], lgs[:, 0, :], ACT.Exp, scale=-1.0).then_inc(S("decay exp"), 1)
            act.wait_ge(S("decay arg"), 1)
            nc.scalar.activation(lgs[:, 2, :], lgs[:, 1, :], ACT.Ln).then_inc(S("decay log"), 1)
            act.wait_ge(S("ctx loaded"), 16)
            squares("nc", HC)
            norm_root("nc")
            two("kT01", 0, kraw, ACT.Identity, 4)
            shift("nc", HC, lambda k: mod2[:, k, 1:2], "ctx ready")
            two("kT23", 2, kraw, ACT.Identity, 6)
            act.wait_ge(S("log decay ready"), 1)
            for tt in range(TT):
                nc.scalar.activation(ctxdec[:, 0, :, tt], lgs[:, 3, 0:4], ACT.Exp, scale=col("rpos", tt))
                nc.scalar.activation(ctxdec[:, 1, :, tt], lgs[:, 3, 4:8], ACT.Exp,
                                     scale=col("pos", tt)).then_inc(S("ctx decay ready"), 1)
            act.wait_ge(S("ctx keys ready"), 4)
            two("q2_01", 0, qraw, ACT.Identity, 0)
            two("q2_23", 2, qraw, ACT.Identity, 2)
            for h in range(RH):
                wait_product(act, f"st{h}")
                nc.scalar.activation(S0[:, h, :, :], bank(f"st{h}")[:, :].rearrange("p (a b) -> p a b", a=2),
                                     ACT.Copy).then_inc(gone(f"st{h}"), 1)
            def decays(h):
                act.wait_ge(S("decay matrix arg"), h + 1)
                if h:
                    act.wait_ge(S("ctx queries ready"), h)
                nc.scalar.activation(Dm, Dm, ACT.Exp)
                nc.scalar.activation(Ef, irow, ACT.Exp, scale=lgs[:, 3, h:h + 1])
                nc.scalar.activation(Eb, irow, ACT.Exp, scale=lgs[:, 4, 4 + h:5 + h],
                                     bias=backb[:, h:h + 1]).then_inc(S("decay matrix ready"), 1)

            def hyena_inputs(*js):
                for j in js:
                    wait_product(act, f"hy{2 * j}")
                    for t in range(2):
                        ins = nc.scalar.activation(hypad[:, 2 * j + t, 1:T + 1],
                                                   bank(f"hy{2 * j}")[:, t * T:t * T + T], ACT.Identity,
                                                   bias=col("b_in", 24 + 2 * j + t))
                    ins.then_inc(gone(f"hy{2 * j}"), 1)

            for j in range(4):
                two(f"g{2 * j}{2 * j + 1}", 2 * j, sg, ACT.Silu, 16 + 2 * j)
                if j == 1:
                    decays(0)
            act.wait_ge(S("hyena pads zero"), 1)
            for h in range(1, RH):
                decays(h)
                hyena_inputs(2 * h - 2, 2 * h - 1)
                readout_act(act, h - 1)
            readout_act(act, RH - 1)
            act.wait_ge(S("readout ready"), RH)
            for j in range(4):
                two(f"gr{2 * j}", 2 * j, sigR, ACT.Sigmoid, 36 + 2 * j)
            for j in range(4):
                two(f"gh{2 * j}", 2 * j, sigH, ACT.Sigmoid, 44 + 2 * j)
            rows(2, 4)
            for tt in range(TT):
                wait_product(act, f"zt{tt}")
                nc.scalar.activation(ztok[:, tt, :], bank(f"zt{tt}")[:, :], ACT.Copy).then_inc(gone(f"zt{tt}"), 1)

            squares("m2", X, X4)
            norm_root("m2")
            rows(2, 5)
            shift("m2", H, lambda k: mod2[:, 24 + k, 0:1], "h4 ready")
            by_token_copies(2)
            routing(1)
            experts_act(2, N3, E2)
            squares("mf", X, [f"moe2_{b}" for b in range(4)])
            norm_root("mf")
            for j in range(4):
                act.wait_ge(S("norm scaled"), DK * NORM["mf"] + 2 * j + 2)
                act.dma_start(out[:, 2 * j:2 * j + 2, :], X[:, 2 * j:2 * j + 2, :]).then_inc(S("stored"), 16)
            act.wait_ge(S("stored"), 64)

        @block.vector
        def _(dve):
            steps = [0]

            def link(ins):
                steps[0] += 1
                ins.then_inc(S("vector step"), 1)
                dve.wait_ge(S("vector step"), steps[0])

            def take(ins, name):
                ins.then_inc(gone(name), 1)
                wait_taken(dve, name)

            V_ = nc.vector

            def log1p(y, w, lnw, tmp, out):
                link(V_.tensor_scalar(tmp, w, 1.0, None, ALU.subtract))
                link(V_.tensor_scalar(out, tmp, 0.0, None, ALU.is_equal))
                link(V_.tensor_tensor(tmp, tmp, out, ALU.add))
                link(V_.reciprocal(tmp, tmp))
                link(V_.tensor_tensor(tmp, tmp, lnw, ALU.mult))
                link(V_.tensor_tensor(tmp, tmp, out, ALU.add))
                link(V_.tensor_tensor(out, tmp, y, ALU.mult))

            dve.wait_ge(S("softplus exp"), 1)
            V_.tensor_scalar(sml[:, 3:6], sml[:, 0:3], 1.0, None, ALU.add).then_inc(S("softplus arg"), 1)
            dve.wait_ge(S("softplus log"), 1)
            log1p(sml[:, 0:3], sml[:, 3:6], sml[:, 6:9], sml[:, 9:12], sml[:, 12:15])
            link(V_.tensor_scalar(sml[:, 15:18], col("lam", 0, 3), -1.0, 0.0, ALU.mult, ALU.max))
            link(V_.tensor_tensor(sml[:, 15:18], sml[:, 15:18], sml[:, 12:15], ALU.add))
            V_.tensor_scalar(lru_scale[:, 0, :], sml[:, 15:18], -8.0, None, ALU.mult)
            V_.tensor_scalar(lru_scale[:, 1, :], sml[:, 15:18], 8.0, None, ALU.mult).then_inc(S("softplus ready"), 1)

            TWO_PI = 2.0 * np.pi
            C1 = 6.28125
            C2 = float(np.float32(np.round((TWO_PI - C1) * 2 ** 20) / 2 ** 20))
            C3 = float(np.float32(TWO_PI - C1 - C2))
            MAGIC = 12582912.0
            PI_BELOW = 3.1415925

            def sine_argument(name, bias):
                wait_product(dve, name)
                take(V_.tensor_scalar(arg, bank(name)[0:64, 0:T], col(bias, rows=slice(0, 64)),
                                      col("f_freq", rows=slice(0, 64)), ALU.add, ALU.mult), name)
                link(V_.tensor_scalar(rnd, arg, float(1.0 / TWO_PI), MAGIC, ALU.mult, ALU.add))
                link(V_.tensor_scalar(rnd, rnd, MAGIC, None, ALU.subtract))
                for c in (C1, C2, C3):
                    link(V_.scalar_tensor_tensor(arg, rnd, -c, arg, ALU.mult, ALU.add))
                V_.tensor_scalar(arg, arg, PI_BELOW, -PI_BELOW, ALU.min, ALU.max).then_inc(S("sine argument"), 1)

            def ada1(p):
                wait_product(dve, f"a1_{p}")
                take(V_.tensor_tensor(mod1[:, 8 * p:8 * p + 8], bank(f"a1_{p}")[:, 0:8], col("b_ada", 8 * p, 8),
                                      ALU.add), f"a1_{p}")

            def ada2(p):
                wait_product(dve, f"a2_{p}")
                take(V_.tensor_tensor(mod2[:, 8 * p:8 * p + 8, :],
                                      bank(f"a2_{p}")[:, 0:16].rearrange("p (a b) -> p a b", b=2),
                                      bc(col("b_ada2", 8 * p, 8).unsqueeze(2), [P, 8, 2]), ALU.add), f"a2_{p}")

            def gain(i, g, scale):
                link(V_.scalar_tensor_tensor(gs[:, i, :], scale, 1.0, col(g, 0, 8), ALU.add, ALU.mult))

            def norm_scale(key, src, dst, scales):
                wait_taken(dve, key + "_ss")
                link(V_.reciprocal(rstd[:, :], root[:, :]))
                for k in range(DK):
                    V_.scalar_tensor_tensor(dst[:, k, :], src[:, k, :], scales(k), rstd[:, :], ALU.mult,
                                            ALU.mult).then_inc(S("norm scaled"), 1)

            ada1(0)
            ada1(1)
            gain(0, "g_mix", mod1[:, 8:16])
            norm_scale("n1", X, H, lambda k: gs[:, 0, k:k + 1])
            wait_taken(dve, "cvg")
            wait_product(dve, "cvv")
            take(V_.tensor_tensor(upad[:, :, CONV_K - 1:], cvsg, bank("cvv")[:, :].rearrange("p (a b) -> p a b", a=2),
                                  ALU.mult), "cvv")
            sine_argument("f1", "f_b1")
            sine_argument("f2", "f_b2")
            dve.wait_ge(S("pads zero"), 1)
            wait_taken(dve, "lrx01")
            wait_taken(dve, "lrx2")
            for j in range(LRU_K):
                for t in range(LT):
                    tap = col("lru_w", t * LRU_K + j)
                    if j == 0:
                        ins = V_.tensor_scalar(xc[:, t, :], lxpad[:, t, 0:T], tap, col("lru_b", t), ALU.mult, ALU.add)
                    else:
                        ins = V_.scalar_tensor_tensor(xc[:, t, :], lxpad[:, t, j:j + T], tap, xc[:, t, :],
                                                      ALU.mult, ALU.add)
                link(ins) if j < LRU_K - 1 else ins.then_inc(S("lru conv ready"), 1)

            def long_conv(taps):
                for j in taps:
                    for t in range(CT):
                        tap = col("conv_w", t * CONV_K + j)
                        if j == 0:
                            ins = V_.tensor_scalar(u2[:, t, :], upad[:, t, 0:T], tap, col("conv_b", t),
                                                   ALU.mult, ALU.add)
                        else:
                            ins = V_.scalar_tensor_tensor(u2[:, t, :], upad[:, t, j:j + T], tap, u2[:, t, :],
                                                          ALU.mult, ALU.add)
                    link(ins) if j < CONV_K - 1 else ins.then_inc(S("conv ready"), 1)

            for n in range(4):
                name = f"f3_{n // 2}{n % 2}"
                wait_product(dve, name)
                dve.wait_ge(S("decay ready"), n // 2 + 1)
                V_.tensor_tensor(filt[:, n // 2, n % 2, :], bank(name)[:, :], decay[:, n // 2, :],
                                 ALU.mult).then_inc(gone(name), 1)
            long_conv(range(0, 8))
            for half in range(2):
                wait_product(dve, f"f4_{half}")
                take(V_.reciprocal(decay[:, half, :], bank(f"f4_{half}")[:, :]), f"f4_{half}")
            for tt in range(TT):
                ins = V_.tensor_tensor(filt[:, tt, :, :], filt[:, tt, :, :], decay[:, :, :], ALU.mult)
            link(ins)
            V_.tensor_tensor(absf[:, :, 0, :], filt[:, :, 0, :], filt[:, :, 1, :], ALU.add)
            V_.tensor_tensor(absf[:, :, 1, :], filt[:, :, 0, :], filt[:, :, 1, :],
                             ALU.subtract).then_inc(S("filter pair ready"), 1)
            long_conv(range(8, CONV_K))
            wait_product(dve, "mu")
            for t in range(CT):
                ins = V_.scalar_tensor_tensor(u2[:, t, :], bank("mu")[:, 0:T], -1.0 / CONV_W, u2[:, t, :],
                                              ALU.mult, ALU.add)
            ins.then_inc(gone("mu"), 1)
            dve.wait_ge(S("gate log ready"), 1)
            link(V_.scalar_tensor_tensor(lgx, lgx, 0.0, W[0:PAIR, 0:2, :], ALU.min, ALU.subtract))
            for pr in range(2):
                ins = V_.tensor_tensor_scan(bcum[:, pr, :], segm, lgx[:, pr, :], 0.0, ALU.mult, ALU.add)
            link(ins)
            for pr in range(2):
                b4 = bcum[:, pr, :].rearrange("p (c s) -> p c s", s=GCH)
                V_.tensor_tensor(diff[:, pr, :].rearrange("p (c s) -> p c s", s=GCH),
                                 bc(b4[:, :, GCH - 1:GCH], [PAIR, T // GCH, GCH]), b4,
                                 ALU.subtract).then_inc(S("gate sums ready"), 1)
            dve.wait_ge(S("gate powers ready"), 1)
            dve.wait_ge(S("heads zero"), 1)
            wait_taken(dve, "q01")
            wait_taken(dve, "k01")
            V_.tensor_tensor(diff, diff, kT1, ALU.mult).then_inc(S("gla keys ready"), 1)
            V_.tensor_tensor(kin, kin, kT1, ALU.mult)
            for h in range(GH):
                ins = V_.scalar_tensor_tensor(qz[:, h, :], qT[:, h // 2, :], col("head", h % 2, rows=slice(0, PAIR)),
                                              eb[:, h // 2, :], ALU.mult, ALU.mult)
            ins.then_inc(S("gla queries ready"), 1)
            wait_taken(dve, "var")
            link(V_.reciprocal(rstd[:, :], root[:, :]))
            V_.tensor_tensor(u2, u2, bc(rstd[:, :].unsqueeze(1), [P, CT, T]), ALU.mult).then_inc(S("conv scaled"), 1)
            wait_taken(dve, "lru2")
            link(V_.tensor_tensor(ig, ig, xc, ALU.mult))
            dve.wait_ge(S("lru decay"), 3)
            link(V_.tensor_scalar(xc, rg, 1.0, None, ALU.add))
            link(V_.reciprocal(xc, xc))
            V_.tensor_tensor(xc, xc, rg, ALU.mult).then_inc(S("lru root arg"), 1)
            wait_product(dve, "k2t")
            for ch in range(2):
                r = slice(64 * ch, 64 * ch + 64)
                ins = V_.tensor_copy(k2z[r, :, ch, :, :].rearrange("p a b c -> p a (b c)"),
                                     bank("k2t")[r, 0:4 * PAIR].rearrange("p (a b) -> p a b", a=TT))
            ins.then_inc(gone("k2t"), 1)
            for n, h in (("sc01", 0), ("sc23", 2)):
                wait_product(dve, n)
                V_.tensor_tensor(sm[:, h:h + 2, :, :].rearrange("p a b c -> p (a b) c"),
                                 bank(n)[:, :].rearrange("p (a b) -> p a b", a=4),
                                 bc(gmask.unsqueeze(1), [P, 4, P]), ALU.mult).then_inc(gone(n), 1)
            ada1(2)
            for c in range(3):
                wait_product(dve, f"kv{c}")
                kv = bank(f"kv{c}")[0:PAIR, 0:4 * GDV].rearrange("p (a b) -> p a b", a=2)
                if c == 0:
                    ins = V_.tensor_copy(states[:, 0, :, :], kv)
                else:
                    for pr in range(2):
                        ins = V_.scalar_tensor_tensor(states[:, c, pr, :], states[:, c - 1, pr, :],
                                                      gdec[:, pr, c:c + 1], kv[:, pr, :], ALU.mult, ALU.add)
                take(ins, f"kv{c}")
            dve.wait_ge(S("lru root ready"), 1)
            link(V_.tensor_tensor(ig, ig, xc, ALU.mult))
            for t in range(LT):
                ins = V_.tensor_tensor_scan(rg[:, t, :], ag[:, t, :], ig[:, t, :], 0.0, ALU.mult, ALU.add)
            link(ins)
            wait_taken(dve, "lry01")
            wait_taken(dve, "lry2")
            V_.tensor_tensor(gy, gy, rg, ALU.mult).then_inc(S("mix r ready"), 1)
            ada1(3)
            for n, o, h in (("os01", "o01", 0), ("os23", "o23", 2)):
                wait_taken(dve, n)
                link(V_.reciprocal(gla_root[:, h:h + 2, :], gla_root[:, h:h + 2, :]))
                tmp = W[0:GDV, 4 + h:6 + h, :]
                take(V_.tensor_tensor(tmp, bank(o)[0:GDV, :].rearrange("p (a b) -> p a b", a=2),
                                      gla_root[:, h:h + 2, :], ALU.mult), o)
            wait_taken(dve, "og23")
            for h in range(GH):
                V_.scalar_tensor_tensor(sog[0:GDV, h, :], W[0:GDV, 4 + h, :], col("gla_g", h, rows=slice(0, GDV)),
                                        sog[0:GDV, h, :], ALU.mult, ALU.mult).then_inc(S("mix o ready"), 1)
            ada1(4)
            ada1(5)
            gain(1, "g_ffn", mod1[:, 32:40])

            def add_to_x(names, gate, width=2):
                for j, n in enumerate(names):
                    wait_product(dve, n)
                    for t in range(2):
                        k = 2 * j + t
                        ins = V_.scalar_tensor_tensor(X[:, k, :], bank(n)[:, t * T:t * T + T], gate(k), X[:, k, :],
                                                      ALU.mult, ALU.add)
                    ins.then_inc(gone(n), 1)

            add_to_x(X1, lambda k: mod1[:, 16 + k:17 + k])
            norm_scale("n2", X, H, lambda k: gs[:, 1, k:k + 1])
            ada2(2)

            def R(lo, n):
                return route[:, lo:lo + n]

            def R2(lo, m):
                return route[:, lo:lo + TT * m].rearrange("p (t m) -> p t m", t=TT)

            def routing(m, n, bias, tie):
                w = 4 + 4 * n
                L = R2(0, w)
                wait_product(dve, f"rt{m + 1}")
                take(V_.tensor_tensor(L, bank(f"rt{m + 1}")[:, 0:TT * w].rearrange("p (t m) -> p t m", t=TT),
                                      bc(col(bias, 0, w).unsqueeze(1), [P, TT, w]), ALU.add), f"rt{m + 1}")
                gmax, gexp, gsum = R(72, 2), rv["gexp"], R(90, 2)
                first, tmp, best = R2(104, 4), R2(264, n), R(94, 2)

                def one_hot(dst, src, top, names_, k):
                    link(V_.tensor_tensor(dst, src, bc(top.unsqueeze(2), [P, TT, k]), ALU.is_equal))
                    link(V_.tensor_tensor(dst, dst, bc(col(names_, 0, k).unsqueeze(1), [P, TT, k]), ALU.mult))
                    link(V_.tensor_reduce(best, dst, AX.X, ALU.max))
                    link(V_.tensor_tensor(dst, dst, bc(best.unsqueeze(2), [P, TT, k]), ALU.is_equal))

                link(V_.tensor_reduce(gmax, L[:, :, 0:4], AX.X, ALU.max))
                V_.tensor_tensor(gexp, L[:, :, 0:4], bc(gmax.unsqueeze(2), [P, TT, 4]),
                                 ALU.subtract).then_inc(S("route group arg"), 1)
                one_hot(first, L[:, :, 0:4], gmax, "tie4", 4)
                es, m1, oh1, e2, m2, oh2 = R2(176, n), R(192, 2), R2(200, n), R2(216, n), R(232, 2), R2(240, n)
                for t in range(TT):
                    prod = route[:, 112:112 + 4 * n].rearrange("p (e g) -> p e g", g=4)
                    link(V_.tensor_tensor(prod, L[:, t, 4:].rearrange("p (g e) -> p e g", g=4),
                                          bc(first[:, t, :].unsqueeze(1), [P, n, 4]), ALU.mult))
                    link(V_.tensor_reduce(es[:, t, :], prod, AX.X, ALU.add))
                link(V_.tensor_reduce(m1, es, AX.X, ALU.max))
                one_hot(oh1, es, m1, f"tie{n}", n)
                link(V_.scalar_tensor_tensor(e2, oh1, -3.0e38, es, ALU.mult, ALU.add))
                link(V_.tensor_reduce(m2, e2, AX.X, ALU.max))
                one_hot(oh2, e2, m2, f"tie{n}", n)
                V_.tensor_tensor(rv["pexp"], m2, m1, ALU.subtract).then_inc(S("route pair arg"), 1)
                dve.wait_ge(S("route group exp"), m + 1)
                E = 4 * n
                both = R2(264, n)
                link(V_.tensor_tensor(both, oh1, oh2, ALU.add))
                for t in range(TT):
                    ins = V_.tensor_tensor(over[:, t, 0:E].rearrange("p (g e) -> p g e", g=4),
                                           bc(first[:, t, :].unsqueeze(2), [P, 4, n]),
                                           bc(both[:, t, :].unsqueeze(1), [P, 4, n]), ALU.mult)
                ins.then_inc(S("chosen"), 1)
                link(V_.tensor_reduce(gsum, gexp, AX.X, ALU.add))
                dve.wait_ge(S("route pair exp"), m + 1)
                w1, w2 = R(258, 2), R(260, 2)
                link(V_.tensor_scalar(w1, rv["pexp"], 1.0, None, ALU.add))
                link(V_.tensor_tensor(w1, w1, gsum, ALU.mult))
                link(V_.reciprocal(w1, w1))
                link(V_.tensor_tensor(w2, w1, rv["pexp"], ALU.mult))
                link(V_.tensor_tensor(oh1, oh1, bc(w1.unsqueeze(2), [P, TT, n]), ALU.mult))
                link(V_.tensor_tensor(oh2, oh2, bc(w2.unsqueeze(2), [P, TT, n]), ALU.mult))
                link(V_.tensor_tensor(oh1, oh1, oh2, ALU.add))
                for t in range(TT):
                    link(V_.tensor_tensor(comb[:, t, 0:4 * n].rearrange("p (g e) -> p g e", g=4),
                                          bc(first[:, t, :].unsqueeze(2), [P, 4, n]),
                                          bc(oh1[:, t, :].unsqueeze(1), [P, 4, n]), ALU.mult))

            def places_and_overflow(m, E):
                name = f"rk{m}"
                wait_product(dve, name)
                take(V_.scalar_tensor_tensor(rank[:, :, 0:E], bank(name)[:, 0:TT * E].rearrange("p (t e) -> p t e", t=TT),
                                             1.0, over[:, :, 0:E], ALU.add, ALU.mult), name)
                link(V_.tensor_scalar(rank[:, :, 0:E], rank[:, :, 0:E], 1.0, None, ALU.subtract))
                link(V_.tensor_scalar(over[:, :, 0:E], rank[:, :, 0:E], float(CAP), None, ALU.is_ge))
                V_.tensor_reduce(n_over[:, 0:1], over[:, :, 0:E], AX.XY, ALU.add).then_inc(S("overflow counted"), 1)
                dve.wait_ge(S("overflow counted"), m)
                V_.tensor_tensor(over[:, :, 0:E], over[:, :, 0:E], comb[:, :, 0:E], ALU.mult)
                wait_product(dve, f"fl{m}")
                take(V_.tensor_copy(flag[:, :], bank(f"fl{m}")[:, 0:1]), f"fl{m}")
                dve.sem_inc(S(f"moe{m} flag ready"), 1)

            def experts_dve(m, n0, count):
                def picks(i, e):
                    for t in range(TT):
                        ins = V_.tensor_scalar(pick[:, e % 2, t, :], places, rank[:, t, bass.ds(i * 2 + e, 1)], None,
                                               ALU.is_equal)
                    ins.then_inc(S(f"moe{m} picks ready"), 1)

                def hidden(i, e):
                    dve.wait_ge(S(f"moe{m} silu ready"), i * 2 + e + 1)
                    V_.tensor_tensor(hidt[CAP:P, :], sact[CAP:P, :], psum[5][CAP:P, :],
                                     ALU.mult).then_inc(S(f"moe{m} hidden"), 1)

                def turn(i, last=False):
                    for e in (0, 1):
                        dve.wait_ge(S(f"moe{m} hidden turned"), i * 2 + e + 1)
                        V_.tensor_copy(hid, psum[7][:, 0:T].rearrange("p (a b) -> p a b", a=4)
                                       ).then_inc(S(f"moe{m} hidden by feature"), 1)
                        if not last:
                            picks(i, e + 2)
                        if e == 0:
                            for t in range(TT):
                                for h in (0, 1):
                                    at_e = bass.ds(i * 2 + h, 1)
                                    ins = V_.tensor_scalar(pickw[:, t, CAP * h:CAP * h + CAP], places,
                                                           rank[:, t, at_e], comb[:, t, at_e],
                                                           ALU.is_equal, ALU.mult)
                            ins.then_inc(S(f"moe{m} weighted picks ready"), 1)
                        if not (last and e):
                            hidden(i, e + 1)
                        used_up(dve, i, 3 if last and e else 3 * e + 2, n0)
                        V_.tensor_copy(yexp[CAP * e:CAP * e + CAP, 512:1024],
                                       psum[6][CAP:P, :]).then_inc(S(f"moe{m} right half ready"), 1)
                        if e:
                            dve.wait_ge(S(f"moe{m} turned"), i + 1)
                            V_.tensor_copy(put, psum[7][:, T:2 * T]).then_inc(S(f"moe{m} put ready"), 1)

                V_.memset(zeros, 0.0).then_inc(S("zeros set"), 1)
                picks(0, 0)
                picks(0, 1)
                hidden(0, 0)
                with dve.Fori(0, count // 2 - 1) as i:
                    turn(i)
                turn(count // 2 - 1, last=True)
                crowded = dve.value_load(flag[0:1, 0:1], min_val=0, max_val=TT * P * 2)
                with dve.If(crowded > 0):
                    dve.sem_inc(S(f"over{m} hidden"), 1)
                    with dve.Fori(0, count) as e:
                        for t in range(TT):
                            ins = V_.tensor_scalar(odiag[:, t, :], ident, over[:, t, bass.ds(e, 1)], None, ALU.mult)
                        ins.then_inc(S(f"over{m} diagonal"), 1)
                        dve.wait_ge(S(f"over{m} weights spread"), e + 1)
                        for f in range(4):
                            dve.wait_ge(S(f"over{m} silu"), e * 4 + f + 1)
                            V_.tensor_tensor(oweigh, oact, psum[6][:, 0:T], ALU.mult).then_inc(S(f"over{m} weighed"), 1)
                            dve.wait_ge(S(f"over{m} weighed"), e * 4 + f + 1)
                            V_.tensor_tensor(ohid, oweigh, psum[4][:, T:2 * T],
                                             ALU.mult).then_inc(S(f"over{m} hidden"), 1)
                for b in range(4, BANKS):
                    wait_product(dve, f"moe{m}_{b}")
                    dve.sem_inc(drained[b], 1)

            routing(0, 4, "br1", "tie4")
            places_and_overflow(1, E1)
            experts_dve(1, N1, E1)
            add_to_x([f"moe1_{b}" for b in range(4)], lambda k: mod1[:, 40 + k:41 + k])
            ada2(0)
            norm_scale("nf", X, X, lambda k: col("g_final", k))
            ada2(1)
            gain(2, "g1", mod2[:, 8:16, 1])
            gain(3, "g1", mod2[:, 8:16, 0])
            norm_scale("m1", X, H, lambda k: gs[:, 3, k:k + 1])
            ada2(3)

            dve.wait_ge(S("decay exp"), 1)
            V_.tensor_scalar(lgs[:, 1, :], lgs[:, 0, :], 1.0, None, ALU.add).then_inc(S("decay arg"), 1)
            dve.wait_ge(S("decay log"), 1)
            log1p(lgs[:, 0, :], lgs[:, 1, :], lgs[:, 2, :], lgs[:, 4, :], lgs[:, 3, :])
            link(V_.scalar_tensor_tensor(lgs[:, 3, :], col("decay", 0, 8), 0.0, lgs[:, 3, :], ALU.min, ALU.subtract))
            V_.tensor_scalar(lgs[:, 4, :], lgs[:, 3, :], -1.0, None, ALU.mult)
            V_.tensor_scalar(backb[:, :], lgs[:, 3, 4:8], float(T + 1), None, ALU.mult).then_inc(S("log decay ready"), 1)
            dve.wait_ge(S("log decay ready"), 1)
            norm_scale("nc", HC, HC, lambda k: gs[:, 2, k:k + 1])
            dve.wait_ge(S("bias loaded"), 16)
            for tt in range(TT):
                wait_product(dve, f"kc{tt}")
                V_.tensor_tensor(KC[:, tt, :], bank(f"kc{tt}")[:, :], brow[:, 0:512], ALU.add).then_inc(gone(f"kc{tt}"), 1)
            for half in range(2):
                c = slice(512 * half, 512 * half + 512)
                for what, dst in (("vx", V), ("vc", VC)):
                    for tt in range(TT):
                        n = f"{what}{half}{tt}"
                        wait_product(dve, n)
                        V_.tensor_tensor(dst[:, tt, c], bank(n)[:, :], brow[:, 512 + 512 * half:1024 + 512 * half],
                                         ALU.add).then_inc(gone(n), 1)

            def rotate(name, h, raw, dst, scale):
                wait_product(dve, name)
                cos, sin = (bc(rope[:, i:i + 1, :], [P, 2, T]) for i in range(2))
                link(V_.scalar_tensor_tensor(dst[:, h:h + 2, :], raw[:, h:h + 2, :], scale, cos, ALU.mult, ALU.mult))
                take(V_.scalar_tensor_tensor(raw[:, h:h + 2, :], bank(name)[:, :].rearrange("p (a b) -> p a b", a=2),
                                             scale, sin, ALU.mult, ALU.mult), name)
                V_.tensor_tensor(dst[:, h:h + 2, :], dst[:, h:h + 2, :], raw[:, h:h + 2, :],
                                 ALU.add).then_inc(S("rotated"), 1)

            dve.wait_ge(S("ctx decay ready"), 2)
            wait_taken(dve, "kc1")
            wait_taken(dve, "vc11")
            for tt in range(TT):
                for way in range(2):
                    V_.tensor_tensor(kdec[:, :, way, tt, :], KC[:, tt, :].rearrange("p (h d) -> p h d", h=RH),
                                     bc(ctxdec[:, way, :, tt:tt + 1], [P, RH, P]),
                                     ALU.mult).then_inc(S("ctx keys ready"), 1)
            rotate("rk01", 0, kraw, kr, 1.0)
            rotate("rk23", 2, kraw, kr, 1.0)
            rotate("rq01", 0, qraw, qr, float(RDK) ** -0.5)
            rotate("rq23", 2, qraw, qr, float(RDK) ** -0.5)

            def readout(h):
                wait_taken(dve, f"rs{h}")
                link(V_.reciprocal(rstd[:, :], root[:, :]))
                take(V_.tensor_tensor(rtmp, bank(f"o{h}")[:, :].rearrange("p (a b) -> p a b", a=2),
                                      bc(rstd[:, :].unsqueeze(1), [P, 2, T]), ALU.mult), f"o{h}")
                V_.tensor_tensor(sg[:, 2 * h:2 * h + 2, :], sg[:, 2 * h:2 * h + 2, :], rtmp,
                                 ALU.mult).then_inc(S("readout ready"), 1)

            dve.wait_ge(S("rotated"), 4)
            for h in range(RH):
                for jt in range(TT):
                    V_.tensor_scalar(Dm[:, jt, :], irow, col("pos1", jt), lgs[:, 4, 4 + h:5 + h],
                                     ALU.subtract, ALU.mult)
                    ins = V_.tensor_scalar(dtmp[:, jt, :], irow, col("pos1", jt), lgs[:, 3, h:h + 1],
                                           ALU.subtract, ALU.mult)
                link(ins)
                V_.tensor_tensor(Dm, Dm, dtmp, ALU.min).then_inc(S("decay matrix arg"), 1)
                dve.wait_ge(S("decay matrix ready"), h + 1)
                V_.tensor_tensor(qf[:, h % 2, :], qr[:, h, :], Ef, ALU.mult)
                V_.tensor_tensor(qb[:, h % 2, :], qr[:, h, :], Eb, ALU.mult).then_inc(S("ctx queries ready"), 1)
                wait_product(dve, f"s{h}")
                take(V_.tensor_tensor(Pm[h % 2], bank(f"s{h}")[:, :].rearrange("p (a b) -> p a b", a=2), Dm,
                                      ALU.mult), f"s{h}")
                if h == 1:
                    wait_taken(dve, "g67")
                if h:
                    readout(h - 1)
            readout(RH - 1)

            for n in range(6):
                wait_taken(dve, f"hy{2 * n}")
            for c in range(HYT):
                for j in range(3):
                    for dst, t in ((x0[:, c, :], c), (cv1, HYT + c), (cv2, 2 * HYT + c)):
                        tap = col("hy_w", 3 * t + j)
                        if j == 0:
                            ins = V_.tensor_scalar(dst, hypad[:, t, 0:T], tap, col("hy_b", t), ALU.mult, ALU.add)
                        else:
                            ins = V_.scalar_tensor_tensor(dst, hypad[:, t, j:j + T], tap, dst, ALU.mult, ALU.add)
                    link(ins)
                V_.tensor_tensor(zT[:, c, :], cv1, cv2, ALU.mult).then_inc(S("z ready"), 1)
                dve.wait_ge(S("z ready"), c + 1)
            ada2(4)
            gain(4, "g2", mod2[:, 32:40, 0])
            for kt in range(2):
                zr, zi = f"zr{kt}", f"zi{kt}"
                wait_product(dve, zi)
                V_.tensor_tensor(Y[:, 0, kt, :], bank(zr)[:, :], HF[:, 0, kt, :], ALU.mult)
                V_.tensor_tensor(Y[:, 1, kt, :], bank(zr)[:, :], HF[:, 1, kt, :], ALU.mult).then_inc(gone(zr), 1)
                V_.tensor_tensor(ztmp[:, 0, :], bank(zi)[:, :], HF[:, 1, kt, :], ALU.mult)
                take(V_.tensor_tensor(ztmp[:, 1, :], bank(zi)[:, :], HF[:, 0, kt, :], ALU.mult), zi)
                V_.tensor_tensor(Y[:, 0, kt, :], Y[:, 0, kt, :], ztmp[:, 0, :], ALU.subtract)
                V_.tensor_tensor(Y[:, 1, kt, :], Y[:, 1, kt, :], ztmp[:, 1, :], ALU.add).then_inc(S("spectrum ready"), 1)
                dve.wait_ge(S("spectrum ready"), kt + 1)
            for j in range(4):
                wait_taken(dve, f"gr{2 * j}")
                wait_taken(dve, f"gh{2 * j}")
            for j in range(4):
                n = f"ro{2 * j}"
                wait_product(dve, n)
                V_.tensor_tensor(H[:, 2 * j:2 * j + 2, :], bank(n)[:, :].rearrange("p (a b) -> p a b", a=2),
                                 sigR[:, 2 * j:2 * j + 2, :], ALU.mult).then_inc(gone(n), 1)
            for c in range(HYT):
                n = f"yt{c // 2 * 2}"
                wait_product(dve, n)
                ins = V_.scalar_tensor_tensor(zT[:, c, :], zT[:, c, :], col("skip", c),
                                              bank(n)[:, (c % 2) * T:(c % 2) * T + T], ALU.mult, ALU.add)
                if c % 2:
                    take(ins, n)
                    V_.tensor_tensor(hyo[:, c - 1:c + 1, :], zT[:, c - 1:c + 1, :], x0[:, c - 1:c + 1, :],
                                     ALU.mult).then_inc(S("hyena ready"), 1)
            for j in range(4):
                n = f"ho{2 * j}"
                wait_product(dve, n)
                take(V_.tensor_tensor(sigH[:, 2 * j:2 * j + 2, :], bank(n)[:, :].rearrange("p (a b) -> p a b", a=2),
                                      sigH[:, 2 * j:2 * j + 2, :], ALU.mult), n)
                V_.tensor_tensor(H[:, 2 * j:2 * j + 2, :], H[:, 2 * j:2 * j + 2, :], sigH[:, 2 * j:2 * j + 2, :],
                                 ALU.add).then_inc(S("merged"), 1)
            add_to_x(X4, lambda k: mod2[:, 16 + k, 0:1])
            norm_scale("m2", X, H, lambda k: gs[:, 4, k:k + 1])
            ada2(5)
            routing(1, 8, "br2", "tie8")
            places_and_overflow(2, E2)
            experts_dve(2, N3, E2)
            add_to_x([f"moe2_{b}" for b in range(4)], lambda k: mod2[:, 40 + k, 0:1])
            norm_scale("mf", X, X, lambda k: col("g_out", k))

        @block.tensor
        def _(pe):
            order = list(place)
            done = [0]

            def begin(name):
                assert order[done[0]] == name
                done[0] += 1
                b, use = place[name]
                if use:
                    pe.wait_ge(drained[b], use)
                return psum[b]

            def end(ins, name):
                ins.then_inc(filled[place[name][0]], 1)

            used = []

            def mm(out_, lhsT, rhs, start, stop):
                ins = nc.tensor.matmul(out_, lhsT, rhs, start=start, stop=stop)
                if used and start and not stop:
                    ins.then_inc(freed[slab_no[used.pop()] % SLOTS], 1)
                return ins

            def ss(name, src_tiles, signal, base, per):
                b = begin(name)
                n = len(src_tiles)
                for k, t in enumerate(src_tiles):
                    if k % per == 0:
                        pe.wait_ge(S(signal), base + k // per + 1)
                    rows = t.shape[0]
                    ins = mm(b[0:rows, 0:T], ones[0:rows, 0:rows], t, k == 0, k == n - 1)
                end(ins, name)

            def norm(key):
                ss(key + "_ss", [W[:, k, :] for k in range(DK)], "squared", 4 * NORM[key], 2)

            def ada(which, p):
                for j in (2 * p, 2 * p + 1):
                    key, name = (f"ada{which}", j), f"r{which}_{j}"
                    wait_slab(pe, slab_no[key])
                    b = begin(name)
                    w = slab(key, DK, 512)
                    for k in range(DK):
                        g = 32 * (k % 4)
                        ins = mm(b[g:g + 32, :], cact[:, k, :], w[:, k, :], k < 4, k >= 4)
                    end(ins, name)
                name = f"a{which}_{p}"
                b = begin(name)
                for j in (2 * p, 2 * p + 1):
                    key = (f"ada{which}", j)
                    wait_taken(pe, f"r{which}_{j}")
                    row = slab(key, 1, 512)
                    for f in range(4):
                        o = (4 * (j % 2) + f) * which
                        ins = mm(b[:, o:o + which], row[:, 0, f * P:f * P + P], col("sel", which - 1, which), True, True)
                    if j % 2:
                        free_and_end(ins, key, name)
                    else:
                        ins.then_inc(freed[slab_no[key] % SLOTS], 1)

            def free_and_end(ins, key, name):
                end(ins, name)
                assert not used
                used.append(key)

            def proj(name, w, c0, src, tiles, m=P, free=None, nk=DK, ready=None):
                b = begin(name)
                for t in range(tiles):
                    for k in range(nk):
                        if ready and t == 0:
                            pe.wait_ge(S(ready), k + 1)
                        ins = mm(b[0:m, t * T:t * T + T], w[:, k, c0 + t * m:c0 + t * m + m], src[:, k, :],
                                 k == 0, k == nk - 1)
                if free:
                    free_and_end(ins, free, name)
                else:
                    end(ins, name)

            def by_token(name, w, c0, width, src, tt, free=None):
                b = begin(name)
                for k in range(DK):
                    ins = mm(b[:, 0:width], src[:, k, tt * P:tt * P + P], w[:, k, c0:c0 + width], k == 0, k == DK - 1)
                if free:
                    free_and_end(ins, free, name)
                else:
                    end(ins, name)

            pe.wait_ge(S("ones set"), 1)
            norm("n1")
            pe.wait_ge(S("c ready"), 2)
            ada(1, 0)
            ada(1, 1)

            keys = [("win", j) for j in range(6)]
            ws = [slab(k, 8, c1 - c0) for k, (c0, c1) in zip(keys, WIN_CUTS)]

            def arrived(key):
                wait_slab(pe, slab_no[key])

            arrived(keys[0])
            proj("cvg", ws[0], CONV_W, H, 2, ready="h1 ready")
            proj("cvv", ws[0], 0, H, 2, free=keys[0])
            pe.wait_ge(S("filter pack loaded"), 16)
            b = begin("f1")
            end(mm(b[0:64, 0:T], fw1, feats, True, True), "f1")
            arrived(keys[1])
            proj("lrx01", ws[1], 0, H, 2)
            pe.wait_ge(S("sine ready"), 1)
            b = begin("f2")
            end(mm(b[0:64, 0:T], fw2, hid1, True, True), "f2")
            proj("lrx2", ws[1], 2 * P, H, 1, free=keys[1])
            pe.wait_ge(S("sine ready"), 2)
            for tt in range(TT):
                for half in range(2):
                    b = begin(f"f3_{tt}{half}")
                    end(mm(b[:, :], hid2[:, tt * P:tt * P + P], fw3[:, half * HYW:half * HYW + HYW], True, True),
                        f"f3_{tt}{half}")
            arrived(keys[2])
            proj("lry01", ws[2], 0, H, 2)
            proj("lry2", ws[2], 2 * P, H, 1, free=keys[2])
            pe.wait_ge(S("filter abs"), 4)
            for half in range(2):
                b = begin(f"f4_{half}")
                for tt in range(TT):
                    ins = mm(b[:, :], ones[:, :], absf[:, tt, half, :], tt == 0, tt == TT - 1)
                end(ins, f"f4_{half}")
            arrived(keys[3])
            proj("q01", ws[3], 0, H, 2, m=PAIR)
            proj("k01", ws[3], GH * GDK, H, 2, m=PAIR, free=keys[3])
            pe.wait_ge(S("filter pair ready"), 1)
            for n in range(4):
                ri, kt = n // 2, n % 2
                b = begin(f"f5_{n}")
                for tt in range(TT):
                    ins = mm(b[:, :], basis[:, ri, tt, kt * P:kt * P + P], absf[:, tt, ri, :], tt == 0, tt == TT - 1)
                end(ins, f"f5_{n}")
            arrived(keys[4])
            for tt in range(TT):
                by_token(f"v{tt}", ws[4], 0, GH * GDV, H, tt)
            proj("glr", ws[4], GH * GDV, H, 1, m=16, free=keys[4])
            pe.wait_ge(S("mixer pack loaded"), 48)
            wait_taken(pe, "glr")
            b = begin("lgp")
            for pr in range(2):
                ins = mm(b[0:PAIR, pr * T:pr * T + T], glaw[:, pr, :], glr, True, True)
            end(ins, "lgp")
            ss("mu", [u2[:, t, :] for t in range(CT)], "conv ready", 0, CT)
            arrived(keys[5])
            proj("og01", ws[5], 0, H, 2, m=GDV)
            ss("var", [W[:, 2 + t, :] for t in range(CT)], "conv squared", 0, CT)
            proj("og23", ws[5], 2 * GDV, H, 2, m=GDV, free=keys[5])
            pe.wait_ge(S("lru conv ready"), 1)
            for t in range(LT):
                b = begin(f"lru{t}")
                for g in range(2):
                    ins = mm(b[:, g * T:g * T + T], lruw[:, g, t, :], xc[:, t, :], True, True)
                end(ins, f"lru{t}")
            pe.wait_ge(S("gla keys ready"), 1)
            b = begin("k2t")
            for tt in range(TT):
                for pr in range(2):
                    o = (2 * tt + pr) * PAIR
                    ins = nc.tensor.transpose(b[:, o:o + PAIR], diff[:, pr, tt * P:tt * P + P],
                                              ident[0:PAIR, 0:PAIR])
            end(ins, "k2t")
            pe.wait_ge(S("gla queries ready"), 1)
            for h in range(GH):
                if h % 2 == 0:
                    b = begin(f"sc{h}{h + 1}")
                for tt in range(TT):
                    o = (2 * (h % 2) + tt) * P
                    s = slice(tt * P, tt * P + P)
                    ins = mm(b[:, o:o + P], kin[:, h // 2, s], qz[:, h, s], True, True)
                if h % 2:
                    end(ins, f"sc{h - 1}{h}")
            ada(1, 2)
            wait_taken(pe, "k2t")
            wait_taken(pe, "v1")
            for c in range(3):
                b = begin(f"kv{c}")
                for pr in range(2):
                    ins = mm(b[0:PAIR, pr * 192:pr * 192 + 192], k2z[:, c // 2, c % 2, pr, :],
                             vtok[:, c // 2, pr * 192:pr * 192 + 192], True, True)
                end(ins, f"kv{c}")
            ada(1, 3)
            wait_taken(pe, "sc23")
            wait_taken(pe, "kv2")
            for h in range(GH):
                if h % 2 == 0:
                    b = begin(f"o{h}{h + 1}")
                for tt in range(TT):
                    o = (h % 2) * T + tt * P
                    mm(b[0:GDV, o:o + P], vtok[:, tt, h * GDV:h * GDV + GDV], sm[:, h, tt, :], True, False)
                    for c in (2 * tt, 2 * tt + 1):
                        if c:
                            e = (h % 2) * GDV
                            ins = mm(b[0:GDV, (h % 2) * T + c * GCH:(h % 2) * T + c * GCH + GCH],
                                     states[:, c - 1, h // 2, e:e + GDV], qz[:, h, c * GCH:c * GCH + GCH],
                                     False, c % 2 == 1)
                if h % 2:
                    end(ins, f"o{h - 1}{h}")
            for h in range(GH):
                if h % 2 == 0:
                    pe.wait_ge(S("gla squared"), h // 2 + 1)
                    b = begin(f"os{h}{h + 1}")
                ins = mm(b[0:GDV, (h % 2) * T:(h % 2) * T + T], ones[0:GDV, 0:GDV], W[0:GDV, 4 + h, :], True, True)
                if h % 2:
                    end(ins, f"os{h - 1}{h}")
            ada(1, 4)
            ada(1, 5)

            pe.wait_ge(S("mix u ready"), 2)
            pe.wait_ge(S("mix r ready"), 1)
            pe.wait_ge(S("mix o ready"), GH)
            mix = ([u2[:, t, :] for t in range(CT)] + [gy[:, t, :] for t in range(LT)]
                   + [sog[0:GDV, h, :] for h in range(GH)])
            for k in range(8):
                j = min(k // 3, 2)
                key = ("wout", j)
                c0, c1 = WOUT_CUTS[j]
                w = c1 - c0
                if k % 3 == 0:
                    arrived(key)
                if k % 2 == 0:
                    b = begin(f"wo{k}{k + 1}")
                for n, src in enumerate(mix):
                    rows = src.shape[0]
                    o = n * w + k * P - c0
                    ins = mm(b[:, (k % 2) * T:(k % 2) * T + T],
                             ring[0:rows, slab_no[key] % SLOTS, o:o + P], src, n == 0, n == len(mix) - 1)
                if k in (2, 7):
                    if k == 7:
                        free_and_end(ins, key, "wo67")
                    else:
                        ins.then_inc(freed[slab_no[key] % SLOTS], 1)
                elif k == 5:
                    free_and_end(ins, key, "wo45")
                elif k % 2:
                    end(ins, f"wo{k - 1}{k}")
            norm("n2")
            ada(2, 2)

            def router(m, n):
                w = 4 + 4 * n
                base = 0 if m == 0 else DK * 20
                v = wr[:, base:base + DK * w].rearrange("p (k w) -> p k w", k=DK)
                b = begin(f"rt{m + 1}")
                for tt in range(TT):
                    for k in range(DK):
                        if tt == 0:
                            pe.wait_ge(S(f"h{2 * m + 2} ready"), k + 1)
                        ins = mm(b[:, tt * w:tt * w + w], H[:, k, tt * P:tt * P + P], v[:, k, :], k == 0, k == DK - 1)
                end(ins, f"rt{m + 1}")

            def turn_h(m):
                for n in range(4):
                    tt, half = n // 2, n % 2
                    b = begin(f"ht{m}_{n}")
                    for k in range(4):
                        ins = nc.tensor.transpose(b[:, k * P:k * P + P], H[:, 4 * half + k, tt * P:tt * P + P], ident)
                    end(ins, f"ht{m}_{n}")

            def ranks(m, E):
                pe.wait_ge(S("chosen"), m)
                b = begin(f"rk{m}")
                mm(b[:, 0:E], before, over[:, 0, 0:E], True, True)
                mm(b[:, E:2 * E], before, over[:, 1, 0:E], True, False)
                end(mm(b[:, E:2 * E], ones[:, :], over[:, 0, 0:E], False, True), f"rk{m}")
                pe.wait_ge(S("overflow counted"), m)
                b = begin(f"fl{m}")
                end(mm(b[:, 0:1], ones[:, :], n_over[:, 0:1], True, True), f"fl{m}")

            def experts_pe(m, n0, count):
                assert not used
                for b in range(BANKS):
                    begin(f"moe{m}_{b}")
                pe.wait_ge(S("zeros set"), m)
                for b in range(4):
                    nc.tensor.matmul(psum[b][:, :], ident, zeros, start=True, stop=False, skip_group_check=True)

                def weights(i, j, k):
                    n = n0 + 2 + j
                    pe.wait_ge(landed[n % SLOTS], i * 32 + 32 * (n // SLOTS + 1))
                    return ring[:, n % SLOTS, :].rearrange("p (k w) -> p k w", k=k)

                def gather(i, e):
                    pe.wait_ge(S(f"moe{m} picks ready"), i * 2 + e + 1)
                    for k in range(DK):
                        for t in range(TT):
                            ins = mm(psum[4][:, k * CAP:k * CAP + CAP], htok[:, t, k * P:k * P + P],
                                     pick[:, e % 2, t, :], t == 0, t == TT - 1)
                    ins.then_inc(S(f"moe{m} gathered"), 1)

                def gate_up(i, e):
                    pe.wait_ge(S(f"moe{m} tokens ready"), i * 2 + e + 1)
                    ws = [weights(i, up_slab(e) - 1 + half, DK) for half in range(2)]
                    for k in range(DK):
                        for half in range(2):
                            ins = mm(psum[5][CAP * half:CAP * half + CAP, :], hexp[:, e % 2, k, :], ws[half][:, k, :],
                                     k == 0, k == DK - 1)
                            if k == DK - 1:
                                ins.then_inc(freed[(n0 + 1 + up_slab(e) + half) % SLOTS], 1)

                def turn_hidden(i, e):
                    pe.wait_ge(S(f"moe{m} hidden"), i * 2 + e + 1)
                    for f in range(4):
                        ins = mm(psum[7][:, CAP * f:CAP * f + CAP], hidt[CAP:P, f * P:f * P + P], ident[CAP:P, CAP:P],
                                 True, True)
                    ins.then_inc(S(f"moe{m} hidden turned"), 1)

                def down(i, e, j):
                    w = weights(i, j, 4)
                    pe.wait_ge(S(f"moe{m} hidden by feature"), i * 2 + e + 1)
                    pe.wait_ge(S(f"moe{m} left half ready"), i * 2 + e + 1)
                    pe.wait_ge(S(f"moe{m} right half ready"), i * 2 + e + 1)
                    for f in range(4):
                        for half in range(2):
                            ins = mm(psum[6][CAP * half:CAP * half + CAP, :], hid[:, f, :],
                                     w[:, f, half * 512:half * 512 + 512], f == 0, f == 3)
                    ins.then_inc(freed[(n0 + 2 + j) % SLOTS], 1)

                def turn(i, last=False):
                    for e in (0, 1):
                        turn_hidden(i, e)
                        if not (last and e):
                            gate_up(i, e + 1)
                        down(i, e, 3 if last and e else 3 * e + 2)
                        if e:
                            pe.wait_ge(S(f"moe{m} weighted picks ready"), i + 1)
                            for t in range(TT):
                                ins = nc.tensor.transpose(psum[7][:, T + t * P:T + t * P + P], pickw[:, t, :], ident)
                            ins.then_inc(S(f"moe{m} turned"), 1)
                        if not last:
                            gather(i, e + 2)
                    pe.wait_ge(S(f"moe{m} left half ready"), i * 2 + 3)
                    pe.wait_ge(S(f"moe{m} right half ready"), i * 2 + 3)
                    pe.wait_ge(S(f"moe{m} put ready"), i + 1)
                    for k in range(DK):
                        ins = nc.tensor.matmul(psum[k // 2][:, (k % 2) * T:(k % 2) * T + T],
                                               yexp[:, k * P:k * P + P], put, start=False, stop=False,
                                               skip_group_check=True)
                    return ins

                pe.sem_inc(S(f"moe{m} left half ready"), 1)
                pe.sem_inc(S(f"moe{m} right half ready"), 1)
                gather(0, 0)
                gate_up(0, 0)
                gather(0, 1)
                with pe.Fori(0, count // 2 - 1) as i:
                    turn(i)
                turn(count // 2 - 1, last=True).then_inc(S(f"moe{m} summed"), 1)
                pe.wait_ge(S(f"moe{m} summed"), 1)

                pe.wait_ge(S(f"moe{m} flag ready"), 1)
                crowded = pe.value_load(flag[0:1, 0:1], min_val=0, max_val=TT * P * 2)
                with pe.If(crowded > 0):
                    pe.sem_inc(S(f"over{m} used"), 1)
                    with pe.Fori(0, count) as e:
                        pe.wait_ge(S(f"over{m} diagonal"), e + 1)
                        for t in range(TT):
                            ins = mm(psum[6][:, t * P:t * P + P], ones[:, :], odiag[:, t, :], True, True)
                        ins.then_inc(S(f"over{m} weights spread"), 1)
                        for f in range(4):
                            pe.wait_ge(S(f"over{m} landed"), e * 192 + 48 * (f + 1))
                            pe.wait_ge(S(f"over{m} hidden"), e * 4 + f + 1)
                            for half, w in enumerate((ogate, oup)):
                                for k in range(DK):
                                    ins = mm(psum[4][:, half * T:half * T + T], w[:, k, :], H[:, k, :],
                                             k == 0, k == DK - 1)
                            ins.then_inc(S(f"over{m} product"), 1)
                            pe.wait_ge(S(f"over{m} hidden"), e * 4 + f + 2)
                            for k in range(DK):
                                ins = nc.tensor.matmul(psum[k // 2][:, (k % 2) * T:(k % 2) * T + T],
                                                       odown[:, k * P:k * P + P], ohid, start=False, stop=False,
                                                       skip_group_check=True)
                            ins.then_inc(S(f"over{m} used"), 1)
                    pe.wait_ge(S(f"over{m} used"), 4 * count + 1)
                for b in range(BANKS):
                    pe.sem_inc(filled[b], 1)

            router(0, 4)
            turn_h(1)
            ranks(1, E1)
            experts_pe(1, N1, E1)
            ada(2, 0)
            norm("nf")
            ada(2, 1)
            norm("m1")
            ada(2, 3)

            pe.wait_ge(S("late pack loaded"), 16)
            key = ("win2", 0)
            w = slab(key, 8, 512)
            arrived(key)
            proj("kT01", w, 0, H, 2, ready="h3 ready")
            norm("nc")
            proj("kT23", w, 2 * P, H, 2)
            pe.wait_ge(S("ctx ready"), DK)
            by_token("kc0", w, 0, 512, HC, 0)
            by_token("kc1", w, 0, 512, HC, 1, free=key)
            for half in range(2):
                key = ("win2", 1 + half)
                w = slab(key, 8, 512)
                arrived(key)
                for what, src in (("vx", H), ("vc", HC)):
                    for tt in range(TT):
                        last = what == "vc" and tt == 1
                        by_token(f"{what}{half}{tt}", w, 0, 512, src, tt, free=key if last else None)
            def swap(name, raw, h):
                b = begin(name)
                for t in range(2):
                    ins = mm(b[:, t * T:t * T + T], perm, raw[:, h + t, :], True, True)
                end(ins, name)

            key = ("win2", 3)
            w = slab(key, 8, 512)
            arrived(key)
            proj("q2_01", w, 0, H, 2)
            proj("q2_23", w, 2 * P, H, 2, free=key)
            wait_taken(pe, "kT23")
            swap("rk01", kraw, 0)
            swap("rk23", kraw, 2)
            pe.wait_ge(S("ctx keys ready"), 4)
            wait_taken(pe, "vc11")
            for h in range(RH):
                b = begin(f"st{h}")
                for way in range(2):
                    for tt in range(TT):
                        ins = mm(b[:, way * RDV:way * RDV + RDV], kdec[:, h, way, tt, :],
                                 VC[:, tt, h * RDV:h * RDV + RDV], tt == 0, tt == TT - 1)
                end(ins, f"st{h}")
            wait_taken(pe, "q2_23")
            swap("rq01", qraw, 0)
            swap("rq23", qraw, 2)
            def gates(j):
                key = ("win2", 4 + j)
                w = slab(key, 8, 512)
                arrived(key)
                proj(f"g{4 * j}{4 * j + 1}", w, 0, H, 2)
                proj(f"g{4 * j + 2}{4 * j + 3}", w, 2 * P, H, 2, free=key)

            def scores(h):
                b = begin(f"s{h}")
                for jt in range(TT):
                    ins = mm(b[:, jt * T:jt * T + T], kr[:, h, jt * P:jt * P + P], qr[:, h, :], True, True)
                end(ins, f"s{h}")

            def attend(h):
                wait_taken(pe, f"s{h}")
                b = begin(f"o{h}")
                for vt in range(2):
                    o = b[:, vt * T:vt * T + T]
                    e = vt * P
                    for jt in range(TT):
                        mm(o, V[:, jt, h * RDV + e:h * RDV + e + P], Pm[h % 2][:, jt, :], jt == 0, False)
                    mm(o, S0[:, h, 0, e:e + P], qf[:, h % 2, :], False, False)
                    ins = mm(o, S0[:, h, 1, e:e + P], qb[:, h % 2, :], False, True)
                end(ins, f"o{h}")

            def readout_sum(h):
                ss(f"rs{h}", [osq[:, t, :] for t in range(2)], "readout squared", h, 2)

            def hyena_inputs(j):
                key = ("win2", 6 + j)
                w = slab(key, 8, 512)
                arrived(key)
                proj(f"hy{4 * j}", w, 0, H, 2)
                proj(f"hy{4 * j + 2}", w, 2 * P, H, 2, free=key)

            gates(0)
            pe.wait_ge(S("rotated"), 4)
            scores(0)
            scores(1)
            gates(1)
            wait_taken(pe, "st3")
            for h in range(RH):
                attend(h)
                if h:
                    readout_sum(h - 1)
                if h < 3:
                    hyena_inputs(h)
                if h < 2:
                    scores(h + 2)
            readout_sum(RH - 1)
            for g, j0 in (("gr", 9), ("gh", 11)):
                for j in range(2):
                    key = ("win2", j0 + j)
                    w = slab(key, 8, 512)
                    arrived(key)
                    proj(f"{g}{4 * j}", w, 0, H, 2)
                    proj(f"{g}{4 * j + 2}", w, 2 * P, H, 2, free=key)
            ada(2, 4)
            pe.wait_ge(S("z ready"), HYT)
            for tt in range(TT):
                b = begin(f"zt{tt}")
                for c in range(HYT):
                    ins = nc.tensor.transpose(b[:, c * P:c * P + P], zT[:, c, tt * P:tt * P + P], ident)
                end(ins, f"zt{tt}")
            for tt in range(TT):
                wait_taken(pe, f"zt{tt}")
            for kt in range(2):
                for ri, n in enumerate((f"zr{kt}", f"zi{kt}")):
                    b = begin(n)
                    for tt in range(TT):
                        ins = mm(b[:, :], mcs[:, ri, tt, kt * P:kt * P + P], ztok[:, tt, :], tt == 0, tt == TT - 1)
                    end(ins, n)
            pe.wait_ge(S("readout ready"), RH)
            for j in range(2):
                key = ("ret_o", j)
                w = slab(key, 8, 512)
                arrived(key)
                proj(f"ro{4 * j}", w, 0, sg, 2)
                proj(f"ro{4 * j + 2}", w, 2 * P, sg, 2, free=key)
            pe.wait_ge(S("spectrum ready"), 2)
            for c in range(HYT):
                if c % 2 == 0:
                    b = begin(f"yt{c}")
                for n in range(4):
                    ri, kt = n // 2, n % 2
                    ins = mm(b[:, (c % 2) * T:(c % 2) * T + T], Y[:, ri, kt, c * P:c * P + P], mcs[:, ri, kt, :],
                             n == 0, n == 3)
                if c % 2:
                    end(ins, f"yt{c - 1}")
            pe.wait_ge(S("hyena ready"), 2)
            key = ("hy_o", 0)
            w = slab(key, 4, 1024)
            arrived(key)
            for j in range(4):
                proj(f"ho{2 * j}", w, 2 * P * j, hyo, 2, nk=HYT, free=key if j == 3 else None)
            pe.wait_ge(S("merged"), 4)
            for j in range(2):
                key = ("wout2", j)
                w = slab(key, 8, 512)
                arrived(key)
                proj(f"w2_{4 * j}", w, 0, H, 2)
                proj(f"w2_{4 * j + 2}", w, 2 * P, H, 2, free=key)
            norm("m2")
            ada(2, 5)
            router(1, 8)
            turn_h(2)
            ranks(2, E2)
            experts_pe(2, N3, E2)
            norm("mf")


_WHOLE = ["w_ada", "w_in", "w_out", "w_gate", "w_up", "w_down", "ada_w_2", "w_in_2", "ret_w_o_2", "hy_w_o_2",
          "w_out_2", "expert_w1_2", "expert_w3_2", "expert_w2_2"]


def packs(i):
    f = np.float32

    def cols_of(v, n):
        return np.ascontiguousarray(np.asarray(v).reshape(n, P).T)

    def padded(v, rows=P):
        v = np.asarray(v)
        out = np.zeros((rows,) + v.shape[1:], f)
        out[:v.shape[0]] = v
        return out

    def taps(w, tiles):
        k = w.shape[0]
        return w.reshape(k, tiles, P).transpose(2, 1, 0).reshape(P, tiles * k)

    def spread(v):
        return np.broadcast_to(np.asarray(v).reshape(1, -1), (P, np.asarray(v).size))

    p = np.arange(P)
    t = np.arange(T)
    c = np.zeros((P, NCOL), f)

    def put(name, v):
        c[:, AT[name]:AT[name] + v.shape[1]] = v

    put("c", cols_of(i["c"], 8))
    both = np.stack([i["c_2"].reshape(8, P), i["c_ctx_2"].reshape(8, P)], 1)
    put("c2", both.reshape(16, P).T)
    put("b_ada", cols_of(i["b_ada"], 48))
    put("b_ada2", cols_of(i["ada_b_2"], 48))
    put("g_mix", cols_of(i["g_mix"], 8))
    put("conv_w", taps(i["conv_dw_w"][0], CT))
    put("conv_b", cols_of(i["conv_dw_b"], 2))
    put("ln_g", cols_of(i["conv_ln_g"], 2))
    put("ln_b", cols_of(i["conv_ln_b"], 2))
    put("lru_w", taps(i["lru_conv_w"][0], LT))
    for name, key in (("lru_b", "lru_conv_b"), ("lru_ba", "lru_b_a"), ("lru_bi", "lru_b_i"), ("lam", "lru_lam")):
        put(name, cols_of(i[key], 3))
    put("gla_b", padded(i["gla_b_gate"][0].reshape(2, PAIR).T))
    put("gla_g", padded(i["gla_norm_g"][0].reshape(GH, GDV).T))
    for name, key in (("g_ffn", "g_ffn"), ("g_final", "g_final"), ("g1", "norm1_g_2"), ("g2", "norm2_g_2"),
                      ("g_out", "final_norm_g_2")):
        put(name, cols_of(i[key], 8))
    put("b_in", cols_of(i["b_in_2"], 52))
    put("decay", spread(i["ret_decay_logit_2"][0]))
    put("hy_w", taps(i["hy_conv_w_2"][0], 12))
    put("hy_b", cols_of(i["hy_conv_b_2"], 12))
    for name, key in (("f_b1", "hy_ffn_b1_2"), ("f_freq", "hy_ffn_freq_2"), ("f_b2", "hy_ffn_b2_2")):
        put(name, padded(i[key].reshape(64, 1)))
    put("skip", cols_of(i["hy_skip_2"], 4))
    put("br1", spread(np.concatenate([i["b_route_group"].reshape(-1), i["b_route_expert"].reshape(-1)])))
    put("br2", spread(np.concatenate([i["router_group_b_2"].reshape(-1), i["router_expert_b_2"].reshape(-1)])))
    times = (np.arange(T, dtype=f) / T).astype(f)
    put("neg_t", -times.reshape(TT, P).T)
    pos = (p[:, None] + P * np.arange(TT)[None, :]).astype(f)
    put("pos", pos)
    put("rpos", T - 1 - pos)
    put("pos1", pos + 1)
    put("tie4", spread(np.arange(4, 0, -1).astype(f)))
    put("tie8", spread(np.arange(8, 0, -1).astype(f)))
    rows = np.arange(P)[:, None]
    put("head", (((rows // GDK == 0) | (rows // GDK == 1)) * (rows // GDK == np.arange(2)[None, :])
                 * float(GDK) ** -0.5).astype(f))
    put("eps", np.full((P, 1), EPS, f))
    put("sel", (rows % 32 == np.arange(3)[None, :]).astype(f))

    def by_feature(x):
        return np.ascontiguousarray(x.reshape(T, DK, P).transpose(2, 1, 0))

    bands = np.linspace(1e-4, 15, 16, dtype=f)
    phase = (f(2.0 * np.pi) * times[:, None] * bands[None, :]).astype(f)
    feats = np.concatenate([times[:, None], np.cos(phase), -np.sin(phase)], -1).astype(f)
    slow, fast = abs(np.log(1e-2)) / 1.5, abs(np.log(1e-2)) / 0.3
    deltas = np.linspace(slow, fast, HYW, dtype=f)

    def tiles(m):
        return m.reshape(TT, P, T).transpose(1, 0, 2)

    w_tau = np.pi * np.outer(t, t + 0.5) / T
    w_mid = np.pi * np.outer(t + 0.5, t + 0.5) / T
    basis = np.stack([tiles(np.cos(w_tau)), tiles(-np.sin(w_tau))], 1).astype(f)
    mcs = np.stack([tiles(np.cos(w_mid)), tiles(-np.sin(w_mid))], 1).astype(f)
    fpack = np.zeros((P, 12 * T), f)
    fpack[:33, 0:T] = feats.T
    fpack[:33, T:T + 64] = i["hy_ffn_w1_2"][0]
    fpack[:64, T + 64:T + 128] = i["hy_ffn_w2_2"][0]
    fpack[:, 2 * T:4 * T] = deltas[None, :]
    fpack[:, 4 * T:8 * T] = basis.reshape(P, -1)
    fpack[:64, 8 * T:12 * T] = i["hy_ffn_w3_2"][0]

    mpack = np.zeros((P, 1408), f)
    lw = mpack[:, 0:768].reshape(P, 2, LT, P)
    for g, key in enumerate(("lru_w_a", "lru_w_i")):
        for b in range(6):
            s = slice(64 * (b % 2), 64 * (b % 2) + 64)
            lw[s, g, b // 2, s] = i[key][0, b]
    j, q = p[:, None], p[None, :]
    mpack[:, 768:896] = (j <= q) & (j // GCH == q // GCH)
    mpack[:, 896:1152] = (t % GCH != 0)[None, :]
    mpack[:16, 1152:1344] = i["gla_w_gate"][0]

    inv = (f(10000.0) ** (-np.arange(32, dtype=f) / f(32))).astype(f)
    ang = np.zeros((P, T), f)
    for blk in range(4):
        where = (t // 64 if blk < 2 else t % 64).astype(f)
        ang[32 * blk:32 * blk + 32] = (inv[:, None] * where[None, :]).astype(f)
    sign = np.where((p // 32) % 2 == 0, -1.0, 1.0)[:, None]
    perm = np.zeros((P, P), f)
    perm[p ^ 32, p] = 1.0
    lpack = np.concatenate([mcs.reshape(P, -1), np.cos(ang), sign * np.sin(ang), perm,
                            np.broadcast_to(t[None, :] + 1, (P, T))], 1).astype(f)

    marks = np.concatenate([np.eye(P), p[:, None] < p[None, :], np.broadcast_to(np.arange(CAP), (P, CAP))],
                           1).astype(f)

    def router(g, e):
        w = np.concatenate([g, e], 1)
        return w.reshape(DK, P, -1).transpose(1, 0, 2).reshape(P, -1)

    e1 = i["w_route_expert"][0].transpose(1, 0, 2).reshape(D, 16)
    wr = np.concatenate([router(i["w_route_group"][0], e1),
                         router(i["router_group_w_2"][0], i["router_expert_w_2"][0])], 1)
    return {"cols": c, "xT": by_feature(i["x"][0]), "ctxT": by_feature(i["ctx_2"][0]), "fpack": fpack,
            "mpack": mpack, "lpack": lpack, "wr": np.ascontiguousarray(wr), "marks": marks,
            "brow": np.ascontiguousarray(spread(i["b_in_2"][:, 512:2048]))}


def kernel(**inputs):
    import concourse.bacc as bacc
    from concourse.bass_utils import run_bass_kernel_spmd

    i = {k: np.asarray(v) for k, v in inputs.items()}
    nc = bacc.Bacc("TRN2", target_bir_lowering=False, num_devices=1)
    arrays = packs(i)
    for name in _WHOLE:
        v = i[name]
        v = v.reshape((-1,) + v.shape[-2:])
        arrays[name] = np.ascontiguousarray(v[0] if v.shape[0] == 1 else v)
    aps = {name: nc.dram_tensor(f"in_{name}", v.shape, F32, kind="ExternalInput").ap() for name, v in arrays.items()}
    out = nc.dram_tensor("out_y", [P, DK, T], F32, kind="ExternalOutput").ap()
    build(nc, aps, out)
    r = run_bass_kernel_spmd(nc, [{f"in_{name}": v for name, v in arrays.items()}], core_ids=[0])
    y = r.results[0]["out_y"]
    return np.ascontiguousarray(y.transpose(2, 1, 0)).reshape(1, T, D)
```
